# Optimizing a Trainium2 kernel written in Bass

```python
import math
import jax, jax.numpy as jnp
from jax import lax
import numpy as np

D_MODEL = 1024
BATCH = 1
SEQ = 1024
DEPTH = 1
DEC_BATCH = 1
DEC_SEQ = 64
PAST_LEN = 512

CHUNK = 64
CONV_W = 4
D_RNN = 1024
RG_BLOCKS = 8
RG_BW = D_RNN // RG_BLOCKS
RG_C = 8.0
D_ML = 2 * D_MODEL
H_ML = 8
DH_IN = D_ML // H_ML
DK = 128
DV = 256
D_FF = 4 * D_MODEL
EPS = 1e-6
IN_SIZES = (D_RNN, D_RNN, D_ML, D_ML, H_ML, H_ML, D_MODEL, D_MODEL)
D_IN_TOTAL = 2 * D_RNN + 2 * D_ML + 2 * H_ML + 2 * D_MODEL

kernel_name = 'hawk_mlstm_parallel_streaming_step'

def rmsnorm(x, g):
    xf = x.astype(jnp.float32)
    y = xf * lax.rsqrt(jnp.mean(xf * xf, axis=-1, keepdims=True) + EPS)
    return (y * g.astype(jnp.float32)).astype(x.dtype)

def causal_conv(x, prev, w, b):
    S = x.shape[1]
    xp = jnp.concatenate([prev.astype(x.dtype), x], axis=1)
    y = b + sum(xp[:, k:k + S] * w[k] for k in range(CONV_W))
    return y, xp[:, -(CONV_W - 1):]

def rglru(xc, h0, wa, ba, wx, bx, lam):
    B, S, _ = xc.shape
    xf = xc.astype(jnp.float32)
    xb = xf.reshape(B, S, RG_BLOCKS, RG_BW)
    r = jax.nn.sigmoid(jnp.einsum('bsnc,ncd->bsnd', xb, wa.astype(jnp.float32)).reshape(B, S, D_RNN) + ba)
    i = jax.nn.sigmoid(jnp.einsum('bsnc,ncd->bsnd', xb, wx.astype(jnp.float32)).reshape(B, S, D_RNN) + bx)
    log_a = -RG_C * r * jax.nn.softplus(-lam.astype(jnp.float32))
    a = jnp.exp(log_a)
    gain = jnp.sqrt(-jnp.expm1(2.0 * log_a))
    bterm = gain * (i * xf)
    bterm = bterm.at[:, 0].add(a[:, 0] * h0.astype(jnp.float32))

    def combine(left, right):
        a1, b1 = left
        a2, b2 = right
        return a1 * a2, a2 * b1 + b2

    _, h = lax.associative_scan(combine, (a, bterm), axis=1)
    return h, h[:, -1]

def mlstm_chunkwise(q, k, v, ig, lf, C0, n0, m0):
    B, S, H, _ = q.shape
    L = CHUNK if S % CHUNK == 0 else S
    nc = S // L
    mask = jnp.tril(jnp.ones((L, L), dtype=bool))

    def chunks(t):
        return jnp.moveaxis(t.reshape((B, nc, L) + t.shape[2:]), 1, 0)

    def step(carry, xs):
        C, n, m = carry
        qc, kc, vc, ic, fc = xs
        bcum = jnp.cumsum(fc, axis=1)
        bl = bcum[:, -1]
        dmat = bcum[:, :, None, :] - bcum[:, None, :, :] + ic[:, None, :, :]
        dmat = jnp.where(mask[None, :, :, None], dmat, -jnp.inf)
        inter = bcum + m[:, None, :]
        m_t = jnp.maximum(inter, jnp.max(dmat, axis=2))
        w_intra = jnp.exp(dmat - m_t[:, :, None, :])
        w_inter = jnp.exp(inter - m_t)
        s = jnp.einsum('bthk,bshk->btsh', qc, kc) * w_intra
        num = jnp.einsum('btsh,bshv->bthv', s, vc) + w_inter[..., None] * jnp.einsum('bthk,bhvk->bthv', qc, C)
        den = jnp.sum(s, axis=2) + w_inter * jnp.einsum('bthk,bhk->bth', qc, n)
        h = num / jnp.maximum(jnp.abs(den), jnp.exp(-m_t))[..., None]
        g = bl[:, None, :] - bcum + ic
        m_new = jnp.maximum(bl + m, jnp.max(g, axis=1))
        wk = jnp.exp(g - m_new[:, None, :])
        decay = jnp.exp(bl + m - m_new)
        C_new = decay[..., None, None] * C + jnp.einsum('bsh,bshv,bshk->bhvk', wk, vc, kc)
        n_new = decay[..., None] * n + jnp.einsum('bsh,bshk->bhk', wk, kc)
        return (C_new, n_new, m_new), h

    carry0 = (C0.astype(jnp.float32), n0.astype(jnp.float32), m0.astype(jnp.float32))
    xs = tuple(chunks(t.astype(jnp.float32)) for t in (q, k, v, ig, lf))
    (C, n, m), h = lax.scan(step, carry0, xs)
    h = jnp.moveaxis(h, 0, 1).reshape(B, S, H, DV)
    return h, C, n, m

def block(x, conv_r, h_r, conv_m, C, n, m, norm_mix, w_in, b_if, cw_r, cb_r, wa, ba, wx, bx, lam,
          cw_m, cb_m, wq, wk, wv, wpa, wpb, w_out, norm_mlp, w_up, w_down):
    B, S, _ = x.shape
    u = rmsnorm(x, norm_mix)
    proj = u @ w_in
    parts = []
    off = 0
    for sz in IN_SIZES:
        parts.append(proj[..., off:off + sz])
        off += sz
    xr, gr, xm, zm, pi, pf, ga, gb = parts
    xr_c, conv_r_new = causal_conv(xr, conv_r, cw_r, cb_r)
    h_seq, h_last = rglru(xr_c, h_r, wa, ba, wx, bx, lam)
    y_a = h_seq.astype(x.dtype) * jax.nn.gelu(gr)
    xm_c, conv_m_new = causal_conv(xm, conv_m, cw_m, cb_m)
    xm_c = jax.nn.silu(xm_c).reshape(B, S, H_ML, DH_IN)
    xv = xm.reshape(B, S, H_ML, DH_IN)
    q = jnp.einsum('bshc,hck->bshk', xm_c, wq) * (DK ** -0.5)
    k = jnp.einsum('bshc,hck->bshk', xm_c, wk)
    v = jnp.einsum('bshc,hcv->bshv', xv, wv)
    ig = (pi + b_if[:H_ML]).astype(jnp.float32)
    lf = jax.nn.log_sigmoid((pf + b_if[H_ML:]).astype(jnp.float32))
    h_m, C_new, n_new, m_new = mlstm_chunkwise(q, k, v, ig, lf, C, n, m)
    y_b = jax.nn.sigmoid(zm) * h_m.reshape(B, S, D_ML).astype(x.dtype)
    mix = jax.nn.sigmoid(ga) * (y_a @ wpa) + jax.nn.sigmoid(gb) * (y_b @ wpb)
    x = x + mix @ w_out
    hmlp = jax.nn.relu(rmsnorm(x, norm_mlp) @ w_up)
    x = x + (hmlp * hmlp) @ w_down
    return x, conv_r_new, h_last, conv_m_new, C_new, n_new, m_new

def setup_inputs(seed: int = 0) -> dict:
    key = jax.random.key(seed)
    ks = jax.random.split(key, 32)
    f32 = jnp.float32
    nrm = lambda k, shape, s: jax.random.normal(k, shape, f32) * s
    u_a = jax.random.uniform(ks[0], (DEPTH, D_RNN), f32, 0.9, 0.999)
    a_base = u_a ** (1.0 / RG_C)
    lam = jnp.log(a_base) - jnp.log1p(-a_base)
    b_if = jnp.concatenate([nrm(ks[1], (DEPTH, H_ML), 0.1),
                            3.0 + nrm(ks[2], (DEPTH, H_ML), 0.3)], axis=-1)
    return {
        'x_prompt': nrm(ks[3], (BATCH, SEQ, D_MODEL), 1.0),
        'x_sample': nrm(ks[4], (DEC_BATCH, DEC_SEQ, D_MODEL), 1.0),
        'state_rglru_conv': nrm(ks[5], (DEPTH, DEC_BATCH, CONV_W - 1, D_RNN), 1.0),
        'state_rglru_h': nrm(ks[6], (DEPTH, DEC_BATCH, D_RNN), 0.5),
        'state_mlstm_conv': nrm(ks[7], (DEPTH, DEC_BATCH, CONV_W - 1, D_ML), 1.0),
        'state_mlstm_C': nrm(ks[8], (DEPTH, DEC_BATCH, H_ML, DV, DK), 0.1),
        'state_mlstm_n': nrm(ks[9], (DEPTH, DEC_BATCH, H_ML, DK), 0.1),
        'state_mlstm_m': nrm(ks[10], (DEPTH, DEC_BATCH, H_ML), 1.0),
        'norm_mix': 1.0 + nrm(ks[11], (DEPTH, D_MODEL), 0.02),
        'w_in': nrm(ks[12], (DEPTH, D_MODEL, D_IN_TOTAL), D_MODEL ** -0.5),
        'b_if': b_if,
        'conv_rglru_w': nrm(ks[13], (DEPTH, CONV_W, D_RNN), CONV_W ** -0.5),
        'conv_rglru_b': nrm(ks[14], (DEPTH, D_RNN), 0.02),
        'rglru_wa': nrm(ks[15], (DEPTH, RG_BLOCKS, RG_BW, RG_BW), RG_BW ** -0.5),
        'rglru_ba': nrm(ks[16], (DEPTH, D_RNN), 0.02),
        'rglru_wx': nrm(ks[17], (DEPTH, RG_BLOCKS, RG_BW, RG_BW), RG_BW ** -0.5),
        'rglru_bx': nrm(ks[18], (DEPTH, D_RNN), 0.02),
        'rglru_lambda': lam,
        'conv_mlstm_w': nrm(ks[19], (DEPTH, CONV_W, D_ML), CONV_W ** -0.5),
        'conv_mlstm_b': nrm(ks[20], (DEPTH, D_ML), 0.02),
        'mlstm_wq': nrm(ks[21], (DEPTH, H_ML, DH_IN, DK), DH_IN ** -0.5),
        'mlstm_wk': nrm(ks[22], (DEPTH, H_ML, DH_IN, DK), DH_IN ** -0.5),
        'mlstm_wv': nrm(ks[23], (DEPTH, H_ML, DH_IN, DV), DH_IN ** -0.5),
        'w_branch_a': nrm(ks[24], (DEPTH, D_RNN, D_MODEL), D_RNN ** -0.5),
        'w_branch_b': nrm(ks[25], (DEPTH, D_ML, D_MODEL), D_ML ** -0.5),
        'w_out': nrm(ks[26], (DEPTH, D_MODEL, D_MODEL), D_MODEL ** -0.5),
        'norm_mlp': 1.0 + nrm(ks[27], (DEPTH, D_MODEL), 0.02),
        'w_mlp_up': nrm(ks[28], (DEPTH, D_MODEL, D_FF), D_MODEL ** -0.5),
        'w_mlp_down': nrm(ks[29], (DEPTH, D_FF, D_MODEL), D_FF ** -0.5),
        'norm_final': 1.0 + nrm(ks[30], (D_MODEL,), 0.02),
    }

def reference(x_prompt, x_sample, state_rglru_conv, state_rglru_h, state_mlstm_conv, state_mlstm_C,
              state_mlstm_n, state_mlstm_m, norm_mix, w_in, b_if, conv_rglru_w, conv_rglru_b,
              rglru_wa, rglru_ba, rglru_wx, rglru_bx, rglru_lambda, conv_mlstm_w, conv_mlstm_b,
              mlstm_wq, mlstm_wk, mlstm_wv, w_branch_a, w_branch_b, w_out, norm_mlp,
              w_mlp_up, w_mlp_down, norm_final):
    Bp = x_prompt.shape[0]
    f32 = jnp.float32
    xp, xs = x_prompt, x_sample
    p_new = [[] for _ in range(6)]
    s_new = [[] for _ in range(6)]
    for l in range(DEPTH):
        w = (norm_mix[l], w_in[l], b_if[l], conv_rglru_w[l], conv_rglru_b[l], rglru_wa[l], rglru_ba[l],
             rglru_wx[l], rglru_bx[l], rglru_lambda[l], conv_mlstm_w[l], conv_mlstm_b[l], mlstm_wq[l],
             mlstm_wk[l], mlstm_wv[l], w_branch_a[l], w_branch_b[l], w_out[l], norm_mlp[l],
             w_mlp_up[l], w_mlp_down[l])
        outp = block(xp,
                     jnp.zeros((Bp, CONV_W - 1, D_RNN), xp.dtype), jnp.zeros((Bp, D_RNN), f32),
                     jnp.zeros((Bp, CONV_W - 1, D_ML), xp.dtype), jnp.zeros((Bp, H_ML, DV, DK), f32),
                     jnp.zeros((Bp, H_ML, DK), f32), jnp.zeros((Bp, H_ML), f32), *w)
        xp = outp[0]
        outs = block(xs, state_rglru_conv[l], state_rglru_h[l], state_mlstm_conv[l], state_mlstm_C[l],
                     state_mlstm_n[l], state_mlstm_m[l], *w)
        xs = outs[0]
        for j in range(6):
            p_new[j].append(outp[j + 1])
            s_new[j].append(outs[j + 1])
    y_prompt = rmsnorm(xp, norm_final)
    y_sample = rmsnorm(xs, norm_final)
    p_conv_r, p_h, p_conv_m, p_C, p_n, p_m = [jnp.stack(t, axis=0) for t in p_new]
    s_conv_r, s_h, s_conv_m, s_C, s_n, s_m = [jnp.stack(t, axis=0) for t in s_new]
    return (y_prompt, y_sample, p_conv_r, p_h, p_conv_m, p_C, p_n, p_m,
            s_conv_r, s_h, s_conv_m, s_C, s_n, s_m)


_drawn_inputs = setup_inputs


def setup_inputs(seed=0):
    import zlib

    import numpy as np

    out = dict(_drawn_inputs(seed))
    spreads = {}
    factors = {'state_mlstm_C': 5.025,
     'state_mlstm_n': 8.0,
     'state_mlstm_m': 7.226,
     'rglru_ba': 8.0,
     'rglru_bx': 7.881,
     'norm_mlp': 3.58,
     'norm_final': 2.761}
    for name, (base, spread) in spreads.items():
        noise = np.random.default_rng([zlib.crc32(name.encode()), seed]).standard_normal(out[name].shape)
        drawn = base * np.exp(spread * noise) if base else spread * noise
        out[name] = __import__('jax').numpy.asarray(drawn.astype(out[name].dtype))
    for name, factor in factors.items():
        out[name] = (out[name] * factor).astype(out[name].dtype)
    return out
```

```python
from contextlib import ExitStack

import numpy as np

import concourse.bass as bass
from concourse import mybir

F32 = mybir.dt.float32
F32R = mybir.dt.float32r
ACT = mybir.ActivationFunctionType
ALU = mybir.AluOpType

P = 128
D_MODEL = 1024
SEQ = 1024
DEC_SEQ = 64
CONV_W = 4
TAIL = CONV_W - 1
HEADS = 8
DK = 128
DV = 256
D_RNN = 1024
D_ML = HEADS * DV
D_FF = 4 * D_MODEL
EPS = 1e-6
RG_C = 8.0

KB = D_MODEL // P
GAP = 4
SAMPLE0 = SEQ + GAP
CARRY = SAMPLE0 - 1
COLS = SAMPLE0 + DEC_SEQ
TILES = 3
TW = COLS // TILES
BANK = 512
CH = 128
NCH = SEQ // CH + 1
KEY0 = [CH * c for c in range(NCH - 1)] + [COLS - CH]
COL0 = [CH * c for c in range(NCH - 1)] + [SAMPLE0]
CLEN = [CH] * (NCH - 1) + [DEC_SEQ]

CHUNK = 512
W_RG = 0
W_GATES = W_RG + 5 * KB
W_AO = W_GATES + 2
W_X0 = W_AO + 4 * KB
W_HEAD = W_X0 + 4
PER_HEAD = 14
W_GB = W_HEAD + PER_HEAD * HEADS - 4
W_OUT = W_GB + 2 * KB
W_MLP = W_OUT + 2 * KB
GROUPS = D_FF // D_MODEL
W_END = W_MLP + 32 * GROUPS

A_RG, B_RG = 1, 1
A_G = A_RG + 2 * KB
B_G = B_RG + 2 * KB
A_AO, B_AO = A_G + 1, B_G
A_X0, B_X0 = A_AO + KB, B_AO + KB
A_HD, B_HD = A_X0 + 1, B_X0 + 1
A_GB, B_GB = A_HD + 8 * HEADS - 1, B_HD + 8 * HEADS - 1
A_WO, B_WO = A_GB + 4, B_GB + 4
A_N2, B_N2 = A_WO + 4, B_WO + 4
A_ML, B_ML = A_N2 + 1, B_N2
A_N3 = A_ML + 8 * GROUPS

S_ID = 0
S_MASK = 128
S_MASK8 = 256
S_RG = 320
S_ML = S_RG + 8 * 13
S_GAIN = S_ML + 16 * 8
S_N0 = S_GAIN + 24
S_BIF = S_N0 + 8
S_M0 = S_BIF + 1
S_COLS = S_M0 + 1

XC, R, I, TH, G, SQ, H, GG = range(8)
IG, LF, EM, FF, MASK, MM, AR, EE = range(8)
AO_STAGE = (FF, MM)
ROWS_DVE, ROWS_ACT = 18, 6

FREE = 1

GELU_C = 0.044715
GELU_K = 0.7978845608028654


def build(nc, x_t, small_d, rowmask_d, w_d, c0_d, rows_d, mixa_d, y_d, conv_d, hlast_d, c_d, n_d, m_d):
    outer = ExitStack()
    sb_in = lambda st, name, shape, dt=F32: st.enter_context(nc.sbuf_tensor(name, shape, dt))
    sb = lambda name, shape, dt=F32: sb_in(outer, name, shape, dt)
    sem = lambda name: outer.enter_context(nc.semaphore(name))

    ps = outer.enter_context(nc.psum_tensor("ps", [P, 8, BANK], F32))
    slot_a, slot_b = ps[:, 0:3, 0:TW], ps[:, 3:6, 0:TW]
    slots = [slot_a, slot_b]

    u_hi = sb("u_hi", [P, KB, COLS], F32R)
    u_lo = sb("u_lo", [P, KB, COLS], F32R)
    acc = sb("acc", [P, KB, COLS])
    w_raw = sb("w_raw", [P, 2, CHUNK])
    w_hi = sb("w_hi", [P, 2, CHUNK], F32R)
    w_lo = sb("w_lo", [P, 2, CHUNK], F32R)
    small = sb("small", [P, S_COLS])
    ones = sb("ones", [P, P])
    eps_c = sb("eps_c", [P, 1])
    c8 = sb("c8", [P, 8, KB])
    rp = sb("rp", [P, 13])
    rc8 = sb("rc8", [P, 1])
    bp = sb("bp", [P, 2, 8])
    ecol = sb("ecol", [P, 2, NCH, HEADS])
    hcol = sb("hcol", [P, 2, NCH])
    dec = sb("dec", [P, NCH])
    cso = sb("cso", [P, 24, 6])
    hso = sb("hso", [P, KB, 2])
    nso = sb("nso", [P, HEADS, 2])
    mso = sb("mso", [HEADS, 2])

    with ExitStack() as st:
        p0 = sb_in(st, "p0", [P, 4, COLS])
    with ExitStack() as st:
        ya_hi = sb_in(st, "ya_hi", [P, KB, COLS], F32R)
        ya_lo = sb_in(st, "ya_lo", [P, KB, COLS], F32R)
        rpre = sb_in(st, "rpre", [P, COLS + TAIL])
        rx_hi = sb_in(st, "rx_hi", [P, COLS], F32R)
        rx_lo = sb_in(st, "rx_lo", [P, COLS], F32R)
    with ExitStack() as st:
        yb_hi = sb_in(st, "yb_hi", [P, 2, COLS], F32R)
        yb_lo = sb_in(st, "yb_lo", [P, 2, COLS], F32R)
        xm_hi = sb_in(st, "xm_hi", [P, 2, COLS], F32R)
        xm_lo = sb_in(st, "xm_lo", [P, 2, COLS], F32R)
        xc_hi = sb_in(st, "xc_hi", [P, 2, COLS], F32R)
        xc_lo = sb_in(st, "xc_lo", [P, 2, COLS], F32R)
        preq = sb_in(st, "preq", [P, COLS + TAIL])
        kz = sb_in(st, "kz", [P, COLS])
        vt = sb_in(st, "vt", [P, NCH * DV])
        bc = sb_in(st, "bc", [P, 3, COLS])
        cst = sb_in(st, "cst", [P, 2, DV + P])
        csm = sb_in(st, "csm", [P, DV + P])
        kt = sb_in(st, "kt", [P, 2, P])
        sw = sb_in(st, "sw", [P, 2, P])
    with ExitStack() as st:
        act_hi = sb_in(st, "act_hi", [P, KB, COLS], F32R)
        act_lo = sb_in(st, "act_lo", [P, KB, COLS], F32R)
        tmp = sb_in(st, "tmp", [P, 4, COLS])
    conv1, conv2 = vt[:, 0:COLS], vt[:, COLS:2 * COLS]

    s_small, s_rowmask, s_raw0, s_raw1 = sem("small_in"), sem("rowmask_in"), sem("raw0_in"), sem("raw1_in")
    s_raw = [s_raw0, s_raw1]
    s_x = [sem(f"x_in{j}") for j in range(KB)]
    s_whi, s_wlo = sem("chunk_hi"), sem("chunk_split")
    s_chunk = sem("chunk_multiplied")
    s_drA, s_drB = sem("slot_a_drained"), sem("slot_b_drained")
    s_dr = [s_drA, s_drB]
    s_half = sem("half_chunk_multiplied")
    s_va, s_q_mm, s_gr_mm, s_bb = sem("v_first_mm"), sem("q_mm"), sem("r_mm"), sem("branch_b_even_mm")
    s_out = sem("stored")
    s_const, s_const_dve = sem("constants_set"), sem("pads_zeroed")
    r_cs, r_hs, m_cs2, m_dec = sem("rg_tails"), sem("rg_h_out"), sem("ml_tails"), sem("ml_decays")
    s_sq, s_ssum, s_norm, s_std, s_rstd, s_nrm, s_nhi, s_nlo = [sem(n) for n in (
        "squared", "squares_summed", "norm_mm", "std", "rstd", "normed", "normed_hi", "normed_lo")]
    s_sp, s_spv = sem("softplus_act"), sem("softplus_dve")
    (r_pre, r_tap0, r_g, r_xhi, r_sq, r_th, r_tg, r_a, r_gain, r_yhi) = [sem("rg_" + n) for n in (
        "pre", "tap0", "g", "x_hi", "sq", "th", "tg", "a", "gain", "y_hi")]
    (r_rp, r_pad, r_conv, r_xlo, r_inner, r_ix, r_a2, r_p, r_b, r_fix, r_scan, r_gg, r_y, r_ylo) = [
        sem("rg_" + n) for n in ("params", "pads", "conv", "x_lo", "inner", "ix", "a2", "p", "b", "carry",
                                 "scan", "gg", "y", "y_lo")]
    w_act, w_dve, w_tr, w_col, w_colz, w_st = [sem("rows_" + n) for n in (
        "act", "dve", "transposed", "cols", "cols_zeroed", "stored")]
    ao_st = [sem(f"mix_a_stored{j}") for j in range(2)]
    (m_pre, m_xhi, m_tap0, m_sig, m_chi, m_v, m_e, m_kt, m_zs, m_yhi) = [sem("ml_" + n) for n in (
        "pre", "x_hi", "tap0", "sig", "c_hi", "v", "e", "kt", "zs", "y_hi")]
    (m_bp, m_pad, m_conv, m_silu, m_clo, m_hcol, m_mask, m_qw, m_sw, m_c, m_rec, m_hn, m_y, m_ylo,
     m_cs, m_no) = [sem("ml_" + n) for n in (
         "params", "pads", "conv", "silu", "c_lo", "head_cols", "masked", "qw", "scores_w", "state", "rec",
         "h", "y", "y_lo", "sample_n", "n_out")]
    m_s_mm, m_u_mm, m_o_mm = sem("scores_mm"), sem("state_mm"), sem("h_mm")
    m_bc, m_c0, m_cout = sem("rows_in"), sem("sample_state_in"), sem("states_stored")
    s_zero = sem("branch_b_zeroed")
    g_t, g_mix, g_hi, g_lo = [sem("merge_" + n) for n in ("t", "mix", "hi", "lo")]
    g_in = [sem(f"mix_a_in{j}") for j in range(2)]
    o_in = [sem(f"x_again_in{j}") for j in range(2)]
    o_sq, o_ssum = sem("res_squared"), sem("res_ssum")
    h_r, h_hi, h_s, h_lo = sem("hid_relu"), sem("hid_hi"), sem("hid_sq"), sem("hid_lo")
    f_sq, f_ssum, f_y = sem("final_squared"), sem("final_ssum"), sem("final_y")

    block = outer.enter_context(nc.Block())

    def as3(ap):
        return ap.rearrange("p (a b) -> p a b", a=TILES)

    def blk(t, n):
        if isinstance(n, int):
            return t[:, n, :]
        return t[:, bass.ds(n, 1), :].rearrange("p a c -> p (a c)")

    def loop(eng, n, body):
        with eng.Fori(0, n) as i:
            body(i)

    @block.sync
    def _(sp):
        sp.dma_start(small[:], small_d).then_inc(s_small, 16)
        for j in range(KB):
            sp.dma_start(acc[:, j, :], x_t[j]).then_inc(s_x[j], 16)
        for c in range(2):
            sp.dma_start(w_raw[:, c, :], w_d[c]).then_inc(s_raw[c], 16)

        def more(i):
            for c in range(2):
                src = w_d[bass.ds(sp.snap(2 * i + 2 + c), 1)].rearrange("a p m -> p (a m)")
                sp.wait_ge(s_wlo, 2 * i + c + 1)
                sp.dma_start(w_raw[:, c, :], src).then_inc(s_raw[c], 16)
        loop(sp, W_END // 2 - 1, more)

        sp.wait_ge(r_cs, 2 * KB)
        sp.wait_ge(m_cs2, 4 * HEADS)
        sp.dma_start(conv_d, cso[:]).then_inc(s_out, 16)
        sp.wait_ge(r_hs, 2 * KB)
        sp.dma_start(hlast_d, hso[:]).then_inc(s_out, 16)
        sp.wait_ge(m_no, 2 * HEADS)
        sp.dma_start(n_d, nso[:]).then_inc(s_out, 16)
        sp.wait_ge(w_dve, ROWS_DVE)
        sp.dma_start(m_d, mso[:]).then_inc(s_out, 16)
        for j in range(KB):
            sp.wait_ge(f_y, j + 1)
            sp.dma_start(y_d[j], acc[:, j, :]).then_inc(s_out, 16)
        sp.wait_ge(s_out, 16 * (4 + KB))
        sp.wait_ge(m_cout, 32 * HEADS + 16)

    @block.gpsimd
    def _(pool):
        nc.gpsimd.memset(ones[:], 1.0).then_inc(s_const, 1)
        nc.gpsimd.memset(eps_c[:], EPS).then_inc(s_const, 1)
        one = ones[:, 0:1].broadcast_to([P, CHUNK])
        pool.wait_ge(s_const, 1)

        def split(c, j, first):
            pool.wait_ge(s_raw[c], 16 * j + 16)
            if not first:
                pool.wait_ge(s_chunk, 2 * j + c - 1)
            nc.gpsimd.tensor_tensor(w_hi[:, c, :], w_raw[:, c, :], one, ALU.mult).then_inc(s_whi, 1)
            pool.wait_ge(s_whi, 2 * j + c + 1)
            nc.gpsimd.tensor_tensor(w_lo[:, c, :], w_raw[:, c, :], w_hi[:, c, :].bitcast(F32),
                                    ALU.subtract).then_inc(s_wlo, 1)
        split(0, 0, True)
        split(1, 0, True)

        def both(i):
            split(0, i + 1, False)
            split(1, i + 1, False)
        loop(pool, W_END // 2 - 1, both)

    @block.tensor
    def _(pe):
        def product(slot, blocks, rhs_hi, rhs_lo, before=None, done=None):
            last_k = len(blocks) - 1
            for k, (chunk, ws, off, last) in enumerate(blocks):
                if chunk is not None:
                    pe.wait_ge(s_wlo, chunk + 1)
                if before is not None:
                    before(k)
                hi, lo = w_hi[:, ws, off:off + P], w_lo[:, ws, off:off + P]
                for n, (w, r) in enumerate(((hi, rhs_hi), (hi, rhs_lo), (lo, rhs_hi))):
                    for t in range(TILES):
                        mm = nc.tensor.matmul(slots[slot][:, t, :], w, r(k)[:, t * TW:(t + 1) * TW],
                                              start=(k == 0 and n == 0), stop=(k == last_k and n == 2))
                if last:
                    mm.then_inc(s_chunk, 1)
                elif k == last_k and done is not None:
                    mm.then_inc(done, 1)

        def full(chunk):
            return [(chunk + k // 4 if k % 4 == 0 else None, k // 4, (k % 4) * P, k % 4 == 3) for k in range(KB)]

        def full_odd(chunk):
            return [(c, 1 - ws, off, last) for c, ws, off, last in full(chunk)]

        U = (lambda k: u_hi[:, k, :], lambda k: u_lo[:, k, :])

        def norm_sum(src, wait):
            wait()
            for t in range(TILES):
                mm = nc.tensor.matmul(slot_a[:, t, :], ones[:], src[:, t * TW:(t + 1) * TW], start=True, stop=True)
            mm.then_inc(s_norm, 1)

        def n1():
            pe.wait_ge(s_const, 2)
            pe.wait_ge(s_ssum, KB)
        norm_sum(p0[:, 2, :], n1)

        def rg(i):
            for half in range(2):
                c = W_RG + 10 * i + 5 * half
                pick = full_odd if half else full
                a0, b0 = A_RG + 4 * i + 2 * half, B_RG + 4 * i + 2 * half
                pe.wait_ge(s_drA, a0)
                product(0, pick(c), *U, before=lambda k: pe.wait_ge(s_nlo, k + 1))
                pe.wait_ge(s_drB, b0)
                product(1, pick(c + 2), *U)
                x = (lambda k: rx_hi[:], lambda k: rx_lo[:])
                pe.wait_ge(s_drA, a0 + 1)
                pe.wait_ge(r_xlo, 2 * i + half + 1)
                product(0, [(c + 4, half, 0, False)], *x, done=s_gr_mm)
                pe.wait_ge(s_drB, b0 + 1)
                product(1, [(None, half, P, True)], *x)
        loop(pe, KB // 2, rg)

        pe.wait_ge(s_drA, A_G)
        product(0, full(W_GATES), *U)

        def ao(n):
            pe.wait_ge(s_drA, A_AO + n)
            product(0, full(W_AO + 4 * n), lambda k: ya_hi[:, k, :], lambda k: ya_lo[:, k, :],
                    before=lambda k: pe.wait_ge(r_ylo, k + 1))
            pe.wait_ge(s_drB, B_AO + n)
            product(1, full(W_AO + 4 * n + 2), *U)
        loop(pe, KB, ao)

        pe.wait_ge(w_dve, ROWS_DVE)
        pe.wait_ge(w_act, ROWS_ACT)
        for r, row in enumerate((EE, MASK)):
            for c in range(NCH):
                o = (r * NCH + c) * HEADS
                mm = nc.tensor.transpose(ps[:, 6, o:o + HEADS], acc[0:HEADS, row, KEY0[c]:KEY0[c] + CH],
                                         small[0:HEADS, S_ID:S_ID + HEADS])
        mm.then_inc(w_tr, 1)

        def xm(chunk, a, b):
            pe.wait_ge(s_drA, a)
            product(0, full(chunk), *U)
            pe.wait_ge(s_drB, b)
            product(1, full(chunk + 2), *U)
        xm(W_X0, A_X0, B_X0)
        pe.wait_ge(w_colz, 1)

        def head(h, last):
            c0, a0, b0 = W_HEAD + PER_HEAD * h, A_HD + 8 * h, B_HD + 8 * h
            pe.wait_ge(s_wlo, c0 + 1)
            pe.wait_ge(m_conv, TAIL * (2 * h + 2))
            pe.wait_ge(s_drA, a0)
            for c in range(NCH):
                if c == 6:
                    pe.wait_ge(s_drB, b0)
                out = ps[:, c // 2, (c % 2) * DV:(c % 2 + 1) * DV]
                k0 = KEY0[c]
                for cb in range(2):
                    wv_hi, wv_lo = (w[:, 0, cb * DV:(cb + 1) * DV] for w in (w_hi, w_lo))
                    x_hi, x_lo = (x[:, cb, k0:k0 + CH] for x in (xm_hi, xm_lo))
                    for n, (l, r) in enumerate(((x_hi, wv_hi), (x_hi, wv_lo), (x_lo, wv_hi))):
                        mm = nc.tensor.matmul(out, l, r, start=(cb == 0 and n == 0), stop=(cb == 1 and n == 2))
                if c == 5:
                    mm.then_inc(s_va, 1)
            mm.then_inc(s_chunk, 1)
            C = (lambda k: xc_hi[:, k, :], lambda k: xc_lo[:, k, :])
            pe.wait_ge(s_drA, a0 + 1)
            product(0, [(c0 + 1, 1, 0, False), (None, 1, P, False)], *C,
                    before=lambda k: pe.wait_ge(m_clo, 2 * h + k + 1), done=s_q_mm)
            pe.wait_ge(s_drB, b0 + 1)
            product(1, [(None, 1, 2 * P, False), (None, 1, 3 * P, True)], *C)

            def scores(c):
                if c == 0:
                    pe.wait_ge(s_drA, a0 + 2)
                    pe.wait_ge(s_drB, b0 + 2)
                k0, t0, n = KEY0[c], COL0[c], CLEN[c]
                nc.tensor.matmul(ps[:, 6 + c % 2, 0:n], kz[:, k0:k0 + CH], preq[:, t0:t0 + n], start=True, stop=True)
                nc.tensor.transpose(ps[:, 2 + 3 * (c % 2), 0:P], kz[:, k0:k0 + CH],
                                    small[:, S_ID:S_ID + P]).then_inc(m_s_mm, 1)

            scores(0)
            scores(1)
            pe.wait_ge(m_qw, h + 1)
            for c in range(NCH):
                t0, n = COL0[c], CLEN[c]
                pe.wait_ge(m_kt, NCH * h + c + 1)
                if c >= 2:
                    pe.wait_ge(m_c, NCH * h + c - 1)
                nc.tensor.matmul(ps[:, c % 2, 0:DV], kt[:, c % 2, :], vt[:, c * DV:(c + 1) * DV],
                                 start=True, stop=True)
                nc.tensor.matmul(ps[:, c % 2, DV:DV + P], kt[:, c % 2, :], ones[:],
                                 start=True, stop=True).then_inc(m_u_mm, 1)
                pe.wait_ge(m_sw, NCH * h + c + 1)
                if c >= 2:
                    pe.wait_ge(m_hn, NCH * h + c - 1)
                state = None
                if c == NCH - 1:
                    pe.wait_ge(m_c0, 16 * h + 16)
                    pe.wait_ge(m_cs, h + 1)
                    state = csm
                elif c >= 1:
                    pe.wait_ge(m_c, NCH * h + c)
                    state = cst[:, c % 2, :]
                for j in range(3):
                    out = ps[:, 3 + c % 2, j * P:j * P + n]
                    lhs = ones[:] if j == 2 else vt[:, c * DV + j * P:c * DV + (j + 1) * P]
                    mm = nc.tensor.matmul(out, lhs, sw[:, c % 2, 0:n], start=True, stop=state is None)
                    if state is not None:
                        mm = nc.tensor.matmul(out, state[:, j * P:(j + 1) * P], bc[:, 1, t0:t0 + n],
                                              start=False, stop=True)
                mm.then_inc(m_o_mm, 1)
                if c + 2 < NCH:
                    scores(c + 2)
            pe.wait_ge(m_hn, NCH * h + NCH)
            pe.wait_ge(m_c, NCH * h + NCH)
            c1, a1, b1 = c0 + 2, a0 + 2, b0 + 2
            if not last:
                xm(c1, a1, b1)
                c1, a1, b1 = c1 + 4, a1 + 1, b1 + 1
            xm(c1, a1, b1)
            c1, a1, b1 = c1 + 4, a1 + 1, b1 + 1
            Y = (lambda k: yb_hi[:, k, :], lambda k: yb_lo[:, k, :])
            for m in range(KB):
                ws, off = (m // 2) % 2, (m % 2) * 2 * P
                first = c1 + m // 2 if m % 2 == 0 else None
                pe.wait_ge(s_dr[m % 2], (b1 if m % 2 else a1) + m // 2)
                product(m % 2, [(first, ws, off, False), (None, ws, off + P, m % 2 == 1)], *Y,
                        before=lambda k: pe.wait_ge(m_ylo, 2 * h + k + 1), done=s_bb)
        loop(pe, HEADS - 1, lambda h: head(h, False))
        head(HEADS - 1, True)

        def gb(i):
            for half in range(2):
                pe.wait_ge(s_dr[half], (A_GB, B_GB)[half] + i)
                product(half, full(W_GB + 4 * i + 2 * half), *U)
        loop(pe, KB // 2, gb)
        A = (lambda k: act_hi[:, k, :], lambda k: act_lo[:, k, :])

        def wo(i):
            for half in range(2):
                pe.wait_ge(s_dr[half], (A_WO, B_WO)[half] + i)
                product(half, full(W_OUT + 4 * i + 2 * half), *A, before=lambda k: pe.wait_ge(g_lo, k + 1))
        loop(pe, KB // 2, wo)

        def n2():
            pe.wait_ge(s_drA, A_N2)
            pe.wait_ge(o_ssum, KB)
        norm_sum(tmp[:, 2, :], n2)

        def mlp(g):
            def up(i):
                for half in range(2):
                    pe.wait_ge(s_dr[half], (A_ML, B_ML)[half] + 8 * g + i)
                    product(half, full(W_MLP + 32 * g + 4 * i + 2 * half), *U,
                            before=lambda k: pe.wait_ge(s_nlo, KB + k + 1))
            loop(pe, KB // 2, up)

            def down(i):
                for half in range(2):
                    pe.wait_ge(s_dr[half], (A_ML, B_ML)[half] + 8 * g + 4 + i)
                    product(half, full(W_MLP + 32 * g + 16 + 4 * i + 2 * half), *A,
                            before=lambda k: pe.wait_ge(h_lo, 8 * g + k + 1))
            loop(pe, KB // 2, down)
        loop(pe, GROUPS, mlp)

        def n3():
            pe.wait_ge(s_drA, A_N3)
            pe.wait_ge(f_ssum, KB)
        norm_sum(tmp[:, 2, :], n3)

    @block.scalar
    def _(act):
        def a(out, in_, f, inc, **kw):
            nc.scalar.activation(out, in_, f, **kw).then_inc(inc, 1)

        act.sem_inc(s_drB, 1)
        act.sem_inc(ao_st[0], 16)
        act.sem_inc(ao_st[1], 16)
        act.sem_inc(m_cout, 16)
        act.wait_ge(s_const, 2)
        act.wait_ge(s_small, 16)

        for j in range(KB):
            act.wait_ge(s_x[j], 16)
            if j >= 2:
                act.wait_ge(s_ssum, j - 1)
            a(p0[:, j % 2, :], acc[:, j, :], ACT.Square, s_sq)

        act.wait_ge(s_spv, 1)
        a(c8[:, 2, :], c8[:, 1, :], ACT.Exp, s_sp, scale=-1.0)

        def std(n, dst):
            act.wait_ge(s_norm, n + 1)
            nc.scalar.activation(as3(dst), slot_a, ACT.Sqrt, scale=1.0 / D_MODEL, bias=eps_c[:, 0:1])\
                .then_inc(s_drA, 1)
        std(0, p0[:, 3, :])
        for j in range(KB):
            act.wait_ge(s_nrm, j + 1)
            a(u_hi[:, j, :], acc[:, j, :], ACT.Copy, s_nhi)

        def rg(n):
            act.wait_ge(s_chunk, W_RG + 5 * n + 2)
            nc.scalar.activation(as3(rpre[:, TAIL:]), slot_a, ACT.Copy).then_inc(s_drA, 1)
            act.wait_ge(r_pad, n + 1)
            act.wait_ge(r_ix, n + FREE)
            a(acc[:, XC, :], rpre[:, 0:COLS], ACT.Identity, r_tap0, scale=rp[:, 0:1], bias=rp[:, 4:5])
            act.wait_ge(s_chunk, W_RG + 5 * n + 4)
            act.wait_ge(r_gg, n + FREE)
            nc.scalar.activation(as3(acc[:, G, :]), slot_b, ACT.Copy).then_inc(s_drB, 1)
            act.wait_ge(r_conv, TAIL * n + TAIL)
            a(rx_hi[:], acc[:, XC, :], ACT.Copy, r_xhi)
            act.wait_ge(s_drB, B_RG + 2 * n + 1)
            a(acc[:, SQ, :], acc[:, G, :], ACT.Square, r_sq)
            act.wait_ge(s_gr_mm, n + 1)
            nc.scalar.activation(as3(acc[:, R, :]), slot_a, ACT.Sigmoid, bias=rp[:, 5:6]).then_inc(s_drA, 1)
            act.wait_ge(s_chunk, W_RG + 5 * n + 5)
            nc.scalar.activation(as3(acc[:, I, :]), slot_b, ACT.Sigmoid, bias=rp[:, 6:7]).then_inc(s_drB, 1)
            act.wait_ge(s_drA, A_RG + 2 * n + 2)
            a(acc[:, TH, :], acc[:, R, :], ACT.Tanh, r_th, scale=rc8[:, 0:1])
            act.wait_ge(r_inner, n + 1)
            a(acc[:, SQ, :], acc[:, SQ, :], ACT.Tanh, r_tg, scale=GELU_C * GELU_K)
            act.wait_ge(r_th, n + 1)
            a(acc[:, R, :], acc[:, R, :], ACT.Exp, r_a, scale=rc8[:, 0:1])
            act.wait_ge(r_p, n + 1)
            a(acc[:, TH, :], acc[:, TH, :], ACT.Sqrt, r_gain, scale=-1.0)
            act.wait_ge(r_y, n + 1)
            a(blk(ya_hi, n), acc[:, GG, :], ACT.Copy, r_yhi)
        loop(act, KB, rg)

        act.wait_ge(r_ylo, KB)
        act.dma_start(acc[0:HEADS, MASK, :], rowmask_d).then_inc(s_rowmask, 16)
        act.wait_ge(s_chunk, W_GATES + 2)
        row = lambda j: acc[0:HEADS, j, :]
        nc.scalar.activation(as3(row(IG)), slot_a[0:HEADS], ACT.Identity,
                             bias=small[0:HEADS, S_BIF:S_BIF + 1]).then_inc(w_act, 1)
        nc.scalar.activation(as3(row(LF)), slot_a[32:32 + HEADS], ACT.Identity,
                             bias=small[32:32 + HEADS, S_BIF:S_BIF + 1]).then_inc(s_drA, 1)
        act.wait_ge(w_dve, 1)
        a(row(EM), row(EM), ACT.Exp, w_act, scale=-1.0)
        act.wait_ge(w_act, 2)
        a(row(EM), row(EM), ACT.Ln, w_act, bias=ones[0:HEADS, 0:1])
        act.wait_ge(w_dve, 7)
        a(row(EM), row(MM), ACT.Exp, w_act, scale=-1.0)
        act.wait_ge(w_dve, 14)
        a(row(LF), row(LF), ACT.Exp, w_act)
        act.wait_ge(w_dve, ROWS_DVE)
        a(row(MASK), row(MASK), ACT.Exp, w_act)
        act.wait_ge(w_act, ROWS_ACT)
        for n, r in enumerate((AR, LF, EM)):
            act.dma_start(rows_d[:, n, :], row(r)).then_inc(w_st, 16)

        def ao(i):
            for half in range(2):
                n = 2 * i + half
                act.wait_ge(s_chunk, W_AO + 4 * n + 4)
                act.wait_ge(s_drA, A_AO + n)
                nc.scalar.activation(as3(acc[:, IG, :]), slot_b, ACT.Sigmoid).then_inc(s_drB, 1)
                dst = mixa_d[bass.ds(n, 1)].rearrange("a p c -> p (a c)")
                act.wait_ge(s_drA, A_AO + n + 1)
                act.dma_start(dst, acc[:, AO_STAGE[half], :]).then_inc(ao_st[half], 16)
        loop(act, KB // 2, ao)

        def xm(h, chunk):
            for cb in range(2):
                act.wait_ge(s_chunk, chunk + 2 * cb + 2)
                a(as3(preq[:, TAIL:]), slots[cb], ACT.Copy, m_pre)
                a(as3(xm_hi[:, cb, :]), slots[cb], ACT.Copy, m_xhi)
                act.wait_ge(m_pad, 4 * h + 2 * cb + 2)
                if cb:
                    act.wait_ge(m_clo, 2 * h + 1)
                a(conv1, preq[:, 0:COLS], ACT.Identity, m_tap0, scale=bp[:, cb, 0:1], bias=bp[:, cb, 4:5])
                act.wait_ge(m_conv, TAIL * (2 * h + cb) + TAIL)
                a(conv2, conv1, ACT.Sigmoid, m_sig)
                act.wait_ge(m_silu, 2 * h + cb + 1)
                a(xc_hi[:, cb, :], conv1, ACT.Copy, m_chi)

        def load_head(h):
            one = bass.ds(h, 1)
            act.dma_start(bc[:].rearrange("p r c -> p (r c)"),
                          rows_d[one].rearrange("a r c -> a (r c)").broadcast_to([P, 3 * COLS]))\
               .then_inc(m_bc, 16)
            act.dma_start(csm[:, 0:DV], c0_d[one].rearrange("a p v -> p (a v)")).then_inc(m_c0, 16)

        act.wait_ge(s_chunk, W_X0 + 2)
        act.wait_ge(w_st, 48)
        for half in range(2):
            act.wait_ge(ao_st[half], 16 * (KB // 2) + 16)
        load_head(0)
        xm(0, W_X0)

        flat = ps[:].rearrange("p a b -> p (a b)")

        def head(h, last):
            c0 = W_HEAD + PER_HEAD * h
            act.wait_ge(s_va, h + 1)
            act.wait_ge(m_clo, 2 * h + 2)
            nc.scalar.activation(vt[:, 0:6 * DV], flat[:, 0:3 * BANK], ACT.Copy).then_inc(s_drA, 1)
            act.wait_ge(s_chunk, c0 + 1)
            nc.scalar.activation(vt[:, 6 * DV:], flat[:, 3 * BANK:3 * BANK + 3 * DV], ACT.Copy).then_inc(s_drB, 1)
            act.wait_ge(s_q_mm, h + 1)
            nc.scalar.activation(as3(preq[:, 0:COLS]), slot_a, ACT.Copy, scale=float(DK) ** -0.5)\
                .then_inc(s_drA, 1)
            act.wait_ge(s_chunk, c0 + 2)
            nc.scalar.activation(as3(kz[:]), slot_b, ACT.Copy).then_inc(s_drB, 1)
            act.wait_ge(m_mask, NCH * (h + 1))
            for s in (slice(0, SEQ), slice(SAMPLE0, COLS)):
                a(bc[:, 0, s], bc[:, 0, s], ACT.Exp, m_e)
            for c in range(NCH):
                act.wait_ge(m_s_mm, NCH * h + c + 1)
                if c >= 2:
                    act.wait_ge(m_u_mm, NCH * h + c - 1)
                a(kt[:, c % 2, :], ps[:, 2 + 3 * (c % 2), 0:P], ACT.Copy, m_kt, scale=hcol[:, 1, c:c + 1])
            act.wait_ge(m_c, NCH * (h + 1))
            for s in range(2):
                act.dma_start(c_d[bass.ds(h + HEADS * s, 1)].rearrange("a p v -> p (a v)"), cst[:, s, 0:DV])\
                   .then_inc(m_cout, 16)
            if not last:
                xm(h + 1, c0 + 2)
            cz = c0 + (2 if last else 6)
            act.wait_ge(s_chunk, cz + 2)
            nc.scalar.activation(as3(kz[:]), slot_a, ACT.Sigmoid).then_inc(s_drA, 1)
            act.wait_ge(s_chunk, cz + 4)
            nc.scalar.activation(as3(preq[:, 0:COLS]), slot_b, ACT.Sigmoid).then_inc(s_drB, 1)
            for cb in range(2):
                act.wait_ge(m_y, 2 * h + cb + 1)
                a(yb_hi[:, cb, :], bc[:, cb, :], ACT.Copy, m_yhi)
            if not last:
                act.wait_ge(m_ylo, 2 * h + 2)
                act.wait_ge(m_o_mm, NCH * (h + 1))
                load_head(h + 1)
        loop(act, HEADS - 1, lambda h: head(h, False))
        head(HEADS - 1, True)

        act.wait_ge(s_drB, B_GB)
        act.wait_ge(s_drA, A_GB)
        act.wait_ge(m_cout, 32 * HEADS + 16)

        def load(dram, n, dst, inc):
            act.dma_start(dst, dram[bass.ds(n, 1)].rearrange("a p c -> p (a c)")).then_inc(inc, 16)

        for half in range(2):
            load(mixa_d, half, tmp[:, 2 + half, :], g_in[half])

        def gb(i, last):
            for half in range(2):
                n = 2 * i + half
                act.wait_ge(s_chunk, W_GB + 2 * n + 2)
                nc.scalar.activation(as3(tmp[:, half, :]), slots[half], ACT.Sigmoid).then_inc(s_dr[half], 1)
                act.wait_ge(g_mix, n + 1)
                a(blk(act_hi, n), tmp[:, half, :], ACT.Copy, g_hi)
                if not last:
                    load(mixa_d, n + 2, tmp[:, 2 + half, :], g_in[half])
        loop(act, KB // 2 - 1, lambda i: gb(i, False))
        gb(KB // 2 - 1, True)

        act.wait_ge(g_lo, KB)
        for half in range(2):
            load(x_t, half, tmp[:, half, :], o_in[half])

        def wo(i, last):
            for half in range(2):
                n = 2 * i + half
                act.wait_ge(s_dr[half], (A_WO, B_WO)[half] + i + 1)
                a(tmp[:, 3, :], blk(acc, n), ACT.Square, o_sq)
                if not last:
                    load(x_t, n + 2, tmp[:, half, :], o_in[half])
        loop(act, KB // 2 - 1, lambda i: wo(i, False))
        wo(KB // 2 - 1, True)
        act.wait_ge(o_ssum, KB)
        std(1, tmp[:, 3, :])
        for j in range(KB):
            act.wait_ge(s_nrm, KB + j + 1)
            a(u_hi[:, j, :], tmp[:, j % 2, :], ACT.Copy, s_nhi)

        def up(g):
            def pair(i):
                for half in range(2):
                    j = 8 * g + 2 * i + half
                    act.wait_ge(s_chunk, W_MLP + 32 * g + 4 * i + 2 * half + 2)
                    act.wait_ge(h_s, j - 1 + 2 * FREE)
                    nc.scalar.activation(as3(tmp[:, half, :]), slots[half], ACT.Relu).then_inc(s_dr[half], 1)
                    act.wait_ge(s_dr[half], (A_ML, B_ML)[half] + 8 * g + i + 1)
                    a(blk(act_hi, 2 * i + half), tmp[:, half, :], ACT.Square, h_hi)
            loop(act, KB // 2, pair)
        loop(act, GROUPS, up)

        def final(i):
            for half in range(2):
                act.wait_ge(s_dr[half], (A_ML, B_ML)[half] + 8 * (GROUPS - 1) + 4 + i + 1)
                a(tmp[:, half, :], blk(acc, 2 * i + half), ACT.Square, f_sq)
        loop(act, KB // 2, final)
        act.wait_ge(f_ssum, KB)
        std(2, tmp[:, 3, :])

    @block.vector
    def _(dve):
        V = nc.vector

        def stt(out, in0, scalar, in1, op0, op1, inc):
            V.scalar_tensor_tensor(out, in0, scalar, in1, op0, op1).then_inc(inc, 1)

        def tt(out, in0, in1, op, inc):
            V.tensor_tensor(out, in0, in1, op).then_inc(inc, 1)

        dve.sem_inc(r_ix, FREE)
        dve.sem_inc(r_gg, FREE)
        dve.sem_inc(h_s, 2 * FREE)
        V.memset(rpre[:, 0:TAIL], 0.0).then_inc(s_const_dve, 1)
        dve.wait_ge(s_small, 16)

        lam = small[:, S_RG + 7:S_RG + 13 * KB:13]
        c = [c8[:, j, :] for j in range(8)]
        steps = [
            lambda: V.scalar_tensor_tensor(c[1], lam, -1.0, lam, ALU.mult, ALU.max),
            lambda: V.tensor_scalar(c[3], c[2], 2.0, None, ALU.add),
            lambda: V.reciprocal(c[4], c[3]),
            lambda: V.tensor_tensor(c[5], c[2], c[4], ALU.mult),
            lambda: V.tensor_tensor(c[6], c[5], c[5], ALU.mult),
            lambda: V.tensor_scalar(c[7], c[6], 1.0 / 15, None, ALU.mult),
        ] + [
            (lambda k=k: V.scalar_tensor_tensor(c[7], c[7], 1.0 / k, c[6], ALU.add, ALU.mult))
            for k in (13, 11, 9, 7, 5, 3)
        ] + [
            lambda: V.scalar_tensor_tensor(c[3], c[7], 1.0, c[5], ALU.add, ALU.mult),
            lambda: V.tensor_tensor(c[4], c[1], lam, ALU.subtract),
            lambda: V.tensor_scalar(c[4], c[4], -RG_C / 2, None, ALU.mult),
            lambda: V.scalar_tensor_tensor(c[0], c[3], -2 * RG_C, c[4], ALU.mult, ALU.add),
        ]
        steps[0]().then_inc(s_spv, 1)

        for j in range(KB):
            dve.wait_ge(s_sq, j + 1)
            if j == 0:
                V.tensor_copy(p0[:, 2, :], p0[:, 0, :]).then_inc(s_ssum, 1)
            else:
                dve.wait_ge(s_ssum, j)
                tt(p0[:, 2, :], p0[:, 2, :], p0[:, j % 2, :], ALU.add, s_ssum)
        dve.wait_ge(s_sp, 1)
        for k, step in enumerate(steps[1:]):
            dve.wait_ge(s_spv, k + 1)
            step().then_inc(s_spv, 1)

        def norm(n, scale, src, dst, drained):
            dve.wait_ge(s_drA, drained)
            V.reciprocal(scale, scale).then_inc(s_rstd, 1)
            dve.wait_ge(s_rstd, n + 1)
            for j in range(KB + 1):
                if j < KB:
                    g = S_GAIN + KB * n + j
                    if j >= 2:
                        dve.wait_ge(s_nlo, KB * n + j - 1)
                    stt(dst(j), src(j), small[:, g:g + 1], scale, ALU.mult, ALU.mult, s_nrm)
                if j >= 1:
                    dve.wait_ge(s_nrm, KB * n + j)
                    dve.wait_ge(s_nhi, KB * n + j)
                    tt(u_lo[:, j - 1, :], dst(j - 1), u_hi[:, j - 1, :].bitcast(F32), ALU.subtract, s_nlo)
        x_blk = lambda j: acc[:, j, :]
        norm(0, p0[:, 3, :], x_blk, x_blk, A_RG)

        dve.wait_ge(s_spv, len(steps))
        dve.wait_ge(s_const_dve, 1)

        def tails(pre, n, inc):
            o = cso[:, bass.ds(n, 1), :].rearrange("p a s -> p (a s)")
            V.tensor_copy(o[:, 0:TAIL], pre[:, SEQ:SEQ + TAIL]).then_inc(inc, 1)
            V.tensor_copy(o[:, TAIL:], pre[:, COLS:COLS + TAIL]).then_inc(inc, 1)

        def rg(n):
            V.tensor_copy(rp[:], small[:, bass.ds(13 * n + S_RG, 13)]).then_inc(r_rp, 1)
            V.tensor_copy(rc8[:], c8[:, 0, bass.ds(n, 1)]).then_inc(r_rp, 1)
            dve.wait_ge(r_rp, 2 * n + 2)
            dve.wait_ge(s_drA, A_RG + 2 * n + 1)
            V.tensor_copy(rpre[:, SAMPLE0:SAMPLE0 + TAIL], rp[:, 8:8 + TAIL]).then_inc(r_pad, 1)
            tails(rpre, n, r_cs)
            for k in range(1, CONV_W):
                dve.wait_ge(r_tap0, n + 1)
                if k > 1:
                    dve.wait_ge(r_conv, TAIL * n + k - 1)
                stt(acc[:, XC, :], rpre[:, k:k + COLS], rp[:, k:k + 1], acc[:, XC, :], ALU.mult, ALU.add, r_conv)
            dve.wait_ge(r_xhi, n + 1)
            dve.wait_ge(r_conv, TAIL * n + TAIL)
            tt(rx_lo[:], acc[:, XC, :], rx_hi[:].bitcast(F32), ALU.subtract, r_xlo)
            dve.wait_ge(r_sq, n + 1)
            stt(acc[:, SQ, :], acc[:, SQ, :], 1.0 / GELU_C, acc[:, G, :], ALU.add, ALU.mult, r_inner)
            dve.wait_ge(s_drB, B_RG + 2 * n + 2)
            tt(acc[:, I, :], acc[:, I, :], acc[:, XC, :], ALU.mult, r_ix)
            dve.wait_ge(r_a, n + 1)
            tt(acc[:, GG, :], acc[:, R, :], acc[:, R, :], ALU.mult, r_a2)
            dve.wait_ge(r_a2, n + 1)
            stt(acc[:, TH, :], acc[:, GG, :], 1.0, acc[:, TH, :], ALU.add, ALU.mult, r_p)
            dve.wait_ge(r_gain, n + 1)
            dve.wait_ge(r_ix, n + 1 + FREE)
            tt(acc[:, I, :], acc[:, I, :], acc[:, TH, :], ALU.mult, r_b)
            dve.wait_ge(r_b, n + 1)
            V.memset(acc[:, R, CARRY:CARRY + 1], 0.0).then_inc(r_fix, 1)
            V.tensor_copy(acc[:, I, CARRY:CARRY + 1], rp[:, 11:12]).then_inc(r_fix, 1)
            dve.wait_ge(r_fix, 2 * n + 2)
            V.tensor_tensor_scan(acc[:, H, :], acc[:, R, :], acc[:, I, :], 0.0, ALU.mult, ALU.add)\
                .then_inc(r_scan, 1)
            dve.wait_ge(r_tg, n + 1)
            stt(acc[:, GG, :], acc[:, SQ, :], 1.0, acc[:, G, :], ALU.add, ALU.mult, r_gg)
            dve.wait_ge(r_scan, n + 1)
            o = hso[:, bass.ds(n, 1), :].rearrange("p a s -> p (a s)")
            V.tensor_copy(o[:, 0:1], acc[:, H, SEQ - 1:SEQ]).then_inc(r_hs, 1)
            V.tensor_copy(o[:, 1:2], acc[:, H, COLS - 1:COLS]).then_inc(r_hs, 1)
            dve.wait_ge(r_gg, n + 1 + FREE)
            stt(acc[:, GG, :], acc[:, GG, :], 0.5, acc[:, H, :], ALU.mult, ALU.mult, r_y)
            dve.wait_ge(r_y, n + 1)
            dve.wait_ge(r_yhi, n + 1)
            tt(blk(ya_lo, n), acc[:, GG, :], blk(ya_hi, n).bitcast(F32), ALU.subtract, r_ylo)
        loop(dve, KB, rg)

        row = lambda j, s=slice(0, COLS): acc[0:HEADS, j, s]
        pr, gap, sa = slice(0, SEQ), slice(SEQ, SAMPLE0), slice(SAMPLE0, COLS)
        chunks = lambda ap: ap.rearrange("p (c t) -> p c t", t=CH)

        def ends(j, first, n):
            e = acc[0:HEADS, j, first:first + CH * n].rearrange("p (c t) -> p c t", t=CH)[:, :, CH - 1:CH]
            return e.broadcast_to([HEADS, n, CH])

        row_steps = [
            lambda: V.scalar_tensor_tensor(row(EM), row(LF), -1.0, row(LF), ALU.mult, ALU.max),
            lambda: V.scalar_tensor_tensor(row(LF), row(LF), 0.0, row(EM), ALU.min, ALU.subtract),
            lambda: V.tensor_tensor_scan(row(FF), row(MASK), row(LF), 0.0, ALU.mult, ALU.add),
            lambda: V.tensor_tensor(row(EE), row(IG), row(FF), ALU.subtract),
            lambda: V.memset(row(LF, slice(CARRY, CARRY + 1)), -1e30),
            lambda: V.tensor_copy(row(IG, slice(CARRY, CARRY + 1)), small[0:HEADS, S_M0:S_M0 + 1]),
            lambda: V.tensor_tensor_scan(row(MM), row(LF), row(IG), 0.0, ALU.add, ALU.max),
            lambda: V.tensor_copy(mso[:, 0:1], row(MM, slice(SEQ - 1, SEQ))),
            lambda: V.tensor_copy(mso[:, 1:2], row(MM, slice(COLS - 1, COLS))),
            lambda: V.tensor_tensor(row(AR), row(FF), row(MM), ALU.subtract),
            lambda: V.tensor_copy(row(LF, slice(0, CH)), row(AR, slice(0, CH))),
            lambda: V.tensor_tensor(chunks(row(LF, slice(CH, SEQ))), chunks(row(AR, slice(CH, SEQ))),
                                    ends(MM, 0, SEQ // CH - 1), ALU.add),
            lambda: V.memset(row(LF, gap), 0.0),
            lambda: V.tensor_scalar(row(LF, sa), row(AR, sa), row(MM, slice(CARRY, CARRY + 1)), None, ALU.add),
            lambda: V.tensor_tensor(chunks(row(MASK, pr)), chunks(row(EE, pr)), ends(AR, 0, SEQ // CH), ALU.add),
            lambda: V.memset(row(MASK, gap), 0.0),
            lambda: V.tensor_scalar(row(MASK, sa), row(EE, sa), row(AR, slice(COLS - 1, COLS)), None, ALU.add),
            lambda: V.memset(row(AR, gap), 0.0),
        ]
        assert len(row_steps) == ROWS_DVE
        dve.wait_ge(w_act, 1)
        dve.wait_ge(s_drA, A_AO)
        for k, step in enumerate(row_steps):
            if k:
                dve.wait_ge(w_dve, k)
            if k == 1:
                dve.wait_ge(w_act, 3)
            if k == 2:
                dve.wait_ge(s_rowmask, 16)
            step().then_inc(w_dve, 1)

        def ao(i):
            for half in range(2):
                n = 2 * i + half
                dve.wait_ge(s_drB, B_AO + n + 1)
                dve.wait_ge(ao_st[half], 16 * i + 16)
                tt(as3(acc[:, AO_STAGE[half], :]), slot_a, as3(acc[:, IG, :]), ALU.mult, s_drA)
        loop(dve, KB // 2, ao)

        dve.wait_ge(w_tr, 1)
        V.tensor_copy(ecol[:].rearrange("p r c h -> p (r c h)"), ps[:, 6, 0:2 * NCH * HEADS]).then_inc(w_col, 1)
        dve.wait_ge(w_col, 1)
        V.memset(ecol[0:CH - DEC_SEQ, 1, NCH - 1, :], 0.0).then_inc(w_colz, 1)
        dve.wait_ge(w_st, 48)
        for half in range(2):
            dve.wait_ge(ao_st[half], 16 * (KB // 2) + 16)
        V.memset(acc[:], 0.0).then_inc(s_zero, 1)
        dve.wait_ge(w_colz, 1)
        dve.wait_ge(s_zero, 1)

        def xm(h):
            V.tensor_copy(bp[:].rearrange("p a b -> p (a b)"), small[:, bass.ds(16 * h + S_ML, 16)])\
                .then_inc(m_bp, 1)
            dve.wait_ge(m_bp, h + 1)
            for cb in range(2):
                dve.wait_ge(m_pre, 2 * h + cb + 1)
                V.tensor_copy(preq[:, SAMPLE0:SAMPLE0 + TAIL], bp[:, cb, 5:5 + TAIL]).then_inc(m_pad, 1)
                V.memset(preq[:, 0:TAIL], 0.0).then_inc(m_pad, 1)
                tails(preq, 2 * h + cb + KB, m_cs2)
                dve.wait_ge(m_xhi, 2 * h + cb + 1)
                tt(as3(xm_lo[:, cb, :]), slots[cb], as3(xm_hi[:, cb, :].bitcast(F32)), ALU.subtract, s_dr[cb])
                for k in range(1, CONV_W):
                    dve.wait_ge(m_tap0, 2 * h + cb + 1)
                    if k > 1:
                        dve.wait_ge(m_conv, TAIL * (2 * h + cb) + k - 1)
                    stt(conv1, preq[:, k:k + COLS], bp[:, cb, k:k + 1], conv1, ALU.mult, ALU.add, m_conv)
                dve.wait_ge(m_sig, 2 * h + cb + 1)
                tt(conv1, conv1, conv2, ALU.mult, m_silu)
                dve.wait_ge(m_chi, 2 * h + cb + 1)
                tt(xc_lo[:, cb, :], conv1, xc_hi[:, cb, :].bitcast(F32), ALU.subtract, m_clo)
        xm(0)

        def head(h, last):
            c0, a0, b0 = W_HEAD + PER_HEAD * h, A_HD + 8 * h, B_HD + 8 * h
            V.tensor_copy(hcol[:].rearrange("p r c -> p (r c)"),
                          ecol[:, :, :, bass.ds(h, 1)].rearrange("p r c a -> p (r c a)")).then_inc(m_hcol, 1)
            V.tensor_copy(csm[:, DV:], small[:, bass.ds(h + S_N0, 1)].broadcast_to([P, P])).then_inc(m_cs, 1)
            dve.wait_ge(m_bc, 16 * h + 16)
            V.tensor_copy(dec[:, 0:NCH - 1], bc[:, 1, CH - 1:SEQ:CH]).then_inc(m_dec, 1)
            V.tensor_copy(dec[:, NCH - 1:], bc[:, 1, COLS - 1:COLS]).then_inc(m_dec, 1)
            dve.wait_ge(m_hcol, h + 1)
            for c in range(NCH):
                t, n = slice(COL0[c], COL0[c] + CLEN[c]), CLEN[c]
                mask = small[:, S_MASK:S_MASK + n] if c < NCH - 1 else small[:, S_MASK8:S_MASK8 + n]
                stt(bc[:, 0, t], bc[:, 0, t], hcol[:, 0, c:c + 1], mask, ALU.add, ALU.add, m_mask)
            dve.wait_ge(s_drA, a0 + 2)
            dve.wait_ge(m_dec, 2 * h + 2)
            tt(bc[:, 1, :], bc[:, 1, :], preq[:, 0:COLS], ALU.mult, m_qw)

            def weigh(c):
                t0, n = COL0[c], CLEN[c]
                dve.wait_ge(m_s_mm, NCH * h + c + 1)
                dve.wait_ge(m_e, 2 * h + 2)
                if c >= 2:
                    dve.wait_ge(m_o_mm, NCH * h + c - 1)
                tt(sw[:, c % 2, 0:n], ps[:, 6 + c % 2, 0:n], bc[:, 0, t0:t0 + n], ALU.mult, m_sw)

            weigh(0)
            weigh(1)
            for c in range(NCH):
                t0, n = COL0[c], CLEN[c]
                dve.wait_ge(m_u_mm, NCH * h + c + 1)
                new = ps[:, c % 2, 0:DV + P]
                if c == 0:
                    dve.wait_ge(m_cout, 32 * h + 16)
                    V.tensor_copy(cst[:, 1, :], new).then_inc(m_c, 1)
                elif c < NCH - 1:
                    dve.wait_ge(m_c, NCH * h + c)
                    stt(cst[:, (c + 1) % 2, :], cst[:, c % 2, :], dec[:, c:c + 1], new, ALU.mult, ALU.add, m_c)
                else:
                    dve.wait_ge(m_c0, 16 * h + 16)
                    dve.wait_ge(m_cs, h + 1)
                    stt(cst[:, 1, :], csm[:], dec[:, c:c + 1], new, ALU.mult, ALU.add, m_c)
                dve.wait_ge(m_o_mm, NCH * h + c + 1)
                r = bc[:, 2, t0:t0 + n]
                d = ps[:, 3 + c % 2, 2 * P:2 * P + n]
                stt(r, d, -1.0, r, ALU.mult, ALU.max, m_rec)
                dve.wait_ge(m_rec, 3 * (NCH * h + c) + 1)
                tt(r, d, r, ALU.max, m_rec)
                dve.wait_ge(m_rec, 3 * (NCH * h + c) + 2)
                V.reciprocal(r, r).then_inc(m_rec, 1)
                dve.wait_ge(m_rec, 3 * (NCH * h + c) + 3)
                o = ps[:, 3 + c % 2, 0:2 * P].rearrange("p (j t) -> p j t", j=2)[:, :, 0:n]
                rb = bc[:, 2:3, t0:t0 + n].broadcast_to([P, 2, n])
                tt(bc[:, 0:2, t0:t0 + n], o, rb, ALU.mult, m_hn)
                if c + 2 < NCH:
                    weigh(c + 2)
            o = nso[:, bass.ds(h, 1), :].rearrange("p a s -> p (a s)")
            dve.wait_ge(m_c, NCH * (h + 1))
            for s in range(2):
                V.tensor_copy(o[:, s:s + 1], cst[:, s, DV:DV + 1]).then_inc(m_no, 1)
            if not last:
                xm(h + 1)
            d = 3 if last else 4
            dve.wait_ge(m_hn, NCH * (h + 1))
            dve.wait_ge(s_drA, a0 + d)
            tt(bc[:, 0, :], bc[:, 0, :], kz[:], ALU.mult, m_y)
            dve.wait_ge(s_drB, b0 + d)
            tt(bc[:, 1, :], bc[:, 1, :], preq[:, 0:COLS], ALU.mult, m_y)
            for cb in range(2):
                dve.wait_ge(m_y, 2 * h + cb + 1)
                dve.wait_ge(m_yhi, 2 * h + cb + 1)
                tt(yb_lo[:, cb, :], bc[:, cb, :], yb_hi[:, cb, :].bitcast(F32), ALU.subtract, m_ylo)
            cy = c0 + (6 if last else 10)
            for m in range(KB):
                if m % 2 == 0:
                    dve.wait_ge(s_bb, 4 * h + m // 2 + 1)
                else:
                    dve.wait_ge(s_chunk, cy + m // 2 + 1)
                tt(as3(acc[:, m, :]), slots[m % 2], as3(acc[:, m, :]), ALU.add, s_dr[m % 2])
        loop(dve, HEADS - 1, lambda h: head(h, False))
        head(HEADS - 1, True)

        dve.wait_ge(s_drA, A_GB)
        dve.wait_ge(s_drB, B_GB)

        def gb(i):
            for half in range(2):
                n = 2 * i + half
                dve.wait_ge(s_dr[half], (A_GB, B_GB)[half] + i + 1)
                tt(tmp[:, half, :], tmp[:, half, :], blk(acc, n), ALU.mult, g_t)
                dve.wait_ge(g_t, n + 1)
                dve.wait_ge(g_in[half], 16 * i + 16)
                tt(tmp[:, half, :], tmp[:, half, :], tmp[:, 2 + half, :], ALU.add, g_mix)
                dve.wait_ge(g_mix, n + 1)
                dve.wait_ge(g_hi, n + 1)
                tt(blk(act_lo, n), tmp[:, half, :], blk(act_hi, n).bitcast(F32), ALU.subtract, g_lo)
        loop(dve, KB // 2, gb)

        V.memset(tmp[:, 2, :], 0.0).then_inc(s_zero, 1)
        dve.wait_ge(s_zero, 2)

        def wo(i):
            for half in range(2):
                n = 2 * i + half
                dve.wait_ge(s_chunk, W_OUT + 2 * n + 2)
                dve.wait_ge(o_in[half], 16 * i + 16)
                tt(as3(blk(acc, n)), slots[half], as3(tmp[:, half, :]), ALU.add, s_dr[half])
                dve.wait_ge(o_sq, n + 1)
                tt(tmp[:, 2, :], tmp[:, 2, :], tmp[:, 3, :], ALU.add, o_ssum)
                dve.wait_ge(o_ssum, n + 1)
        loop(dve, KB // 2, wo)
        norm(1, tmp[:, 3, :], x_blk, lambda j: tmp[:, j % 2, :], A_ML)

        def up(g):
            def pair(i):
                for half in range(2):
                    j = 8 * g + 2 * i + half
                    dve.wait_ge(s_dr[half], (A_ML, B_ML)[half] + 8 * g + i + 1)
                    tt(tmp[:, 2 + half, :], tmp[:, half, :], tmp[:, half, :], ALU.mult, h_s)
                    dve.wait_ge(h_s, j + 1 + 2 * FREE)
                    dve.wait_ge(h_hi, j + 1)
                    tt(blk(act_lo, 2 * i + half), tmp[:, 2 + half, :],
                       blk(act_hi, 2 * i + half).bitcast(F32), ALU.subtract, h_lo)
            loop(dve, KB // 2, pair)

        def add(g, i, half):
            dve.wait_ge(s_chunk, W_MLP + 32 * g + 16 + 4 * i + 2 * half + 2)
            o = as3(blk(acc, 2 * i + half))
            tt(o, slots[half], o, ALU.add, s_dr[half])

        def group(g):
            up(g)

            def down(i):
                for half in range(2):
                    add(g, i, half)
            loop(dve, KB // 2, down)
        loop(dve, GROUPS - 1, group)
        up(GROUPS - 1)
        V.memset(tmp[:, 2, :], 0.0).then_inc(s_zero, 1)
        dve.wait_ge(s_zero, 3)

        def down_last(i):
            for half in range(2):
                add(GROUPS - 1, i, half)
                dve.wait_ge(f_sq, 2 * i + half + 1)
                tt(tmp[:, 2, :], tmp[:, 2, :], tmp[:, half, :], ALU.add, f_ssum)
                dve.wait_ge(f_ssum, 2 * i + half + 1)
        loop(dve, KB // 2, down_last)
        dve.wait_ge(s_drA, A_N3 + 1)
        V.reciprocal(tmp[:, 3, :], tmp[:, 3, :]).then_inc(s_rstd, 1)
        dve.wait_ge(s_rstd, 3)
        for j in range(KB):
            g = S_GAIN + 2 * KB + j
            stt(acc[:, j, :], acc[:, j, :], small[:, g:g + 1], tmp[:, 3, :], ALU.mult, ALU.mult, f_y)

    outer.close()


def kernel(**inputs):
    import concourse.bacc as _bacc
    from concourse.bass_utils import run_bass_kernel_spmd as _run

    x = {k: np.asarray(v) for k, v in inputs.items()}
    f32 = np.float32

    cols = np.zeros((D_MODEL, COLS), f32)
    cols[:, :SEQ] = x["x_prompt"][0].T
    cols[:, SAMPLE0:] = x["x_sample"][0].T
    x_t = cols.reshape(KB, P, COLS)

    def tiles(w):
        k, m = w.shape
        t = w.reshape(k // (4 * P), 4, P, m // P, P).transpose(3, 0, 2, 1, 4)
        return t.reshape(m // P, k // (4 * P), P, CHUNK)

    w_in = x["w_in"][0]
    at = np.cumsum([0, D_RNN, D_RNN, D_ML, D_ML, HEADS, HEADS, D_MODEL, D_MODEL])
    xr, gr, xm, zm = (tiles(w_in[:, at[i]:at[i + 1]]) for i in range(4))
    ga, gb = (tiles(w_in[:, at[i]:at[i + 1]]) for i in (6, 7))
    gates = np.zeros((D_MODEL, P), f32)
    gates[:, 0:HEADS] = w_in[:, at[4]:at[5]]
    gates[:, 32:32 + HEADS] = w_in[:, at[5]:at[6]]
    wa, wx = x["rglru_wa"][0], x["rglru_wx"][0]
    wpa, wout = tiles(x["w_branch_a"][0]), tiles(x["w_out"][0])
    wpb, wup = x["w_branch_b"][0], tiles(x["w_mlp_up"][0])
    wdn = tiles(x["w_mlp_down"][0])
    wq, wk, wv = x["mlstm_wq"][0], x["mlstm_wk"][0], x["mlstm_wv"][0]
    ch = []
    for n in range(KB):
        pair = np.zeros((1, P, CHUNK), f32)
        pair[0, :, 0:P], pair[0, :, P:2 * P] = wa[n], wx[n]
        ch += [xr[n], gr[n], pair]
    ch += [tiles(gates)[0]]
    for n in range(KB):
        ch += [wpa[n], ga[n]]
    ch += [xm[0], xm[1]]
    for h in range(HEADS):
        v = wv[h].reshape(2, P, DV).transpose(1, 0, 2).reshape(1, P, CHUNK)
        qk = np.stack([wq[h].reshape(2, P, DK), wk[h].reshape(2, P, DK)])
        ch += [v, qk.transpose(2, 0, 1, 3).reshape(1, P, CHUNK)]
        if h + 1 < HEADS:
            ch += [xm[2 * h + 2], xm[2 * h + 3]]
        ch += [zm[2 * h], zm[2 * h + 1]]
        b = wpb[h * DV:(h + 1) * DV].reshape(2, P, 4, 2, P).transpose(2, 1, 3, 0, 4)
        ch += [b.reshape(4, P, CHUNK)]
    ch += [gb[n] for n in range(KB)] + [wout[n] for n in range(KB)]
    for g in range(GROUPS):
        ch += [wup[KB * g + j] for j in range(KB)]
        ch += [wdn[n, 2 * g:2 * g + 2] for n in range(KB)]
    w = np.concatenate(ch)
    assert w.shape == (W_END, P, CHUNK)

    small = np.zeros((P, S_COLS), f32)
    small[:, S_ID:S_ID + P] = np.eye(P, dtype=f32)
    key, query = np.arange(P)[:, None], np.arange(P)[None, :]
    small[:, S_MASK:S_MASK + P] = np.where(key <= query, 0.0, -1e30)
    shift = key - (P - DEC_SEQ)
    small[:, S_MASK8:S_MASK8 + DEC_SEQ] = np.where((shift >= 0) & (shift <= query[:, :DEC_SEQ]), 0.0, -1e30)
    rg = np.zeros((KB, P, 13), f32)
    rg[:, :, 0:4] = x["conv_rglru_w"][0].reshape(CONV_W, KB, P).transpose(1, 2, 0)
    for i, k in ((4, "conv_rglru_b"), (5, "rglru_ba"), (6, "rglru_bx"), (7, "rglru_lambda")):
        rg[:, :, i] = x[k][0].reshape(KB, P)
    rg[:, :, 8:11] = x["state_rglru_conv"][0, 0].reshape(TAIL, KB, P).transpose(1, 2, 0)
    rg[:, :, 11] = x["state_rglru_h"][0, 0].reshape(KB, P)
    small[:, S_RG:S_ML] = rg.transpose(1, 0, 2).reshape(P, -1)
    ml = np.zeros((2 * HEADS, P, 8), f32)
    ml[:, :, 0:4] = x["conv_mlstm_w"][0].reshape(CONV_W, 2 * HEADS, P).transpose(1, 2, 0)
    ml[:, :, 4] = x["conv_mlstm_b"][0].reshape(2 * HEADS, P)
    ml[:, :, 5:8] = x["state_mlstm_conv"][0, 0].reshape(TAIL, 2 * HEADS, P).transpose(1, 2, 0)
    small[:, S_ML:S_GAIN] = ml.transpose(1, 0, 2).reshape(P, -1)
    gains = np.stack([x["norm_mix"][0], x["norm_mlp"][0], x["norm_final"]])
    small[:, S_GAIN:S_N0] = gains.reshape(3, KB, P).transpose(2, 0, 1).reshape(P, -1)
    small[:, S_N0:S_BIF] = x["state_mlstm_n"][0, 0].T
    small[0:HEADS, S_BIF] = x["b_if"][0, :HEADS]
    small[32:32 + HEADS, S_BIF] = x["b_if"][0, HEADS:]
    small[0:HEADS, S_M0] = x["state_mlstm_m"][0, 0]
    rowmask = np.ones((HEADS, COLS), f32)
    rowmask[:, COL0 + [SEQ]] = 0.0

    nc = _bacc.Bacc("TRN2", target_bir_lowering=False, num_devices=1)
    arrays = {
        "x_t": x_t, "small": small, "rowmask": rowmask, "w": w,
        "c0": np.ascontiguousarray(x["state_mlstm_C"][0, 0].transpose(0, 2, 1)),
    }
    given = {k: nc.dram_tensor("in_" + k, v.shape, F32, kind="ExternalInput").ap() for k, v in arrays.items()}
    made = {k: nc.dram_tensor("out_" + k, s, F32, kind=kind).ap() for k, s, kind in (
        ("rows", (HEADS, 3, COLS), "Internal"), ("mixa", (KB, P, COLS), "Internal"),
        ("y", (KB, P, COLS), "ExternalOutput"), ("conv", (P, 24, 6), "ExternalOutput"),
        ("hlast", (P, KB, 2), "ExternalOutput"), ("c", (2 * HEADS, P, DV), "ExternalOutput"),
        ("n", (P, HEADS, 2), "ExternalOutput"), ("m", (HEADS, 2), "ExternalOutput"))}
    build(nc, given["x_t"], given["small"], given["rowmask"], given["w"], given["c0"], made["rows"],
          made["mixa"], made["y"], made["conv"], made["hlast"], made["c"], made["n"], made["m"])
    r = _run(nc, [{"in_" + k: np.ascontiguousarray(v) for k, v in arrays.items()}], core_ids=[0]).results[0]

    y = r["out_y"].reshape(D_MODEL, COLS).T
    c = r["out_c"].reshape(2, HEADS, P, DV).transpose(0, 1, 3, 2)
    out = [np.ascontiguousarray(y[None, :SEQ]), np.ascontiguousarray(y[None, SAMPLE0:])]
    for s in range(2):
        conv = r["out_conv"][:, :, TAIL * s:TAIL * s + TAIL].transpose(2, 1, 0)
        out += [
            conv[:, :KB].reshape(1, 1, TAIL, D_RNN),
            r["out_hlast"][:, :, s].T.reshape(1, 1, D_RNN),
            conv[:, KB:].reshape(1, 1, TAIL, D_ML),
            c[s].reshape(1, 1, HEADS, DV, DK),
            r["out_n"][:, :, s].T.reshape(1, 1, HEADS, DK),
            r["out_m"][:, s].reshape(1, 1, HEADS),
        ]
    return tuple(np.ascontiguousarray(o) for o in out)
```

```python
from contextlib import ExitStack

import numpy as np

import concourse.bass as bass
from concourse import mybir

F32 = mybir.dt.float32
F32R = mybir.dt.float32r
ACT = mybir.ActivationFunctionType
ALU = mybir.AluOpType

P = 128
D_MODEL = 1024
SEQ = 1024
DEC_SEQ = 64
CONV_W = 4
TAIL = CONV_W - 1
HEADS = 8
DK = 128
DV = 256
D_RNN = 1024
D_ML = HEADS * DV
D_FF = 4 * D_MODEL
EPS = 1e-6
RG_C = 8.0

KB = D_MODEL // P
GAP = 4
SAMPLE0 = SEQ + GAP
CARRY = SAMPLE0 - 1
COLS = SAMPLE0 + DEC_SEQ
TILES = 3
TW = COLS // TILES
BANK = 512
CH = 128
NCH = SEQ // CH + 1
KEY0 = [CH * c for c in range(NCH - 1)] + [COLS - CH]
COL0 = [CH * c for c in range(NCH - 1)] + [SAMPLE0]
VW = DV + 1
CLEN = [CH] * (NCH - 1) + [DEC_SEQ]

CHUNK = 512
W_RG = 0
W_GATES = W_RG + 5 * KB
W_AO = W_GATES + 2
W_X0 = W_AO + 4 * KB
W_HEAD = W_X0 + 4
PER_HEAD = 14
W_GB = W_HEAD + PER_HEAD * HEADS - 4
W_OUT = W_GB + 2 * KB
W_MLP = W_OUT + 2 * KB
GROUPS = D_FF // D_MODEL
W_END = W_MLP + 32 * GROUPS

A_RG, B_RG = 1, 1
A_G = A_RG + 2 * KB
B_G = B_RG + 2 * KB
A_AO, B_AO = A_G + 1, B_G
A_X0, B_X0 = A_AO + KB, B_AO + KB
A_HD, B_HD = A_X0 + 1, B_X0 + 1
A_GB, B_GB = A_HD + 8 * HEADS - 1, B_HD + 8 * HEADS - 1
A_WO, B_WO = A_GB + 4, B_GB + 4
A_ML, B_ML = A_WO + 4, B_WO + 4
A_N2 = A_ML + 4
A_N3 = A_ML + 8 * GROUPS + 1

S_ID = 0
S_MASK = 128
S_MASK8 = 256
S_RG = 320
S_ML = S_RG + 8 * 13
S_GAIN = S_ML + 16 * 8
S_N0 = S_GAIN + 24
S_BIF = S_N0 + 8
S_M0 = S_BIF + 1
S_COLS = S_M0 + 1

XC, R, I, TH, G, SQ, H, GG = range(8)
IG, LF, EM, FF, MASK, MM, AR, EE = range(8)
ROWS_DVE, ROWS_ACT = 18, 6

FREE = 1

GELU_C = 0.044715
GELU_K = 0.7978845608028654


def build(nc, x_t, small_d, rowmask_d, w_d, c0_d, rows_d, mixa_d, y_d, conv_d, hlast_d, c_d, n_d, m_d):
    outer = ExitStack()
    sb_in = lambda st, name, shape, dt=F32: st.enter_context(nc.sbuf_tensor(name, shape, dt))
    sb = lambda name, shape, dt=F32: sb_in(outer, name, shape, dt)
    sem = lambda name: outer.enter_context(nc.semaphore(name))

    ps = outer.enter_context(nc.psum_tensor("ps", [P, 8, BANK], F32))
    slot_a, slot_b = ps[:, 0:3, 0:TW], ps[:, 3:6, 0:TW]
    slots = [slot_a, slot_b]

    u_hi = sb("u_hi", [P, KB, COLS], F32R)
    u_lo = sb("u_lo", [P, KB, COLS], F32R)
    acc = sb("acc", [P, KB, COLS])
    w_raw = sb("w_raw", [P, 2, CHUNK])
    w_hi = sb("w_hi", [P, 2, CHUNK], F32R)
    w_lo = sb("w_lo", [P, 2, CHUNK], F32R)
    small = sb("small", [P, S_COLS])
    ones = sb("ones", [P, P])
    eps_c = sb("eps_c", [P, 1])
    warm = sb("warm", [P, 1])
    c8 = sb("c8", [P, 8, KB])
    rp = sb("rp", [P, 13])
    rc8 = sb("rc8", [P, 1])
    bp = sb("bp", [P, 2, 8])
    ecol = sb("ecol", [P, 2, NCH, HEADS])
    hcol = sb("hcol", [P, 2, NCH])
    dec = sb("dec", [P, NCH])
    cso = sb("cso", [P, 24, 6])
    hso = sb("hso", [P, KB, 2])
    nso = sb("nso", [P, HEADS, 2])
    mso = sb("mso", [HEADS, 2])

    with ExitStack() as st:
        p0 = sb_in(st, "p0", [P, 4, COLS])
    with ExitStack() as st:
        ya_hi = sb_in(st, "ya_hi", [P, KB, COLS], F32R)
        ya_lo = sb_in(st, "ya_lo", [P, KB, COLS], F32R)
        rpre = sb_in(st, "rpre", [P, COLS + TAIL])
        rx_hi = sb_in(st, "rx_hi", [P, COLS], F32R)
        rx_lo = sb_in(st, "rx_lo", [P, COLS], F32R)
    with ExitStack() as st:
        yb_hi = sb_in(st, "yb_hi", [P, 2, COLS], F32R)
        yb_lo = sb_in(st, "yb_lo", [P, 2, COLS], F32R)
        xm_hi = sb_in(st, "xm_hi", [P, 2, COLS], F32R)
        xm_lo = sb_in(st, "xm_lo", [P, 2, COLS], F32R)
        xc_hi = sb_in(st, "xc_hi", [P, 2, COLS], F32R)
        xc_lo = sb_in(st, "xc_lo", [P, 2, COLS], F32R)
        preq = sb_in(st, "preq", [P, COLS + TAIL])
        vt = sb_in(st, "vt", [P, NCH * VW])
        bc = sb_in(st, "bc", [P, 4, COLS])
        cst = sb_in(st, "cst", [P, 2, VW])
        csm = sb_in(st, "csm", [P, VW])
        kt = sb_in(st, "kt", [P, 2, P])
        sw = sb_in(st, "sw", [P, 2, P])
        zw = sb_in(st, "zw", [P, 2, P])
    with ExitStack() as st:
        act_hi = sb_in(st, "act_hi", [P, KB, COLS], F32R)
        act_lo = sb_in(st, "act_lo", [P, KB, COLS], F32R)
        tmp = sb_in(st, "tmp", [P, 4, COLS])
    kz = bc[:, 2, :]
    vt3 = vt[:].rearrange("p (c v) -> p c v", v=VW)
    conv1, conv2 = vt[:, 0:COLS], vt[:, COLS:2 * COLS]

    s_small, s_rowmask, s_raw0, s_raw1 = sem("small_in"), sem("rowmask_in"), sem("raw0_in"), sem("raw1_in")
    s_raw = [s_raw0, s_raw1]
    s_x = [sem(f"x_in{j}") for j in range(KB)]
    s_whi, s_wlo = sem("chunk_hi"), sem("chunk_split")
    s_chunk = sem("chunk_multiplied")
    s_drA, s_drB = sem("slot_a_drained"), sem("slot_b_drained")
    s_dr = [s_drA, s_drB]
    s_half = sem("half_chunk_multiplied")
    s_va, s_k_mm, s_r_mm, s_bb = sem("v_first_mm"), sem("k_mm"), sem("r_mm"), sem("branch_b_even_mm")
    s_out = sem("stored")
    s_const, s_const_dve = sem("constants_set"), sem("pads_zeroed")
    r_cs, r_hs, m_cs2, m_dec = sem("rg_tails"), sem("rg_h_out"), sem("ml_tails"), sem("ml_decays")
    s_sq, s_ssum, s_norm, s_std, s_rstd, s_nrm, s_nhi, s_nlo = [sem(n) for n in (
        "squared", "squares_summed", "norm_mm", "std", "rstd", "normed", "normed_hi", "normed_lo")]
    s_sp, s_spv = sem("softplus_act"), sem("softplus_dve")
    (r_pre, r_tap0, r_g, r_xhi, r_sq, r_th, r_tg, r_a, r_gain, r_yhi) = [sem("rg_" + n) for n in (
        "pre", "tap0", "g", "x_hi", "sq", "th", "tg", "a", "gain", "y_hi")]
    (r_rp, r_pad, r_conv, r_xlo, r_inner, r_ix, r_a2, r_p, r_b, r_fix, r_scan, r_gg, r_y, r_ylo) = [
        sem("rg_" + n) for n in ("params", "pads", "conv", "x_lo", "inner", "ix", "a2", "p", "b", "carry",
                                 "scan", "gg", "y", "y_lo")]
    w_act, w_dve, w_tr, w_col, w_colz, w_st = [sem("rows_" + n) for n in (
        "act", "dve", "transposed", "cols", "cols_zeroed", "stored")]
    ao_st = sem("mix_a_stored")
    (m_pre, m_xhi, m_tap0, m_sig, m_chi, m_v, m_e, m_kt, m_zs, m_yhi) = [sem("ml_" + n) for n in (
        "pre", "x_hi", "tap0", "sig", "c_hi", "v", "e", "kt", "zs", "y_hi")]
    (m_bp, m_pad, m_conv, m_silu, m_clo, m_hcol, m_mask, m_qw, m_sw, m_c, m_rec, m_hn, m_y, m_ylo,
     m_cs, m_no) = [sem("ml_" + n) for n in (
         "params", "pads", "conv", "silu", "c_lo", "head_cols", "masked", "qw", "scores_w", "state", "rec",
         "h", "y", "y_lo", "sample_n", "n_out")]
    m_s_mm, m_u_mm, m_o_mm = sem("scores_mm"), sem("state_mm"), sem("h_mm")
    m_one, m_z, m_oe = sem("ml_v_ones"), sem("ml_z"), sem("ml_o_out")
    m_bc, m_c0, m_cout = sem("rows_in"), sem("sample_state_in"), sem("states_stored")
    s_zero = sem("branch_b_zeroed")
    s_warm = sem("table_loaded")
    g_t, g_mix, g_hi, g_lo = [sem("merge_" + n) for n in ("t", "mix", "hi", "lo")]
    g_in = [sem(f"mix_a_in{j}") for j in range(2)]
    o_in = [sem(f"x_again_in{j}") for j in range(2)]
    o_sq, o_ssum = sem("res_squared"), sem("res_ssum")
    h_acc = sem("mixer_added")
    h_r, h_hi, h_s, h_lo = sem("hid_relu"), sem("hid_hi"), sem("hid_sq"), sem("hid_lo")
    f_sq, f_ssum, f_y = sem("final_squared"), sem("final_ssum"), sem("final_y")

    block = outer.enter_context(nc.Block())

    def as3(ap):
        return ap.rearrange("p (a b) -> p a b", a=TILES)

    def blk(t, n):
        if isinstance(n, int):
            return t[:, n, :]
        return t[:, bass.ds(n, 1), :].rearrange("p a c -> p (a c)")

    def gain2(n):
        if isinstance(n, int):
            return small[:, S_GAIN + KB + n:S_GAIN + KB + n + 1]
        return small[:, bass.ds(n + S_GAIN + KB, 1)]

    def a_up(g, half):
        return (A_ML if isinstance(g, int) and g == 0 else A_ML + 1, B_ML)[half] + 8 * g

    def loop(eng, n, body):
        with eng.Fori(0, n) as i:
            body(i)

    @block.sync
    def _(sp):
        sp.dma_start(small[:], small_d).then_inc(s_small, 16)
        for j in range(KB):
            sp.dma_start(acc[:, j, :], x_t[j]).then_inc(s_x[j], 16)
        for c in range(2):
            sp.dma_start(w_raw[:, c, :], w_d[c]).then_inc(s_raw[c], 16)

        def more(i):
            for c in range(2):
                src = w_d[bass.ds(sp.snap(2 * i + 2 + c), 1)].rearrange("a p m -> p (a m)")
                sp.wait_ge(s_wlo, 2 * i + c + 1)
                sp.dma_start(w_raw[:, c, :], src).then_inc(s_raw[c], 16)
        loop(sp, W_END // 2 - 1, more)

        sp.wait_ge(r_cs, 2 * KB)
        sp.wait_ge(m_cs2, 4 * HEADS)
        sp.dma_start(conv_d, cso[:]).then_inc(s_out, 16)
        sp.wait_ge(r_hs, 2 * KB)
        sp.dma_start(hlast_d, hso[:]).then_inc(s_out, 16)
        sp.wait_ge(m_no, 2 * HEADS)
        sp.dma_start(n_d, nso[:]).then_inc(s_out, 16)
        sp.wait_ge(w_dve, ROWS_DVE)
        sp.dma_start(m_d, mso[:]).then_inc(s_out, 16)
        for j in range(KB):
            sp.wait_ge(f_y, j + 1)
            sp.dma_start(y_d[j], acc[:, j, :]).then_inc(s_out, 16)
        sp.wait_ge(s_out, 16 * (4 + KB))
        sp.wait_ge(m_cout, 32 * HEADS + 16)

    @block.gpsimd
    def _(pool):
        nc.gpsimd.memset(ones[:], 1.0).then_inc(s_const, 1)
        nc.gpsimd.memset(eps_c[:], EPS).then_inc(s_const, 1)
        one = ones[:, 0:1].broadcast_to([P, CHUNK])
        pool.wait_ge(s_const, 1)

        def split(c, j, first):
            pool.wait_ge(s_raw[c], 16 * j + 16)
            if not first:
                pool.wait_ge(s_chunk, 2 * j + c - 1)
            nc.gpsimd.tensor_tensor(w_hi[:, c, :], w_raw[:, c, :], one, ALU.mult).then_inc(s_whi, 1)
            pool.wait_ge(s_whi, 2 * j + c + 1)
            nc.gpsimd.tensor_tensor(w_lo[:, c, :], w_raw[:, c, :], w_hi[:, c, :].bitcast(F32),
                                    ALU.subtract).then_inc(s_wlo, 1)
        split(0, 0, True)
        split(1, 0, True)

        def both(i):
            split(0, i + 1, False)
            split(1, i + 1, False)
        loop(pool, W_END // 2 - 1, both)

    @block.tensor
    def _(pe):
        def product(slot, blocks, rhs_hi, rhs_lo, before=None, done=None):
            last_k = len(blocks) - 1
            for k, (chunk, ws, off, last) in enumerate(blocks):
                if chunk is not None:
                    pe.wait_ge(s_wlo, chunk + 1)
                if before is not None:
                    before(k)
                hi, lo = w_hi[:, ws, off:off + P], w_lo[:, ws, off:off + P]
                for n, (w, r) in enumerate(((hi, rhs_hi), (hi, rhs_lo), (lo, rhs_hi))):
                    for t in range(TILES):
                        mm = nc.tensor.matmul(slots[slot][:, t, :], w, r(k)[:, t * TW:(t + 1) * TW],
                                              start=(k == 0 and n == 0), stop=(k == last_k and n == 2))
                if last:
                    mm.then_inc(s_chunk, 1)
                elif k == last_k and done is not None:
                    mm.then_inc(done, 1)

        def full(chunk):
            return [(chunk + k // 4 if k % 4 == 0 else None, k // 4, (k % 4) * P, k % 4 == 3) for k in range(KB)]

        def full_odd(chunk):
            return [(c, 1 - ws, off, last) for c, ws, off, last in full(chunk)]

        U = (lambda k: u_hi[:, k, :], lambda k: u_lo[:, k, :])

        def norm_sum(src, wait):
            wait()
            for t in range(TILES):
                mm = nc.tensor.matmul(slot_a[:, t, :], ones[:], src[:, t * TW:(t + 1) * TW], start=True, stop=True)
            mm.then_inc(s_norm, 1)

        def n1():
            pe.wait_ge(s_const, 2)
            pe.wait_ge(s_ssum, KB)
        norm_sum(p0[:, 2, :], n1)

        def rg(i):
            for half in range(2):
                c = W_RG + 10 * i + 5 * half
                pick = full_odd if half else full
                a0, b0 = A_RG + 4 * i + 2 * half, B_RG + 4 * i + 2 * half
                pe.wait_ge(s_drA, a0)
                product(0, pick(c), *U, before=lambda k: pe.wait_ge(s_nlo, k + 1))
                pe.wait_ge(s_drB, b0)
                product(1, pick(c + 2), *U)
                x = (lambda k: rx_hi[:], lambda k: rx_lo[:])
                pe.wait_ge(s_drA, a0 + 1)
                pe.wait_ge(r_xlo, 2 * i + half + 1)
                product(0, [(c + 4, half, 0, False)], *x, done=s_r_mm)
                pe.wait_ge(s_drB, b0 + 1)
                product(1, [(None, half, P, True)], *x)
        loop(pe, KB // 2, rg)

        pe.wait_ge(s_drA, A_G)
        product(0, full(W_GATES), *U)

        def ao(n):
            pe.wait_ge(s_drB, B_AO + n)
            product(1, full(W_AO + 4 * n), *U)
            pe.wait_ge(s_drA, A_AO + n)
            product(0, full(W_AO + 4 * n + 2), lambda k: ya_hi[:, k, :], lambda k: ya_lo[:, k, :],
                    before=lambda k: pe.wait_ge(r_ylo, k + 1 + FREE))
        loop(pe, KB, ao)

        pe.wait_ge(w_dve, ROWS_DVE)
        pe.wait_ge(w_act, ROWS_ACT)
        for r, row in enumerate((EE, MASK)):
            for c in range(NCH):
                o = (r * NCH + c) * HEADS
                mm = nc.tensor.transpose(ps[:, 6, o:o + HEADS], acc[0:HEADS, row, KEY0[c]:KEY0[c] + CH],
                                         small[0:HEADS, S_ID:S_ID + HEADS])
        mm.then_inc(w_tr, 1)

        def xm(chunk, a, b):
            pe.wait_ge(s_drA, a)
            product(0, full(chunk), *U)
            pe.wait_ge(s_drB, b)
            product(1, full(chunk + 2), *U)
        xm(W_X0, A_X0, B_X0)
        pe.wait_ge(w_colz, 1)

        def head(h, last):
            c0, a0, b0 = W_HEAD + PER_HEAD * h, A_HD + 8 * h, B_HD + 8 * h
            C = (lambda k: xc_hi[:, k, :], lambda k: xc_lo[:, k, :])
            pe.wait_ge(s_drA, a0)
            product(0, [(c0, 0, 0, False), (None, 0, P, False)], *C,
                    before=lambda k: pe.wait_ge(m_clo, 2 * h + k + 1), done=s_k_mm)
            pe.wait_ge(s_drB, b0)
            product(1, [(None, 0, 2 * P, False), (None, 0, 3 * P, True)], *C)

            pe.wait_ge(s_wlo, c0 + 2)
            pe.wait_ge(s_drA, a0 + 1)
            for c in range(NCH):
                if c == 6:
                    pe.wait_ge(s_drB, b0 + 1)
                out = ps[:, c // 2, (c % 2) * DV:(c % 2 + 1) * DV]
                k0 = KEY0[c]
                for cb in range(2):
                    wv_hi, wv_lo = (w[:, 1, cb * DV:(cb + 1) * DV] for w in (w_hi, w_lo))
                    x_hi, x_lo = (x[:, cb, k0:k0 + CH] for x in (xm_hi, xm_lo))
                    for n, (l, r) in enumerate(((x_hi, wv_hi), (x_hi, wv_lo), (x_lo, wv_hi))):
                        mm = nc.tensor.matmul(out, l, r, start=(cb == 0 and n == 0), stop=(cb == 1 and n == 2))
                if c == 5:
                    mm.then_inc(s_va, 1)
            mm.then_inc(s_chunk, 1)

            def scores(c):
                if c == 0:
                    pe.wait_ge(s_drB, b0 + 1)
                    pe.wait_ge(s_drA, a0 + 2)
                k0, t0, n = KEY0[c], COL0[c], CLEN[c]
                nc.tensor.matmul(ps[:, 6 + c % 2, 0:n], kz[:, k0:k0 + CH], preq[:, t0:t0 + n], start=True, stop=True)
                nc.tensor.transpose(ps[:, 2 + 3 * (c % 2), 0:P], kz[:, k0:k0 + CH],
                                    small[:, S_ID:S_ID + P]).then_inc(m_s_mm, 1)

            scores(0)
            scores(1)
            pe.wait_ge(m_one, h + 1)
            pe.wait_ge(m_qw, h + 1)
            for c in range(NCH):
                t0, n = COL0[c], CLEN[c]
                pe.wait_ge(m_kt, NCH * h + c + 1)
                if c >= 2:
                    pe.wait_ge(m_c, NCH * h + c - 1)
                nc.tensor.matmul(ps[:, c % 2, 0:VW], kt[:, c % 2, :], vt3[:, c, :],
                                 start=True, stop=True).then_inc(m_u_mm, 1)
                pe.wait_ge(m_sw, NCH * h + c + 1)
                if c == 0:
                    pe.wait_ge(s_drB, b0 + 2)
                else:
                    if c < NCH - 1:
                        pe.wait_ge(m_c, NCH * h + c)
                    else:
                        pe.wait_ge(m_c0, 16 * h + 16)
                if c >= 2:
                    pe.wait_ge(m_oe, NCH * h + c - 1)
                state = None if c == 0 else csm if c == NCH - 1 else cst[:, c % 2, :]
                for j in range(2):
                    out = ps[:, 3 + c % 2, j * P:j * P + n]
                    nc.tensor.matmul(out, vt3[:, c, j * P:(j + 1) * P], sw[:, c % 2, 0:n],
                                     start=True, stop=state is None)
                    if state is not None:
                        nc.tensor.matmul(out, state[:, j * P:(j + 1) * P], bc[:, 1, t0:t0 + n],
                                         start=False, stop=True)
                if c:
                    pe.wait_ge(m_z, (NCH - 1) * h + c)
                nc.tensor.matmul(ps[:, 3 + c % 2, 2 * P:2 * P + n], ones[:], (zw if c else sw)[:, c % 2, 0:n],
                                 start=True, stop=True).then_inc(m_o_mm, 1)
                if c + 2 < NCH:
                    scores(c + 2)
            pe.wait_ge(m_c, NCH * h + NCH)
            c1 = c0 + 2
            product(0, full(c1), *U)
            pe.wait_ge(m_oe, NCH * h + NCH)
            product(1, full(c1 + 2), *U)
            c1, a1, b1 = c1 + 4, a0 + 3, b0 + 3
            if not last:
                xm(c1, a1, b1)
                c1, a1, b1 = c1 + 4, a1 + 1, b1 + 1
            Y = (lambda k: yb_hi[:, k, :], lambda k: yb_lo[:, k, :])
            for m in range(KB):
                ws, off = (m // 2) % 2, (m % 2) * 2 * P
                first = c1 + m // 2 if m % 2 == 0 else None
                pe.wait_ge(s_dr[m % 2], (b1 if m % 2 else a1) + m // 2)
                product(m % 2, [(first, ws, off, False), (None, ws, off + P, m % 2 == 1)], *Y,
                        before=lambda k: pe.wait_ge(m_ylo, 2 * h + k + 1), done=s_bb)
        loop(pe, HEADS - 1, lambda h: head(h, False))
        head(HEADS - 1, True)

        def gb(i):
            for half in range(2):
                pe.wait_ge(s_dr[half], (A_GB, B_GB)[half] + i)
                product(half, full(W_GB + 4 * i + 2 * half), *U)
        loop(pe, KB // 2, gb)
        A = (lambda k: act_hi[:, k, :], lambda k: act_lo[:, k, :])

        def wo(i):
            for half in range(2):
                pe.wait_ge(s_dr[half], (A_WO, B_WO)[half] + i)
                product(half, full(W_OUT + 4 * i + 2 * half), *A, before=lambda k: pe.wait_ge(g_lo, k + 1))
        loop(pe, KB // 2, wo)

        def up(g, a):
            def pair(i):
                for half in range(2):
                    pe.wait_ge(s_dr[half], (a, B_ML)[half] + 8 * g + i)
                    product(half, full(W_MLP + 32 * g + 4 * i + 2 * half), *U,
                            before=lambda k: pe.wait_ge(s_nlo, KB + k + 1))
            loop(pe, KB // 2, pair)

        def down(g):
            def pair(i):
                for half in range(2):
                    pe.wait_ge(s_dr[half], (A_ML + 1, B_ML)[half] + 8 * g + 4 + i)
                    product(half, full(W_MLP + 32 * g + 16 + 4 * i + 2 * half), *A,
                            before=lambda k: pe.wait_ge(h_lo, 8 * g + k + 1 + FREE))
            loop(pe, KB // 2, pair)

        def n2():
            pe.wait_ge(s_drA, A_N2)
            pe.wait_ge(o_ssum, KB)

        def group(g):
            up(g, A_ML + 1)
            down(g)
        up(0, A_ML)
        norm_sum(tmp[:, 3, :], n2)
        down(0)
        with pe.Fori(1, GROUPS) as g:
            group(g)

        def n3():
            pe.wait_ge(s_drA, A_N3)
            pe.wait_ge(f_ssum, KB)
        norm_sum(tmp[:, 1, :], n3)

    @block.scalar
    def _(act):
        def a(out, in_, f, inc, **kw):
            nc.scalar.activation(out, in_, f, **kw).then_inc(inc, 1)

        act.sem_inc(s_drB, 1)
        act.sem_inc(ao_st, 16)
        act.sem_inc(m_cout, 16)
        act.wait_ge(s_const, 2)
        act.wait_ge(s_small, 16)

        for j in range(KB):
            act.wait_ge(s_x[j], 16)
            if j >= 2:
                act.wait_ge(s_ssum, j - 1)
            a(p0[:, j % 2, :], acc[:, j, :], ACT.Square, s_sq)

        act.wait_ge(s_spv, 1)
        a(c8[:, 2, :], c8[:, 1, :], ACT.Exp, s_sp, scale=-1.0)

        def std(n, dst):
            act.wait_ge(s_norm, n + 1)
            nc.scalar.activation(as3(dst), slot_a, ACT.Sqrt, scale=1.0 / D_MODEL, bias=eps_c[:, 0:1])\
                .then_inc(s_drA, 1)
        std(0, p0[:, 3, :])
        for j in range(KB):
            act.wait_ge(s_nrm, j + 1)
            a(u_hi[:, j, :], acc[:, j, :], ACT.Copy, s_nhi)

        def convolve(n):
            act.wait_ge(s_chunk, W_RG + 5 * n + 2)
            nc.scalar.activation(as3(rpre[:, TAIL:]), slot_a, ACT.Copy).then_inc(s_drA, 1)
            act.wait_ge(r_pad, n + 1)
            a(acc[:, XC, :], rpre[:, 0:COLS], ACT.Identity, r_tap0, scale=rp[:, 0:1], bias=rp[:, 4:5])

        def x_hi(n):
            act.wait_ge(r_conv, TAIL * n + TAIL)
            a(rx_hi[:], acc[:, XC, :], ACT.Copy, r_xhi)

        def gr_out(n):
            act.wait_ge(s_chunk, W_RG + 5 * n + 4)
            nc.scalar.activation(as3(acc[:, G, :]), slot_b, ACT.Copy).then_inc(s_drB, 1)

        def gates_out(n):
            act.wait_ge(s_r_mm, n + 1)
            nc.scalar.activation(as3(acc[:, R, :]), slot_a, ACT.Sigmoid, bias=rp[:, 5:6]).then_inc(s_drA, 1)
            act.wait_ge(s_chunk, W_RG + 5 * n + 5)
            nc.scalar.activation(as3(acc[:, I, :]), slot_b, ACT.Sigmoid, bias=rp[:, 6:7]).then_inc(s_drB, 1)

        def y_hi(n):
            act.wait_ge(r_y, n + 1)
            a(blk(ya_hi, n), acc[:, GG, :], ACT.Copy, r_yhi)

        def rg(n, last):
            act.wait_ge(s_drB, B_RG + 2 * n + 1)
            a(acc[:, SQ, :], acc[:, G, :], ACT.Square, r_sq)
            act.wait_ge(s_drA, A_RG + 2 * n + 2)
            a(acc[:, TH, :], acc[:, R, :], ACT.Tanh, r_th, scale=rc8[:, 0:1])
            act.wait_ge(r_inner, n + 1)
            a(acc[:, SQ, :], acc[:, SQ, :], ACT.Tanh, r_tg, scale=GELU_C * GELU_K)
            act.wait_ge(r_th, n + 1)
            a(acc[:, R, :], acc[:, R, :], ACT.Exp, r_a, scale=rc8[:, 0:1])
            if not last:
                act.wait_ge(r_ix, n + 1)
                convolve(n + 1)
            act.wait_ge(r_p, n + 1)
            a(acc[:, TH, :], acc[:, TH, :], ACT.Sqrt, r_gain, scale=-1.0)
            if not last:
                x_hi(n + 1)
                nc.scalar.activation(warm[:], eps_c[:], ACT.Sigmoid).then_inc(s_warm, 1)
                act.wait_ge(r_gg, n + 1)
                gr_out(n + 1)
                act.wait_ge(r_scan, n + 1)
                gates_out(n + 1)
            y_hi(n)
        convolve(0)
        x_hi(0)
        gr_out(0)
        gates_out(0)
        loop(act, KB - 1, lambda n: rg(n, False))
        rg(KB - 1, True)

        act.wait_ge(r_ylo, KB + FREE)
        act.dma_start(acc[0:HEADS, MASK, :], rowmask_d).then_inc(s_rowmask, 16)
        act.wait_ge(s_chunk, W_GATES + 2)
        row = lambda j: acc[0:HEADS, j, :]
        nc.scalar.activation(as3(row(IG)), slot_a[0:HEADS], ACT.Identity,
                             bias=small[0:HEADS, S_BIF:S_BIF + 1]).then_inc(w_act, 1)
        nc.scalar.activation(as3(row(LF)), slot_a[32:32 + HEADS], ACT.Identity,
                             bias=small[32:32 + HEADS, S_BIF:S_BIF + 1]).then_inc(s_drA, 1)

        def ao(n):
            act.wait_ge(s_chunk, W_AO + 4 * n + 2)
            act.wait_ge(ao_st, 16 * n + 16)
            nc.scalar.activation(as3(rpre[:, 0:COLS]), slot_b, ACT.Sigmoid).then_inc(s_drB, 1)
            dst = mixa_d[bass.ds(n, 1)].rearrange("a p c -> p (a c)")
            act.wait_ge(s_drA, A_AO + n + 1)
            act.dma_start(dst, rpre[:, 0:COLS]).then_inc(ao_st, 16)

        act.wait_ge(w_dve, 1)
        a(row(EM), row(EM), ACT.Exp, w_act, scale=-1.0)
        act.wait_ge(w_act, 2)
        a(row(EM), row(EM), ACT.Ln, w_act, bias=ones[0:HEADS, 0:1])
        ao(0)
        act.wait_ge(w_dve, 7)
        a(row(EM), row(MM), ACT.Exp, w_act, scale=-1.0)
        act.wait_ge(w_dve, 14)
        a(row(LF), row(LF), ACT.Exp, w_act)
        act.wait_ge(w_dve, ROWS_DVE)
        a(row(MASK), row(MASK), ACT.Exp, w_act)
        act.wait_ge(w_act, ROWS_ACT)
        for n, r in enumerate((AR, LF, EM)):
            act.dma_start(rows_d[:, n, :], row(r)).then_inc(w_st, 16)
        with act.Fori(1, KB) as n:
            ao(n)

        def xm(h, chunk):
            for cb in range(2):
                act.wait_ge(s_chunk, chunk + 2 * cb + 2)
                a(as3(preq[:, TAIL:]), slots[cb], ACT.Copy, m_pre)
                a(as3(xm_hi[:, cb, :]), slots[cb], ACT.Copy, m_xhi)
                act.wait_ge(m_pad, 4 * h + 2 * cb + 2)
                if cb:
                    act.wait_ge(m_clo, 2 * h + 1)
                a(conv1, preq[:, 0:COLS], ACT.Identity, m_tap0, scale=bp[:, cb, 0:1], bias=bp[:, cb, 4:5])
                act.wait_ge(m_conv, TAIL * (2 * h + cb) + TAIL)
                a(conv2, conv1, ACT.Sigmoid, m_sig)
                act.wait_ge(m_silu, 2 * h + cb + 1)
                a(xc_hi[:, cb, :], conv1, ACT.Copy, m_chi)

        def load_head(h):
            one = bass.ds(h, 1)
            src = rows_d[one].rearrange("a r c -> a (r c)")
            act.dma_start(bc[:, 0:2, :].rearrange("p r c -> p (r c)"),
                          src[:, 0:2 * COLS].broadcast_to([P, 2 * COLS])).then_inc(m_bc, 16)
            act.dma_start(bc[:, 3, :], src[:, 2 * COLS:].broadcast_to([P, COLS])).then_inc(m_bc, 16)
            act.dma_start(csm[:, 0:DV], c0_d[one].rearrange("a p v -> p (a v)")).then_inc(m_c0, 16)

        act.wait_ge(s_chunk, W_X0 + 2)
        act.wait_ge(w_st, 48)
        act.wait_ge(ao_st, 16 * KB + 16)
        load_head(0)
        xm(0, W_X0)

        flat = ps[:].rearrange("p a b -> p (a b)")

        def head(h, last):
            c0 = W_HEAD + PER_HEAD * h
            act.wait_ge(s_k_mm, h + 1)
            nc.scalar.activation(as3(kz), slot_a, ACT.Copy).then_inc(s_drA, 1)
            act.wait_ge(s_chunk, c0 + 1)
            nc.scalar.activation(as3(preq[:, 0:COLS]), slot_b, ACT.Copy, scale=float(DK) ** -0.5)\
                .then_inc(s_drB, 1)
            act.wait_ge(m_mask, NCH * (h + 1))
            for s in (slice(0, SEQ), slice(SAMPLE0, COLS)):
                a(bc[:, 0, s], bc[:, 0, s], ACT.Exp, m_e)
            act.wait_ge(s_va, h + 1)
            act.wait_ge(m_clo, 2 * h + 2)
            half_v = lambda lo, n: flat[:, lo * BANK:lo * BANK + n * DV].rearrange("p (c v) -> p c v", v=DV)
            nc.scalar.activation(vt3[:, 0:6, 0:DV], half_v(0, 6), ACT.Copy).then_inc(s_drA, 1)
            act.wait_ge(s_chunk, c0 + 2)
            nc.scalar.activation(vt3[:, 6:NCH, 0:DV], half_v(3, NCH - 6), ACT.Copy).then_inc(s_drB, 1)

            def keys(c):
                act.wait_ge(m_s_mm, NCH * h + c + 1)
                if c >= 2:
                    act.wait_ge(m_u_mm, NCH * h + c - 1)
                a(kt[:, c % 2, :], ps[:, 2 + 3 * (c % 2), 0:P], ACT.Copy, m_kt, scale=hcol[:, 1, c:c + 1])
            keys(0)
            keys(1)
            for c in range(NCH):
                t0, n = COL0[c], CLEN[c]
                act.wait_ge(m_o_mm, NCH * h + c + 1)
                o = ps[:, 3 + c % 2, 0:3 * P].rearrange("p (j t) -> p j t", j=3)[:, :, 0:n]
                a(bc[:, 0:3, t0:t0 + n], o, ACT.Copy, m_oe)
                if c + 2 < NCH:
                    keys(c + 2)
            act.wait_ge(m_c, NCH * (h + 1))
            for s in range(2):
                act.dma_start(c_d[bass.ds(h + HEADS * s, 1)].rearrange("a p v -> p (a v)"), cst[:, s, 0:DV])\
                   .then_inc(m_cout, 16)
            act.wait_ge(s_chunk, c0 + 4)
            act.wait_ge(m_rec, 3 * h + 2)
            nc.scalar.activation(as3(kz), slot_a, ACT.Sigmoid).then_inc(s_drA, 1)
            act.wait_ge(s_chunk, c0 + 6)
            nc.scalar.activation(as3(preq[:, 0:COLS]), slot_b, ACT.Sigmoid).then_inc(s_drB, 1)
            for cb in range(2):
                act.wait_ge(m_y, 2 * h + cb + 1)
                a(yb_hi[:, cb, :], bc[:, cb, :], ACT.Copy, m_yhi)
            if not last:
                act.wait_ge(m_ylo, 2 * h + 2)
                act.wait_ge(m_o_mm, NCH * (h + 1))
                load_head(h + 1)
                xm(h + 1, c0 + 6)
        loop(act, HEADS - 1, lambda h: head(h, False))
        head(HEADS - 1, True)

        act.wait_ge(s_drB, B_GB)
        act.wait_ge(s_drA, A_GB)
        act.wait_ge(m_cout, 32 * HEADS + 16)

        def load(dram, n, dst, inc):
            act.dma_start(dst, dram[bass.ds(n, 1)].rearrange("a p c -> p (a c)")).then_inc(inc, 16)

        for half in range(2):
            load(mixa_d, half, tmp[:, 2 + half, :], g_in[half])

        def gb(i, last):
            for half in range(2):
                n = 2 * i + half
                act.wait_ge(s_chunk, W_GB + 2 * n + 2)
                nc.scalar.activation(as3(tmp[:, half, :]), slots[half], ACT.Sigmoid).then_inc(s_dr[half], 1)
                act.wait_ge(g_mix, n + 1)
                a(blk(act_hi, n), tmp[:, half, :], ACT.Copy, g_hi)
                if not last:
                    load(mixa_d, n + 2, tmp[:, 2 + half, :], g_in[half])
        loop(act, KB // 2 - 1, lambda i: gb(i, False))
        gb(KB // 2 - 1, True)

        act.wait_ge(g_lo, KB)
        for half in range(2):
            load(x_t, half, tmp[:, half, :], o_in[half])

        def wo(i, last):
            for half in range(2):
                n = 2 * i + half
                act.wait_ge(s_dr[half], (A_WO, B_WO)[half] + i + 1)
                a(blk(u_hi, n), blk(acc, n), ACT.Identity, s_nhi, scale=gain2(n))
                a(tmp[:, 2, :], blk(acc, n), ACT.Square, o_sq)
                if not last:
                    load(x_t, n + 2, tmp[:, half, :], o_in[half])
        loop(act, KB // 2 - 1, lambda i: wo(i, False))
        wo(KB // 2 - 1, True)

        def up(g):
            def pair(i):
                for half in range(2):
                    j = 8 * g + 2 * i + half
                    act.wait_ge(s_chunk, W_MLP + 32 * g + 4 * i + 2 * half + 2)
                    act.wait_ge(h_s, j - 1 + 2 * FREE)
                    nc.scalar.activation(as3(tmp[:, half, :]), slots[half], ACT.Relu).then_inc(s_dr[half], 1)
                    act.wait_ge(s_dr[half], a_up(g, half) + i + 1)
                    a(blk(act_hi, 2 * i + half), tmp[:, half, :], ACT.Square, h_hi)
            loop(act, KB // 2, pair)
        up(0)
        act.wait_ge(s_norm, 2)
        nc.scalar.activation(as3(tmp[:, 3, :]), slot_a, ACT.Identity, scale=1.0 / D_MODEL, bias=eps_c[:, 0:1])\
            .then_inc(s_drA, 1)
        with act.Fori(1, GROUPS) as g:
            up(g)

        def final(i):
            for half in range(2):
                n = 2 * i + half
                act.wait_ge(h_acc, KB * (GROUPS - 1) + n + 1 + FREE)
                a(tmp[:, 0, :], blk(acc, n), ACT.Square, f_sq)
        loop(act, KB // 2, final)
        std(2, tmp[:, 3, :])

    @block.vector
    def _(dve):
        V = nc.vector

        def stt(out, in0, scalar, in1, op0, op1, inc):
            V.scalar_tensor_tensor(out, in0, scalar, in1, op0, op1).then_inc(inc, 1)

        def tt(out, in0, in1, op, inc):
            V.tensor_tensor(out, in0, in1, op).then_inc(inc, 1)

        dve.sem_inc(r_ylo, FREE)
        dve.sem_inc(h_s, 2 * FREE)
        dve.sem_inc(h_lo, FREE)
        dve.sem_inc(h_acc, FREE)
        V.memset(rpre[:, 0:TAIL], 0.0).then_inc(s_const_dve, 1)
        dve.wait_ge(s_small, 16)

        lam = small[:, S_RG + 7:S_RG + 13 * KB:13]
        c = [c8[:, j, :] for j in range(8)]
        steps = [
            lambda: V.scalar_tensor_tensor(c[1], lam, -1.0, lam, ALU.mult, ALU.max),
            lambda: V.tensor_scalar(c[3], c[2], 2.0, None, ALU.add),
            lambda: V.reciprocal(c[4], c[3]),
            lambda: V.tensor_tensor(c[5], c[2], c[4], ALU.mult),
            lambda: V.tensor_tensor(c[6], c[5], c[5], ALU.mult),
            lambda: V.tensor_scalar(c[7], c[6], 1.0 / 15, None, ALU.mult),
        ] + [
            (lambda k=k: V.scalar_tensor_tensor(c[7], c[7], 1.0 / k, c[6], ALU.add, ALU.mult))
            for k in (13, 11, 9, 7, 5, 3)
        ] + [
            lambda: V.scalar_tensor_tensor(c[3], c[7], 1.0, c[5], ALU.add, ALU.mult),
            lambda: V.tensor_tensor(c[4], c[1], lam, ALU.subtract),
            lambda: V.tensor_scalar(c[4], c[4], -RG_C / 2, None, ALU.mult),
            lambda: V.scalar_tensor_tensor(c[0], c[3], -2 * RG_C, c[4], ALU.mult, ALU.add),
        ]
        steps[0]().then_inc(s_spv, 1)

        for j in range(KB):
            dve.wait_ge(s_sq, j + 1)
            if j == 0:
                V.tensor_copy(p0[:, 2, :], p0[:, 0, :]).then_inc(s_ssum, 1)
            else:
                dve.wait_ge(s_ssum, j)
                tt(p0[:, 2, :], p0[:, 2, :], p0[:, j % 2, :], ALU.add, s_ssum)
        dve.wait_ge(s_sp, 1)
        for k, step in enumerate(steps[1:]):
            dve.wait_ge(s_spv, k + 1)
            step().then_inc(s_spv, 1)

        def norm(n, scale, src, dst, drained):
            dve.wait_ge(s_drA, drained)
            V.reciprocal(scale, scale).then_inc(s_rstd, 1)
            dve.wait_ge(s_rstd, n + 1)
            for j in range(KB + 1):
                if j < KB:
                    g = S_GAIN + KB * n + j
                    if j >= 2:
                        dve.wait_ge(s_nlo, KB * n + j - 1)
                    stt(dst(j), src(j), small[:, g:g + 1], scale, ALU.mult, ALU.mult, s_nrm)
                if j >= 1:
                    dve.wait_ge(s_nrm, KB * n + j)
                    dve.wait_ge(s_nhi, KB * n + j)
                    tt(u_lo[:, j - 1, :], dst(j - 1), u_hi[:, j - 1, :].bitcast(F32), ALU.subtract, s_nlo)
        x_blk = lambda j: acc[:, j, :]
        norm(0, p0[:, 3, :], x_blk, x_blk, A_RG)

        dve.wait_ge(s_spv, len(steps))
        dve.wait_ge(s_const_dve, 1)

        def tails(pre, n, inc):
            o = cso[:, bass.ds(n, 1), :].rearrange("p a s -> p (a s)")
            V.tensor_copy(o[:, 0:TAIL], pre[:, SEQ:SEQ + TAIL]).then_inc(inc, 1)
            V.tensor_copy(o[:, TAIL:], pre[:, COLS:COLS + TAIL]).then_inc(inc, 1)

        def convolve(n):
            V.tensor_copy(rp[:], small[:, bass.ds(13 * n + S_RG, 13)]).then_inc(r_rp, 1)
            V.tensor_copy(rc8[:], c8[:, 0, bass.ds(n, 1)]).then_inc(r_rp, 1)
            dve.wait_ge(r_rp, 2 * n + 2)
            dve.wait_ge(s_drA, A_RG + 2 * n + 1)
            V.tensor_copy(rpre[:, SAMPLE0:SAMPLE0 + TAIL], rp[:, 8:8 + TAIL]).then_inc(r_pad, 1)
            tails(rpre, n, r_cs)
            for k in range(1, CONV_W):
                dve.wait_ge(r_tap0, n + 1)
                if k > 1:
                    dve.wait_ge(r_conv, TAIL * n + k - 1)
                stt(acc[:, XC, :], rpre[:, k:k + COLS], rp[:, k:k + 1], acc[:, XC, :], ALU.mult, ALU.add, r_conv)

        def x_lo(n):
            dve.wait_ge(r_xhi, n + 1)
            dve.wait_ge(r_conv, TAIL * n + TAIL)
            tt(rx_lo[:], acc[:, XC, :], rx_hi[:].bitcast(F32), ALU.subtract, r_xlo)

        def inner(n):
            dve.wait_ge(r_sq, n + 1)
            stt(acc[:, SQ, :], acc[:, SQ, :], 1.0 / GELU_C, acc[:, G, :], ALU.add, ALU.mult, r_inner)

        def ix(n):
            dve.wait_ge(s_drB, B_RG + 2 * n + 2)
            tt(acc[:, I, :], acc[:, I, :], acc[:, XC, :], ALU.mult, r_ix)

        def rg(n, last):
            inner(n)
            dve.wait_ge(r_tg, n + 1)
            dve.wait_ge(r_ylo, n + FREE)
            stt(acc[:, GG, :], acc[:, SQ, :], 1.0, acc[:, G, :], ALU.add, ALU.mult, r_gg)
            dve.wait_ge(r_a, n + 1)
            tt(acc[:, H, :], acc[:, R, :], acc[:, R, :], ALU.mult, r_a2)
            dve.wait_ge(r_a2, n + 1)
            stt(acc[:, TH, :], acc[:, H, :], 1.0, acc[:, TH, :], ALU.add, ALU.mult, r_p)
            if not last:
                convolve(n + 1)
            dve.wait_ge(r_gain, n + 1)
            dve.wait_ge(r_ix, n + 1)
            tt(acc[:, I, :], acc[:, I, :], acc[:, TH, :], ALU.mult, r_b)
            dve.wait_ge(r_b, n + 1)
            V.memset(acc[:, R, CARRY:CARRY + 1], 0.0).then_inc(r_fix, 1)
            V.tensor_copy(acc[:, I, CARRY:CARRY + 1], h0(n)).then_inc(r_fix, 1)
            if not last:
                x_lo(n + 1)
            dve.wait_ge(r_fix, 2 * n + 2)
            V.tensor_tensor_scan(acc[:, H, :], acc[:, R, :], acc[:, I, :], 0.0, ALU.mult, ALU.add)\
                .then_inc(r_scan, 1)
            dve.wait_ge(r_scan, n + 1)
            o = hso[:, bass.ds(n, 1), :].rearrange("p a s -> p (a s)")
            V.tensor_copy(o[:, 0:1], acc[:, H, SEQ - 1:SEQ]).then_inc(r_hs, 1)
            V.tensor_copy(o[:, 1:2], acc[:, H, COLS - 1:COLS]).then_inc(r_hs, 1)
            dve.wait_ge(r_gg, n + 1)
            stt(acc[:, GG, :], acc[:, GG, :], 0.5, acc[:, H, :], ALU.mult, ALU.mult, r_y)
            if not last:
                ix(n + 1)
            dve.wait_ge(r_y, n + 1)
            dve.wait_ge(r_yhi, n + 1)
            tt(blk(ya_lo, n), acc[:, GG, :], blk(ya_hi, n).bitcast(F32), ALU.subtract, r_ylo)

        h0 = lambda n: small[:, bass.ds(13 * n + S_RG + 11, 1)]
        convolve(0)
        x_lo(0)
        ix(0)
        loop(dve, KB - 1, lambda n: rg(n, False))
        rg(KB - 1, True)

        row = lambda j, s=slice(0, COLS): acc[0:HEADS, j, s]
        pr, gap, sa = slice(0, SEQ), slice(SEQ, SAMPLE0), slice(SAMPLE0, COLS)
        chunks = lambda ap: ap.rearrange("p (c t) -> p c t", t=CH)

        def ends(j, first, n):
            e = acc[0:HEADS, j, first:first + CH * n].rearrange("p (c t) -> p c t", t=CH)[:, :, CH - 1:CH]
            return e.broadcast_to([HEADS, n, CH])

        row_steps = [
            lambda: V.scalar_tensor_tensor(row(EM), row(LF), -1.0, row(LF), ALU.mult, ALU.max),
            lambda: V.scalar_tensor_tensor(row(LF), row(LF), 0.0, row(EM), ALU.min, ALU.subtract),
            lambda: V.tensor_tensor_scan(row(FF), row(MASK), row(LF), 0.0, ALU.mult, ALU.add),
            lambda: V.tensor_tensor(row(EE), row(IG), row(FF), ALU.subtract),
            lambda: V.memset(row(LF, slice(CARRY, CARRY + 1)), -1e30),
            lambda: V.tensor_copy(row(IG, slice(CARRY, CARRY + 1)), small[0:HEADS, S_M0:S_M0 + 1]),
            lambda: V.tensor_tensor_scan(row(MM), row(LF), row(IG), 0.0, ALU.add, ALU.max),
            lambda: V.tensor_copy(mso[:, 0:1], row(MM, slice(SEQ - 1, SEQ))),
            lambda: V.tensor_copy(mso[:, 1:2], row(MM, slice(COLS - 1, COLS))),
            lambda: V.tensor_tensor(row(AR), row(FF), row(MM), ALU.subtract),
            lambda: V.tensor_copy(row(LF, slice(0, CH)), row(AR, slice(0, CH))),
            lambda: V.tensor_tensor(chunks(row(LF, slice(CH, SEQ))), chunks(row(AR, slice(CH, SEQ))),
                                    ends(MM, 0, SEQ // CH - 1), ALU.add),
            lambda: V.memset(row(LF, gap), 0.0),
            lambda: V.tensor_scalar(row(LF, sa), row(AR, sa), row(MM, slice(CARRY, CARRY + 1)), None, ALU.add),
            lambda: V.tensor_tensor(chunks(row(MASK, pr)), chunks(row(EE, pr)), ends(AR, 0, SEQ // CH), ALU.add),
            lambda: V.memset(row(MASK, gap), 0.0),
            lambda: V.tensor_scalar(row(MASK, sa), row(EE, sa), row(AR, slice(COLS - 1, COLS)), None, ALU.add),
            lambda: V.memset(row(AR, gap), 0.0),
        ]
        assert len(row_steps) == ROWS_DVE
        dve.wait_ge(w_act, 1)
        dve.wait_ge(s_drA, A_AO)
        def some_rows(first, end):
            for k in range(first, end):
                if k:
                    dve.wait_ge(w_dve, k)
                if k == 1:
                    dve.wait_ge(w_act, 3)
                if k == 2:
                    dve.wait_ge(s_rowmask, 16)
                row_steps[k]().then_inc(w_dve, 1)

        def ao(n):
            dve.wait_ge(s_drB, B_AO + n + 1)
            dve.wait_ge(s_chunk, W_AO + 4 * n + 4)
            o = as3(rpre[:, 0:COLS])
            tt(o, slot_a, o, ALU.mult, s_drA)
        some_rows(0, 7)
        ao(0)
        some_rows(7, ROWS_DVE)
        with dve.Fori(1, KB) as n:
            ao(n)

        dve.wait_ge(w_tr, 1)
        V.tensor_copy(ecol[:].rearrange("p r c h -> p (r c h)"), ps[:, 6, 0:2 * NCH * HEADS]).then_inc(w_col, 1)
        dve.wait_ge(w_col, 1)
        V.memset(ecol[0:CH - DEC_SEQ, 1, NCH - 1, :], 0.0).then_inc(w_colz, 1)
        dve.wait_ge(w_st, 48)
        V.memset(acc[:], 0.0).then_inc(s_zero, 1)
        dve.wait_ge(w_colz, 1)
        dve.wait_ge(s_zero, 1)

        def xm(h, between=lambda step: None):
            V.tensor_copy(bp[:].rearrange("p a b -> p (a b)"), small[:, bass.ds(16 * h + S_ML, 16)])\
                .then_inc(m_bp, 1)
            dve.wait_ge(m_bp, h + 1)
            for cb in range(2):
                other = between if cb else (lambda step: None)
                dve.wait_ge(m_pre, 2 * h + cb + 1)
                V.tensor_copy(preq[:, SAMPLE0:SAMPLE0 + TAIL], bp[:, cb, 5:5 + TAIL]).then_inc(m_pad, 1)
                V.memset(preq[:, 0:TAIL], 0.0).then_inc(m_pad, 1)
                tails(preq, 2 * h + cb + KB, m_cs2)
                dve.wait_ge(m_xhi, 2 * h + cb + 1)
                tt(as3(xm_lo[:, cb, :]), slots[cb], as3(xm_hi[:, cb, :].bitcast(F32)), ALU.subtract, s_dr[cb])
                other(0)
                for k in range(1, CONV_W):
                    dve.wait_ge(m_tap0, 2 * h + cb + 1)
                    if k > 1:
                        dve.wait_ge(m_conv, TAIL * (2 * h + cb) + k - 1)
                    stt(conv1, preq[:, k:k + COLS], bp[:, cb, k:k + 1], conv1, ALU.mult, ALU.add, m_conv)
                    if k == 2:
                        other(1)
                other(2)
                dve.wait_ge(m_sig, 2 * h + cb + 1)
                tt(conv1, conv1, conv2, ALU.mult, m_silu)
                other(3)
                dve.wait_ge(m_chi, 2 * h + cb + 1)
                dve.wait_ge(m_silu, 2 * h + cb + 1)
                tt(xc_lo[:, cb, :], conv1, xc_hi[:, cb, :].bitcast(F32), ALU.subtract, m_clo)
        xm(0)

        def head(h, last):
            c0, a0, b0 = W_HEAD + PER_HEAD * h, A_HD + 8 * h, B_HD + 8 * h
            V.tensor_copy(hcol[:].rearrange("p r c -> p (r c)"),
                          ecol[:, :, :, bass.ds(h, 1)].rearrange("p r c a -> p (r c a)")).then_inc(m_hcol, 1)
            V.tensor_copy(csm[:, DV:], small[:, bass.ds(h + S_N0, 1)]).then_inc(m_cs, 1)
            dve.wait_ge(m_clo, 2 * h + 2)
            V.memset(vt3[:, :, DV:], 1.0).then_inc(m_one, 1)
            dve.wait_ge(m_bc, 32 * h + 32)
            V.tensor_copy(dec[:, 0:NCH - 1], bc[:, 1, CH - 1:SEQ:CH]).then_inc(m_dec, 1)
            V.tensor_copy(dec[:, NCH - 1:], bc[:, 1, COLS - 1:COLS]).then_inc(m_dec, 1)
            dve.wait_ge(m_hcol, h + 1)
            for c in range(NCH):
                t, n = slice(COL0[c], COL0[c] + CLEN[c]), CLEN[c]
                mask = small[:, S_MASK:S_MASK + n] if c < NCH - 1 else small[:, S_MASK8:S_MASK8 + n]
                stt(bc[:, 0, t], bc[:, 0, t], hcol[:, 0, c:c + 1], mask, ALU.add, ALU.add, m_mask)
            dve.wait_ge(s_drB, b0 + 1)
            dve.wait_ge(m_dec, 2 * h + 2)
            tt(bc[:, 1, :], bc[:, 1, :], preq[:, 0:COLS], ALU.mult, m_qw)

            def weigh(c):
                t0, n = COL0[c], CLEN[c]
                dve.wait_ge(m_s_mm, NCH * h + c + 1)
                dve.wait_ge(m_e, 2 * h + 2)
                if c >= 2:
                    dve.wait_ge(m_o_mm, NCH * h + c - 1)
                tt(sw[:, c % 2, 0:n], ps[:, 6 + c % 2, 0:n], bc[:, 0, t0:t0 + n], ALU.mult, m_sw)

            weigh(0)
            weigh(1)
            for c in range(NCH):
                t0, n = COL0[c], CLEN[c]
                dve.wait_ge(m_u_mm, NCH * h + c + 1)
                new = ps[:, c % 2, 0:VW]
                if c == 0:
                    dve.wait_ge(m_cout, 32 * h + 16)
                    V.tensor_copy(cst[:, 1, :], new).then_inc(m_c, 1)
                elif c < NCH - 1:
                    dve.wait_ge(m_c, NCH * h + c)
                    stt(cst[:, (c + 1) % 2, :], cst[:, c % 2, :], dec[:, c:c + 1], new, ALU.mult, ALU.add, m_c)
                else:
                    dve.wait_ge(m_c0, 16 * h + 16)
                    dve.wait_ge(m_cs, h + 1)
                    stt(cst[:, 1, :], csm[:], dec[:, c:c + 1], new, ALU.mult, ALU.add, m_c)
                if c + 1 < NCH:
                    t1, n1 = COL0[c + 1], CLEN[c + 1]
                    state = csm if c + 2 == NCH else cst[:, (c + 1) % 2, :]
                    dve.wait_ge(m_c, NCH * h + c + 1)
                    dve.wait_ge(m_cs, h + 1)
                    dve.wait_ge(m_qw, h + 1)
                    dve.wait_ge(m_sw, NCH * h + c + 2)
                    if c >= 1:
                        dve.wait_ge(m_o_mm, NCH * h + c)
                    stt(zw[:, (c + 1) % 2, 0:n1], bc[:, 1, t1:t1 + n1], state[:, DV:VW],
                        sw[:, (c + 1) % 2, 0:n1], ALU.mult, ALU.add, m_z)
                if c + 2 < NCH:
                    weigh(c + 2)
            o = nso[:, bass.ds(h, 1), :].rearrange("p a s -> p (a s)")
            dve.wait_ge(m_c, NCH * (h + 1))
            for s in range(2):
                V.tensor_copy(o[:, s:s + 1], cst[:, s, DV:DV + 1]).then_inc(m_no, 1)
            dve.wait_ge(m_oe, NCH * (h + 1))
            r = bc[:, 3, :]
            stt(r, kz, -1.0, r, ALU.mult, ALU.max, m_rec)
            dve.wait_ge(m_rec, 3 * h + 1)
            tt(r, kz, r, ALU.max, m_rec)
            dve.wait_ge(m_rec, 3 * h + 2)
            V.reciprocal(r, r).then_inc(m_rec, 1)
            dve.wait_ge(m_rec, 3 * h + 3)
            tt(bc[:, 0:2, :], bc[:, 0:2, :], bc[:, 3:4, :].broadcast_to([P, 2, COLS]), ALU.mult, m_hn)
            dve.wait_ge(m_hn, h + 1)
            dve.wait_ge(s_drA, a0 + 3)
            tt(bc[:, 0, :], bc[:, 0, :], kz, ALU.mult, m_y)
            dve.wait_ge(s_drB, b0 + 3)
            tt(bc[:, 1, :], bc[:, 1, :], preq[:, 0:COLS], ALU.mult, m_y)
            for cb in range(2):
                dve.wait_ge(m_y, 2 * h + cb + 1)
                dve.wait_ge(m_yhi, 2 * h + cb + 1)
                tt(yb_lo[:, cb, :], bc[:, cb, :], yb_hi[:, cb, :].bitcast(F32), ALU.subtract, m_ylo)
            cy = c0 + (6 if last else 10)

            def add(m):
                if m % 2 == 0:
                    dve.wait_ge(s_bb, 4 * h + m // 2 + 1)
                else:
                    dve.wait_ge(s_chunk, cy + m // 2 + 1)
                tt(as3(acc[:, m, :]), slots[m % 2], as3(acc[:, m, :]), ALU.add, s_dr[m % 2])
            done = 0
            if not last:
                done = 4
                xm(h + 1, add)
            for m in range(done, KB):
                add(m)
        loop(dve, HEADS - 1, lambda h: head(h, False))
        head(HEADS - 1, True)

        dve.wait_ge(s_drA, A_GB)
        dve.wait_ge(s_drB, B_GB)

        def gb(i):
            for half in range(2):
                n = 2 * i + half
                dve.wait_ge(s_dr[half], (A_GB, B_GB)[half] + i + 1)
                tt(tmp[:, half, :], tmp[:, half, :], blk(acc, n), ALU.mult, g_t)
                dve.wait_ge(g_t, n + 1)
                dve.wait_ge(g_in[half], 16 * i + 16)
                tt(tmp[:, half, :], tmp[:, half, :], tmp[:, 2 + half, :], ALU.add, g_mix)
                dve.wait_ge(g_mix, n + 1)
                dve.wait_ge(g_hi, n + 1)
                tt(blk(act_lo, n), tmp[:, half, :], blk(act_hi, n).bitcast(F32), ALU.subtract, g_lo)
        loop(dve, KB // 2, gb)

        V.memset(tmp[:, 3, :], 0.0).then_inc(s_zero, 1)
        dve.wait_ge(s_zero, 2)

        def wo(i):
            for half in range(2):
                n = 2 * i + half
                dve.wait_ge(s_chunk, W_OUT + 2 * n + 2)
                dve.wait_ge(o_in[half], 16 * i + 16)
                tt(as3(blk(acc, n)), slots[half], as3(tmp[:, half, :]), ALU.add, s_dr[half])
                dve.wait_ge(s_dr[half], (A_WO, B_WO)[half] + i + 1)
                dve.wait_ge(s_nhi, KB + n + 1)
                stt(blk(u_lo, n), blk(acc, n), gain2(n), blk(u_hi, n).bitcast(F32), ALU.mult, ALU.subtract, s_nlo)
                dve.wait_ge(o_sq, n + 1)
                tt(tmp[:, 3, :], tmp[:, 3, :], tmp[:, 2, :], ALU.add, o_ssum)
                dve.wait_ge(o_ssum, n + 1)
        loop(dve, KB // 2, wo)

        def up(g):
            def pair(i):
                dve.wait_ge(h_acc, KB * g + FREE)
                for half in range(2):
                    j = 8 * g + 2 * i + half
                    dve.wait_ge(s_dr[half], a_up(g, half) + i + 1)
                    dve.wait_ge(h_lo, j + FREE)
                    tt(tmp[:, 2, :], tmp[:, half, :], tmp[:, half, :], ALU.mult, h_s)
                    dve.wait_ge(h_s, j + 1 + 2 * FREE)
                    dve.wait_ge(h_hi, j + 1)
                    tt(blk(act_lo, 2 * i + half), tmp[:, 2, :],
                       blk(act_hi, 2 * i + half).bitcast(F32), ALU.subtract, h_lo)
            loop(dve, KB // 2, pair)

        def down(g, last=False):
            def pair(i):
                dve.wait_ge(h_lo, 8 * g + 8 + FREE)
                for half in range(2):
                    n = 2 * i + half
                    dve.wait_ge(s_chunk, W_MLP + 32 * g + 16 + 2 * n + 2)
                    dve.wait_ge(h_acc, KB * g + n + FREE)
                    tt(as3(tmp[:, 2, :]), slots[half], as3(tmp[:, 3, :]), ALU.mult, s_dr[half])
                    dve.wait_ge(s_dr[half], (A_ML + 1, B_ML)[half] + 8 * g + 4 + i + 1)
                    tt(blk(acc, n), blk(acc, n), tmp[:, 2, :], ALU.add, h_acc)
                    if last:
                        dve.wait_ge(f_sq, n + 1)
                        tt(tmp[:, 1, :], tmp[:, 1, :], tmp[:, 0, :], ALU.add, f_ssum)
                        dve.wait_ge(f_ssum, n + 1)
            loop(dve, KB // 2, pair)
        up(0)
        dve.wait_ge(s_drA, A_N2 + 1)
        V.reciprocal(tmp[:, 3, :], tmp[:, 3, :]).then_inc(s_rstd, 1)
        dve.wait_ge(s_rstd, 2)
        down(0)
        with dve.Fori(1, GROUPS - 1) as g:
            up(g)
            down(g)
        up(GROUPS - 1)
        V.memset(tmp[:, 1, :], 0.0).then_inc(s_zero, 1)
        dve.wait_ge(s_zero, 3)
        down(GROUPS - 1, True)
        dve.wait_ge(s_drA, A_N3 + 1)
        V.reciprocal(tmp[:, 3, :], tmp[:, 3, :]).then_inc(s_rstd, 1)
        dve.wait_ge(s_rstd, 3)
        for j in range(KB):
            g = S_GAIN + 2 * KB + j
            stt(acc[:, j, :], acc[:, j, :], small[:, g:g + 1], tmp[:, 3, :], ALU.mult, ALU.mult, f_y)

    outer.close()


def kernel(**inputs):
    import concourse.bacc as _bacc
    from concourse.bass_utils import run_bass_kernel_spmd as _run

    x = {k: np.asarray(v) for k, v in inputs.items()}
    f32 = np.float32

    cols = np.zeros((D_MODEL, COLS), f32)
    cols[:, :SEQ] = x["x_prompt"][0].T
    cols[:, SAMPLE0:] = x["x_sample"][0].T
    x_t = cols.reshape(KB, P, COLS)

    def tiles(w):
        k, m = w.shape
        t = w.reshape(k // (4 * P), 4, P, m // P, P).transpose(3, 0, 2, 1, 4)
        return t.reshape(m // P, k // (4 * P), P, CHUNK)

    w_in = x["w_in"][0]
    at = np.cumsum([0, D_RNN, D_RNN, D_ML, D_ML, HEADS, HEADS, D_MODEL, D_MODEL])
    xr, gr, xm, zm = (tiles(w_in[:, at[i]:at[i + 1]]) for i in range(4))
    ga, gb = (tiles(w_in[:, at[i]:at[i + 1]]) for i in (6, 7))
    gates = np.zeros((D_MODEL, P), f32)
    gates[:, 0:HEADS] = w_in[:, at[4]:at[5]]
    gates[:, 32:32 + HEADS] = w_in[:, at[5]:at[6]]
    wa, wx = x["rglru_wa"][0], x["rglru_wx"][0]
    wpa, wout = tiles(x["w_branch_a"][0]), tiles(x["w_out"][0])
    wpb, wup = x["w_branch_b"][0], tiles(x["w_mlp_up"][0])
    wdn = tiles(x["w_mlp_down"][0])
    wq, wk, wv = x["mlstm_wq"][0], x["mlstm_wk"][0], x["mlstm_wv"][0]
    ch = []
    for n in range(KB):
        pair = np.zeros((1, P, CHUNK), f32)
        pair[0, :, 0:P], pair[0, :, P:2 * P] = wa[n], wx[n]
        ch += [xr[n], gr[n], pair]
    ch += [tiles(gates)[0]]
    for n in range(KB):
        ch += [ga[n], wpa[n]]
    ch += [xm[0], xm[1]]
    for h in range(HEADS):
        v = wv[h].reshape(2, P, DV).transpose(1, 0, 2).reshape(1, P, CHUNK)
        kq = np.stack([wk[h].reshape(2, P, DK), wq[h].reshape(2, P, DK)])
        ch += [kq.transpose(2, 0, 1, 3).reshape(1, P, CHUNK), v, zm[2 * h], zm[2 * h + 1]]
        if h + 1 < HEADS:
            ch += [xm[2 * h + 2], xm[2 * h + 3]]
        b = wpb[h * DV:(h + 1) * DV].reshape(2, P, 4, 2, P).transpose(2, 1, 3, 0, 4)
        ch += [b.reshape(4, P, CHUNK)]
    ch += [gb[n] for n in range(KB)] + [wout[n] for n in range(KB)]
    for g in range(GROUPS):
        ch += [wup[KB * g + j] for j in range(KB)]
        ch += [wdn[n, 2 * g:2 * g + 2] for n in range(KB)]
    w = np.concatenate(ch)
    assert w.shape == (W_END, P, CHUNK)

    small = np.zeros((P, S_COLS), f32)
    small[:, S_ID:S_ID + P] = np.eye(P, dtype=f32)
    key, query = np.arange(P)[:, None], np.arange(P)[None, :]
    small[:, S_MASK:S_MASK + P] = np.where(key <= query, 0.0, -1e30)
    shift = key - (P - DEC_SEQ)
    small[:, S_MASK8:S_MASK8 + DEC_SEQ] = np.where((shift >= 0) & (shift <= query[:, :DEC_SEQ]), 0.0, -1e30)
    rg = np.zeros((KB, P, 13), f32)
    rg[:, :, 0:4] = x["conv_rglru_w"][0].reshape(CONV_W, KB, P).transpose(1, 2, 0)
    for i, k in ((4, "conv_rglru_b"), (5, "rglru_ba"), (6, "rglru_bx"), (7, "rglru_lambda")):
        rg[:, :, i] = x[k][0].reshape(KB, P)
    rg[:, :, 8:11] = x["state_rglru_conv"][0, 0].reshape(TAIL, KB, P).transpose(1, 2, 0)
    rg[:, :, 11] = x["state_rglru_h"][0, 0].reshape(KB, P)
    small[:, S_RG:S_ML] = rg.transpose(1, 0, 2).reshape(P, -1)
    ml = np.zeros((2 * HEADS, P, 8), f32)
    ml[:, :, 0:4] = x["conv_mlstm_w"][0].reshape(CONV_W, 2 * HEADS, P).transpose(1, 2, 0)
    ml[:, :, 4] = x["conv_mlstm_b"][0].reshape(2 * HEADS, P)
    ml[:, :, 5:8] = x["state_mlstm_conv"][0, 0].reshape(TAIL, 2 * HEADS, P).transpose(1, 2, 0)
    small[:, S_ML:S_GAIN] = ml.transpose(1, 0, 2).reshape(P, -1)
    gains = np.stack([x["norm_mix"][0], x["norm_mlp"][0], x["norm_final"]])
    small[:, S_GAIN:S_N0] = gains.reshape(3, KB, P).transpose(2, 0, 1).reshape(P, -1)
    small[:, S_N0:S_BIF] = x["state_mlstm_n"][0, 0].T
    small[0:HEADS, S_BIF] = x["b_if"][0, :HEADS]
    small[32:32 + HEADS, S_BIF] = x["b_if"][0, HEADS:]
    small[0:HEADS, S_M0] = x["state_mlstm_m"][0, 0]
    rowmask = np.ones((HEADS, COLS), f32)
    rowmask[:, COL0 + [SEQ]] = 0.0

    nc = _bacc.Bacc("TRN2", target_bir_lowering=False, num_devices=1)
    arrays = {
        "x_t": x_t, "small": small, "rowmask": rowmask, "w": w,
        "c0": np.ascontiguousarray(x["state_mlstm_C"][0, 0].transpose(0, 2, 1)),
    }
    given = {k: nc.dram_tensor("in_" + k, v.shape, F32, kind="ExternalInput").ap() for k, v in arrays.items()}
    made = {k: nc.dram_tensor("out_" + k, s, F32, kind=kind).ap() for k, s, kind in (
        ("rows", (HEADS, 3, COLS), "Internal"), ("mixa", (KB, P, COLS), "Internal"),
        ("y", (KB, P, COLS), "ExternalOutput"), ("conv", (P, 24, 6), "ExternalOutput"),
        ("hlast", (P, KB, 2), "ExternalOutput"), ("c", (2 * HEADS, P, DV), "ExternalOutput"),
        ("n", (P, HEADS, 2), "ExternalOutput"), ("m", (HEADS, 2), "ExternalOutput"))}
    build(nc, given["x_t"], given["small"], given["rowmask"], given["w"], given["c0"], made["rows"],
          made["mixa"], made["y"], made["conv"], made["hlast"], made["c"], made["n"], made["m"])
    r = _run(nc, [{"in_" + k: np.ascontiguousarray(v) for k, v in arrays.items()}], core_ids=[0]).results[0]

    y = r["out_y"].reshape(D_MODEL, COLS).T
    c = r["out_c"].reshape(2, HEADS, P, DV).transpose(0, 1, 3, 2)
    out = [np.ascontiguousarray(y[None, :SEQ]), np.ascontiguousarray(y[None, SAMPLE0:])]
    for s in range(2):
        conv = r["out_conv"][:, :, TAIL * s:TAIL * s + TAIL].transpose(2, 1, 0)
        out += [
            conv[:, :KB].reshape(1, 1, TAIL, D_RNN),
            r["out_hlast"][:, :, s].T.reshape(1, 1, D_RNN),
            conv[:, KB:].reshape(1, 1, TAIL, D_ML),
            c[s].reshape(1, 1, HEADS, DV, DK),
            r["out_n"][:, :, s].T.reshape(1, 1, HEADS, DK),
            r["out_m"][:, s].reshape(1, 1, HEADS),
        ]
    return tuple(np.ascontiguousarray(o) for o in out)
```

```python
from contextlib import ExitStack

import numpy as np

import concourse.bass as bass
from concourse import mybir

F32 = mybir.dt.float32
F32R = mybir.dt.float32r
ACT = mybir.ActivationFunctionType
ALU = mybir.AluOpType

P = 128
D_MODEL = 1024
SEQ = 1024
DEC_SEQ = 64
CONV_W = 4
TAIL = CONV_W - 1
HEADS = 8
DK = 128
DV = 256
D_RNN = 1024
D_ML = HEADS * DV
D_FF = 4 * D_MODEL
EPS = 1e-6
RG_C = 8.0

KB = D_MODEL // P
GAP = 4
SAMPLE0 = SEQ + GAP
CARRY = SAMPLE0 - 1
COLS = SAMPLE0 + DEC_SEQ
TILES = 3
TW = COLS // TILES
BANK = 512
CH = 128
NCH = SEQ // CH + 1
KEY0 = [CH * c for c in range(NCH - 1)] + [COLS - CH]
COL0 = [CH * c for c in range(NCH - 1)] + [SAMPLE0]
VW = DV + 1
CLEN = [CH] * (NCH - 1) + [DEC_SEQ]

CHUNK = 512
W_RG = 0
W_GATES = W_RG + 5 * KB
W_AO = W_GATES + 2
W_X0 = W_AO + 4 * KB
W_HEAD = W_X0 + 4
PER_HEAD = 14
W_GB = W_HEAD + PER_HEAD * HEADS - 4
W_OUT = W_GB + 2 * KB
W_MLP = W_OUT + 2 * KB
GROUPS = D_FF // D_MODEL
W_END = W_MLP + 32 * GROUPS

A_RG, B_RG = 1, 1
A_G = A_RG + 2 * KB
B_G = B_RG + 2 * KB
A_AO, B_AO = A_G + 1, B_G
A_X0, B_X0 = A_AO + KB, B_AO + KB
A_HD, B_HD = A_X0 + 1, B_X0 + 1
A_GB, B_GB = A_HD + 8 * HEADS - 1, B_HD + 8 * HEADS - 1
A_WO, B_WO = A_GB + 4, B_GB + 4
A_ML, B_ML = A_WO + 4, B_WO + 4
A_N2 = A_ML + 4
A_N3 = A_ML + 8 * GROUPS + 1

LAST_TILES = [(0, 452), (452, 832), (832, COLS)]
POOL_BLOCKS = KB // 2

S_ID = 0
S_MASK = 128
S_MASK8 = 256
S_RG = 320
S_ML = S_RG + 8 * 13
S_GAIN = S_ML + 16 * 8
S_N0 = S_GAIN + 24
S_BIF = S_N0 + 8
S_M0 = S_BIF + 1
S_COLS = S_M0 + 1

XC, R, I, TH, G, SQ, H, GG = range(8)
IG, LF, EM, FF, MASK, MM, AR, EE = range(8)
ROWS_DVE, ROWS_ACT = 18, 7

FREE = 1

GELU_C = 0.044715
GELU_K = 0.7978845608028654


def build(nc, x_t, small_d, rowmask_d, w_d, c0_d, rows_d, mixa_d, y_d, conv_d, hlast_d, c_d, n_d, m_d):
    outer = ExitStack()
    sb_in = lambda st, name, shape, dt=F32: st.enter_context(nc.sbuf_tensor(name, shape, dt))
    sb = lambda name, shape, dt=F32: sb_in(outer, name, shape, dt)
    sem = lambda name: outer.enter_context(nc.semaphore(name))

    ps = outer.enter_context(nc.psum_tensor("ps", [P, 8, BANK], F32))
    slot_a, slot_b = ps[:, 0:3, 0:TW], ps[:, 3:6, 0:TW]
    slots = [slot_a, slot_b]

    u_hi = sb("u_hi", [P, KB, COLS], F32R)
    u_lo = sb("u_lo", [P, KB, COLS], F32R)
    acc = sb("acc", [P, KB, COLS])
    w_raw = sb("w_raw", [P, 2, CHUNK])
    w_hi = sb("w_hi", [P, 2, CHUNK], F32R)
    w_lo = sb("w_lo", [P, 2, CHUNK], F32R)
    small = sb("small", [P, S_COLS])
    ones = sb("ones", [P, P])
    eps_c = sb("eps_c", [P, 1])
    warm = sb("warm", [P, 1])
    rstd = sb("rstd", [P, COLS])
    cso = sb("cso", [P, 24, 6])
    hso = sb("hso", [P, KB, 2])
    nso = sb("nso", [P, HEADS, 2])
    mso = sb("mso", [HEADS, 2])

    with ExitStack() as st:
        p0 = sb_in(st, "p0", [P, 4, COLS])
    with ExitStack() as st:
        ya_hi = sb_in(st, "ya_hi", [P, KB, COLS], F32R)
        ya_lo = sb_in(st, "ya_lo", [P, KB, COLS], F32R)
        rpre = sb_in(st, "rpre", [P, COLS + TAIL])
        rx_hi = sb_in(st, "rx_hi", [P, COLS], F32R)
        rx_lo = sb_in(st, "rx_lo", [P, COLS], F32R)
        c8 = sb_in(st, "c8", [P, 8, KB])
        rp = sb_in(st, "rp", [P, 13])
        rc8 = sb_in(st, "rc8", [P, 1])
        rcol = sb_in(st, "rcol", [P, NCH])
    with ExitStack() as st:
        yb_hi = sb_in(st, "yb_hi", [P, 2, COLS], F32R)
        yb_lo = sb_in(st, "yb_lo", [P, 2, COLS], F32R)
        xm_hi = sb_in(st, "xm_hi", [P, 2, COLS], F32R)
        xm_lo = sb_in(st, "xm_lo", [P, 2, COLS], F32R)
        preq = sb_in(st, "preq", [P, COLS + TAIL])
        vt = sb_in(st, "vt", [P, NCH * VW])
        bc = sb_in(st, "bc", [P, 3, COLS])
        cst = sb_in(st, "cst", [P, 2, VW])
        csm = sb_in(st, "csm", [P, VW])
        kt = sb_in(st, "kt", [P, 2, P])
        sw = sb_in(st, "sw", [P, 2, P])
        zw = sb_in(st, "zw", [P, 2, P])
        bp = sb_in(st, "bp", [P, 2, 8])
        ecol = sb_in(st, "ecol", [P, 2, NCH, HEADS])
        hcol = sb_in(st, "hcol", [P, 2, NCH])
        dec = sb_in(st, "dec", [P, NCH])
        with ExitStack() as st2:
            xc_hi = sb_in(st2, "xc_hi", [P, 2, COLS], F32R)
            xc_lo = sb_in(st2, "xc_lo", [P, 2, COLS], F32R)
        em = sb_in(st, "em", [P, 1, COLS])
    with ExitStack() as st:
        act_hi = sb_in(st, "act_hi", [P, KB, COLS], F32R)
        act_lo = sb_in(st, "act_lo", [P, KB, COLS], F32R)
        tmp = sb_in(st, "tmp", [P, 4, COLS])
    kz = bc[:, 2, :]
    vt3 = vt[:].rearrange("p (c v) -> p c v", v=VW)
    conv1, conv2 = vt[:, 0:COLS], vt[:, COLS:2 * COLS]

    s_small, s_rowmask, s_raw0, s_raw1 = sem("small_in"), sem("rowmask_in"), sem("raw0_in"), sem("raw1_in")
    s_raw = [s_raw0, s_raw1]
    s_x = [sem(f"x_in{j}") for j in range(KB)]
    s_whi, s_wlo = sem("chunk_hi"), sem("chunk_split")
    s_chunk = sem("chunk_multiplied")
    s_drA, s_drB = sem("slot_a_drained"), sem("slot_b_drained")
    s_dr = [s_drA, s_drB]
    s_va, s_k_mm, s_r_mm, s_bb = sem("v_first_mm"), sem("k_mm"), sem("r_mm"), sem("branch_b_even_mm")
    s_out = sem("stored")
    s_const, s_const_dve = sem("constants_set"), sem("pads_zeroed")
    r_cs, r_hs, m_cs2, m_dec = sem("rg_tails"), sem("rg_h_out"), sem("ml_tails"), sem("ml_decays")
    s_sq, s_ssum, s_norm, s_std, s_rstd, s_nhi, s_nlo = [sem(n) for n in (
        "squared", "squares_summed", "norm_mm", "std", "rstd", "input_hi", "input_lo")]
    n_diag, n_bc, n_out = sem("rstd_diagonals"), sem("rstd_broadcast_mm"), sem("rstd_out")
    s_sp, s_spv = sem("softplus_act"), sem("softplus_dve")
    (r_pre, r_tap0, r_g, r_xhi, r_sq, r_th, r_tg, r_a, r_gain, r_yhi) = [sem("rg_" + n) for n in (
        "pre", "tap0", "g", "x_hi", "sq", "th", "tg", "a", "gain", "y_hi")]
    (r_rp, r_pad, r_conv, r_xlo, r_inner, r_ix, r_a2, r_p, r_b, r_fix, r_scan, r_gg, r_y, r_ylo) = [
        sem("rg_" + n) for n in ("params", "pads", "conv", "x_lo", "inner", "ix", "a2", "p", "b", "carry",
                                 "scan", "gg", "y", "y_lo")]
    w_pre, w_act, w_dve, w_tr, w_col, w_colz, w_st = [sem("rows_" + n) for n in (
        "pre", "act", "dve", "transposed", "cols", "cols_zeroed", "stored")]
    ao_sig, ao_st = sem("ga_sigmoid"), sem("mix_a_stored")
    (m_xhi, m_tap0, m_sig, m_chi, m_v, m_e, m_kt, m_zs, m_yhi) = [sem("ml_" + n) for n in (
        "x_hi", "tap0", "sig", "c_hi", "v", "e", "kt", "zs", "y_hi")]
    (m_bp, m_pad, m_xlo, m_conv, m_silu, m_clo, m_hcol, m_mask, m_qw, m_sw, m_c, m_rec, m_hn, m_y, m_ylo,
     m_cs, m_no) = [sem("ml_" + n) for n in (
         "params", "pads", "x_lo", "conv", "silu", "c_lo", "head_cols", "masked", "qw", "scores_w", "state", "rec",
         "h", "y", "y_lo", "sample_n", "n_out")]
    m_s_mm, m_u_mm, m_o_mm = sem("scores_mm"), sem("state_mm"), sem("h_mm")
    m_one, m_z, m_oe = sem("ml_v_ones"), sem("ml_z"), sem("ml_o_out")
    m_em = sem("ml_exp_m_in")
    m_bc, m_c0, m_cout = sem("rows_in"), sem("sample_state_in"), sem("states_stored")
    s_zero = sem("branch_b_zeroed")
    s_warm = sem("table_loaded")
    g_sig, g_t, g_mix, g_hi, g_lo = [sem("merge_" + n) for n in ("sig", "t", "mix", "hi", "lo")]
    g_in = [sem(f"mix_a_in{j}") for j in range(2)]
    o_in = [sem(f"x_again_in{j}") for j in range(2)]
    o_sq, o_ssum = sem("res_squared"), sem("res_ssum")
    h_acc = sem("mixer_added")
    h_hi, h_s, h_lo = sem("hid_hi"), sem("hid_sq"), sem("hid_lo")
    f_mm, f_prod, f_sq, f_gain, f_ssum = [sem("final_" + n) for n in (
        "tile_mm", "product", "squared", "gain", "ssum")]
    f_norm, f_std, f_rstd, f_yv, f_yp = [sem("final_" + n) for n in ("norm_mm", "std", "rstd", "y_dve", "y_pool")]

    block = outer.enter_context(nc.Block())

    def as3(ap):
        return ap.rearrange("p (a b) -> p a b", a=TILES)

    def blk(t, n):
        if isinstance(n, int):
            return t[:, n, :]
        return t[:, bass.ds(n, 1), :].rearrange("p a c -> p (a c)")

    def gain(n):
        return small[:, S_GAIN + n:S_GAIN + n + 1]

    def gain3(n):
        if isinstance(n, int):
            return small[:, S_GAIN + 2 * KB + n:S_GAIN + 2 * KB + n + 1]
        return small[:, bass.ds(n + S_GAIN + 2 * KB, 1)]

    def gain2(n):
        if isinstance(n, int):
            return small[:, S_GAIN + KB + n:S_GAIN + KB + n + 1]
        return small[:, bass.ds(n + S_GAIN + KB, 1)]

    def a_up(g, half):
        return (A_ML if isinstance(g, int) and g == 0 else A_ML + 1, B_ML)[half] + 8 * g

    def last_rstd(lo, hi, blocks):
        return rstd[:, lo:hi].rearrange("p (a c) -> p a c", a=1).broadcast_to([P, blocks, hi - lo])

    def loop(eng, n, body):
        with eng.Fori(0, n) as i:
            body(i)

    @block.sync
    def _(sp):
        sp.dma_start(small[:], small_d).then_inc(s_small, 16)
        for j in range(KB):
            sp.dma_start(acc[:, j, :], x_t[j]).then_inc(s_x[j], 16)
            if j < 2:
                sp.dma_start(w_raw[:, j, :], w_d[j]).then_inc(s_raw[j], 16)

        def more(i):
            for c in range(2):
                src = w_d[bass.ds(sp.snap(2 * i + 2 + c), 1)].rearrange("a p m -> p (a m)")
                sp.wait_ge(s_wlo, 2 * i + c + 1)
                sp.dma_start(w_raw[:, c, :], src).then_inc(s_raw[c], 16)
        loop(sp, W_END // 2 - 1, more)

        sp.wait_ge(r_cs, 2 * KB)
        sp.wait_ge(m_cs2, 4 * HEADS)
        sp.dma_start(conv_d, cso[:]).then_inc(s_out, 16)
        sp.wait_ge(r_hs, 2 * KB)
        sp.dma_start(hlast_d, hso[:]).then_inc(s_out, 16)
        sp.wait_ge(m_no, 2 * HEADS)
        sp.dma_start(n_d, nso[:]).then_inc(s_out, 16)
        sp.wait_ge(w_dve, ROWS_DVE)
        sp.dma_start(m_d, mso[:]).then_inc(s_out, 16)
        for t, (lo, hi) in enumerate(LAST_TILES):
            for done, js in ((f_yv, slice(POOL_BLOCKS, KB)), (f_yp, slice(0, POOL_BLOCKS))):
                sp.wait_ge(done, t + 1)
                sp.dma_start(y_d[js, :, lo:hi].rearrange("j p c -> p j c"), acc[:, js, lo:hi]).then_inc(s_out, 16)
        sp.wait_ge(s_out, 16 * (4 + 2 * TILES))
        sp.wait_ge(m_cout, 32 * HEADS + 16)

    @block.gpsimd
    def _(pool):
        nc.gpsimd.memset(ones[:], 1.0).then_inc(s_const, 1)
        nc.gpsimd.memset(eps_c[:], EPS).then_inc(s_const, 1)
        one = ones[:, 0:1].broadcast_to([P, CHUNK])
        pool.wait_ge(s_const, 1)

        def split(c, j, first):
            pool.wait_ge(s_raw[c], 16 * j + 16)
            if not first:
                pool.wait_ge(s_chunk, 2 * j + c - 1)
            nc.gpsimd.tensor_tensor(w_hi[:, c, :], w_raw[:, c, :], one, ALU.mult).then_inc(s_whi, 1)
            pool.wait_ge(s_whi, 2 * j + c + 1)
            nc.gpsimd.tensor_tensor(w_lo[:, c, :], w_raw[:, c, :], w_hi[:, c, :].bitcast(F32),
                                    ALU.subtract).then_inc(s_wlo, 1)
        split(0, 0, True)
        split(1, 0, True)

        def both(i):
            split(0, i + 1, False)
            split(1, i + 1, False)
        loop(pool, W_END // 2 - 1, both)

        for t, (lo, hi) in enumerate(LAST_TILES):
            pool.wait_ge(f_gain, KB - 1 + t + 1)
            pool.wait_ge(f_rstd, t + 1)
            y = acc[:, 0:POOL_BLOCKS, lo:hi]
            nc.gpsimd.tensor_tensor(y, y, last_rstd(lo, hi, POOL_BLOCKS), ALU.mult).then_inc(f_yp, 1)

    @block.tensor
    def _(pe):
        def product(slot, blocks, rhs_hi, rhs_lo, before=None, done=None):
            last_k = len(blocks) - 1
            for k, (chunk, ws, off, last) in enumerate(blocks):
                if chunk is not None:
                    pe.wait_ge(s_wlo, chunk + 1)
                if before is not None:
                    before(k)
                hi, lo = w_hi[:, ws, off:off + P], w_lo[:, ws, off:off + P]
                for n, (w, r) in enumerate(((hi, rhs_hi), (hi, rhs_lo), (lo, rhs_hi))):
                    for t in range(TILES):
                        mm = nc.tensor.matmul(slots[slot][:, t, :], w, r(k)[:, t * TW:(t + 1) * TW],
                                              start=(k == 0 and n == 0), stop=(k == last_k and n == 2))
                if last:
                    mm.then_inc(s_chunk, 1)
                elif k == last_k and done is not None:
                    mm.then_inc(done, 1)

        def full(chunk):
            return [(chunk + k // 4 if k % 4 == 0 else None, k // 4, (k % 4) * P, k % 4 == 3) for k in range(KB)]

        def full_odd(chunk):
            return [(c, 1 - ws, off, last) for c, ws, off, last in full(chunk)]

        U = (lambda k: u_hi[:, k, :], lambda k: u_lo[:, k, :])

        def norm_sum(src, wait):
            wait()
            for t in range(TILES):
                mm = nc.tensor.matmul(slot_a[:, t, :], ones[:], src[:, t * TW:(t + 1) * TW], start=True, stop=True)
            mm.then_inc(s_norm, 1)

        def first_norm():
            pe.wait_ge(s_const, 2)
            pe.wait_ge(s_ssum, KB - 1)
            for c in range(NCH):
                mm = nc.tensor.matmul(ps[:, 6, c:c + 1], p0[:, 2, KEY0[c]:KEY0[c] + CH], ones[:, 0:1],
                                      start=True, stop=True)
            mm.then_inc(s_norm, 1)

        def broadcast(t):
            pe.wait_ge(n_diag, 2)
            if t == 2:
                pe.wait_ge(n_out, 1)
            nc.tensor.matmul(ps[:, 6 + t % 2, 0:TW], ones[:], p0[:, 3, t * TW:(t + 1) * TW],
                             start=True, stop=True).then_inc(n_bc, 1)

        def rg(i, first=False):
            for half in range(2):
                start = first and half == 0
                c = W_RG + 10 * i + 5 * half
                pick = full_odd if half else full
                a0, b0 = A_RG + 4 * i + 2 * half, B_RG + 4 * i + 2 * half
                pe.wait_ge(s_drA, a0)
                product(0, pick(c), *U, before=(lambda k: pe.wait_ge(s_nlo, k + 1)) if start else None)
                pe.wait_ge(s_drB, b0)
                if start:
                    first_norm()
                product(1, pick(c + 2), *U, before=(lambda k: [broadcast(t) for t in range(TILES)] if k == 1 else None)
                        if start else None)
                x = (lambda k: rx_hi[:], lambda k: rx_lo[:])
                pe.wait_ge(s_drA, a0 + 1)
                pe.wait_ge(r_xlo, 2 * i + half + 1)
                product(0, [(c + 4, half, 0, False)], *x, done=s_r_mm)
                pe.wait_ge(s_drB, b0 + 1)
                product(1, [(None, half, P, True)], *x)
        rg(0, True)
        with pe.Fori(1, KB // 2) as i:
            rg(i)

        pe.wait_ge(s_drA, A_G)
        product(0, full(W_GATES), *U)

        def ao(n):
            pe.wait_ge(s_drB, B_AO + n)
            product(1, full(W_AO + 4 * n), *U)
            pe.wait_ge(s_drA, A_AO + n)
            product(0, full(W_AO + 4 * n + 2), lambda k: ya_hi[:, k, :], lambda k: ya_lo[:, k, :],
                    before=lambda k: pe.wait_ge(r_ylo, k + 1 + FREE))
        loop(pe, KB, ao)

        def xm(chunk, a, b):
            pe.wait_ge(s_drA, a)
            product(0, full(chunk), *U)
            pe.wait_ge(s_drB, b)
            product(1, full(chunk + 2), *U)
        xm(W_X0, A_X0, B_X0)

        pe.wait_ge(w_dve, ROWS_DVE)
        pe.wait_ge(w_act, ROWS_ACT)
        for r, row in enumerate((EE, MASK)):
            for c in range(NCH):
                o = (r * NCH + c) * HEADS
                mm = nc.tensor.transpose(ps[:, 6, o:o + HEADS], acc[0:HEADS, row, KEY0[c]:KEY0[c] + CH],
                                         small[0:HEADS, S_ID:S_ID + HEADS])
        mm.then_inc(w_tr, 1)

        def head(h, last):
            c0, a0, b0 = W_HEAD + PER_HEAD * h, A_HD + 8 * h, B_HD + 8 * h
            C = (lambda k: xc_hi[:, k, :], lambda k: xc_lo[:, k, :])
            pe.wait_ge(s_drA, a0)
            product(0, [(c0, 0, 0, False), (None, 0, P, False)], *C,
                    before=lambda k: pe.wait_ge(m_clo, 2 * h + k + 1), done=s_k_mm)
            pe.wait_ge(s_drB, b0)
            product(1, [(None, 0, 2 * P, False), (None, 0, 3 * P, True)], *C)

            pe.wait_ge(s_wlo, c0 + 2)
            pe.wait_ge(s_drA, a0 + 1)
            for c in range(NCH):
                if c == 6:
                    pe.wait_ge(s_drB, b0 + 1)
                out = ps[:, c // 2, (c % 2) * DV:(c % 2 + 1) * DV]
                k0 = KEY0[c]
                for cb in range(2):
                    wv_hi, wv_lo = (w[:, 1, cb * DV:(cb + 1) * DV] for w in (w_hi, w_lo))
                    x_hi, x_lo = (x[:, cb, k0:k0 + CH] for x in (xm_hi, xm_lo))
                    for n, (l, r) in enumerate(((x_hi, wv_hi), (x_hi, wv_lo), (x_lo, wv_hi))):
                        mm = nc.tensor.matmul(out, l, r, start=(cb == 0 and n == 0), stop=(cb == 1 and n == 2))
                if c == 5:
                    mm.then_inc(s_va, 1)
            mm.then_inc(s_chunk, 1)

            def scores(c):
                if c == 0:
                    pe.wait_ge(w_colz, 1)
                    pe.wait_ge(s_drB, b0 + 1)
                    pe.wait_ge(s_drA, a0 + 2)
                k0, t0, n = KEY0[c], COL0[c], CLEN[c]
                nc.tensor.matmul(ps[:, 6 + c % 2, 0:n], kz[:, k0:k0 + CH], preq[:, t0:t0 + n], start=True, stop=True)
                nc.tensor.transpose(ps[:, 2 + 3 * (c % 2), 0:P], kz[:, k0:k0 + CH],
                                    small[:, S_ID:S_ID + P]).then_inc(m_s_mm, 1)

            scores(0)
            scores(1)
            pe.wait_ge(m_one, h + 1)
            pe.wait_ge(m_qw, h + 1)
            for c in range(NCH):
                t0, n = COL0[c], CLEN[c]
                pe.wait_ge(m_kt, NCH * h + c + 1)
                if c >= 2:
                    pe.wait_ge(m_c, NCH * h + c - 1)
                nc.tensor.matmul(ps[:, c % 2, 0:VW], kt[:, c % 2, :], vt3[:, c, :],
                                 start=True, stop=True).then_inc(m_u_mm, 1)
                pe.wait_ge(m_sw, NCH * h + c + 1)
                if c == 0:
                    pe.wait_ge(s_drB, b0 + 2)
                else:
                    if c < NCH - 1:
                        pe.wait_ge(m_c, NCH * h + c)
                    else:
                        pe.wait_ge(m_c0, 16 * h + 16)
                if c >= 2:
                    pe.wait_ge(m_oe, NCH * h + c - 1)
                state = None if c == 0 else csm if c == NCH - 1 else cst[:, c % 2, :]
                for j in range(2):
                    out = ps[:, 3 + c % 2, j * P:j * P + n]
                    nc.tensor.matmul(out, vt3[:, c, j * P:(j + 1) * P], sw[:, c % 2, 0:n],
                                     start=True, stop=state is None)
                    if state is not None:
                        nc.tensor.matmul(out, state[:, j * P:(j + 1) * P], bc[:, 1, t0:t0 + n],
                                         start=False, stop=True)
                if c:
                    pe.wait_ge(m_z, (NCH - 1) * h + c)
                nc.tensor.matmul(ps[:, 3 + c % 2, 2 * P:2 * P + n], ones[:], (zw if c else sw)[:, c % 2, 0:n],
                                 start=True, stop=True).then_inc(m_o_mm, 1)
                if c + 2 < NCH:
                    scores(c + 2)
            pe.wait_ge(m_c, NCH * h + NCH)
            c1 = c0 + 2
            product(0, full(c1), *U)
            pe.wait_ge(m_oe, NCH * h + NCH)
            product(1, full(c1 + 2), *U)
            c1, a1, b1 = c1 + 4, a0 + 3, b0 + 3
            if not last:
                xm(c1, a1, b1)
                c1, a1, b1 = c1 + 4, a1 + 1, b1 + 1
            Y = (lambda k: yb_hi[:, k, :], lambda k: yb_lo[:, k, :])
            for m in range(KB):
                ws, off = (m // 2) % 2, (m % 2) * 2 * P
                first = c1 + m // 2 if m % 2 == 0 else None
                pe.wait_ge(s_dr[m % 2], (b1 if m % 2 else a1) + m // 2)
                product(m % 2, [(first, ws, off, False), (None, ws, off + P, m % 2 == 1)], *Y,
                        before=lambda k: pe.wait_ge(m_ylo, 2 * h + k + 1), done=s_bb)
        loop(pe, HEADS - 1, lambda h: head(h, False))
        head(HEADS - 1, True)

        def gb(i):
            for half in range(2):
                pe.wait_ge(s_dr[half], (A_GB, B_GB)[half] + i)
                product(half, full(W_GB + 4 * i + 2 * half), *U)
        loop(pe, KB // 2, gb)
        A = (lambda k: act_hi[:, k, :], lambda k: act_lo[:, k, :])

        def wo(i):
            for half in range(2):
                pe.wait_ge(s_dr[half], (A_WO, B_WO)[half] + i)
                product(half, full(W_OUT + 4 * i + 2 * half), *A, before=lambda k: pe.wait_ge(g_lo, k + 1))
        loop(pe, KB // 2, wo)

        def up(g, a):
            def pair(i):
                for half in range(2):
                    pe.wait_ge(s_dr[half], (a, B_ML)[half] + 8 * g + i)
                    product(half, full(W_MLP + 32 * g + 4 * i + 2 * half), *U,
                            before=lambda k: pe.wait_ge(s_nlo, KB + k + 1))
            loop(pe, KB // 2, pair)

        def down(g, last=False):
            def pair(i, halves=2):
                for half in range(halves):
                    pe.wait_ge(s_dr[half], (A_ML + 1, B_ML)[half] + 8 * g + 4 + i)
                    product(half, full(W_MLP + 32 * g + 16 + 4 * i + 2 * half), *A,
                            before=lambda k: pe.wait_ge(h_lo, 8 * g + k + 1 + FREE))
            loop(pe, KB // 2 - last, pair)
            if last:
                pair(KB // 2 - 1, 1)

        def n2():
            pe.wait_ge(s_drA, A_N2)
            pe.wait_ge(o_ssum, KB)

        def group(g):
            up(g, A_ML + 1)
            down(g)
        up(0, A_ML)
        norm_sum(tmp[:, 3, :], n2)
        down(0)
        with pe.Fori(1, GROUPS - 1) as g:
            group(g)
        up(GROUPS - 1, A_ML + 1)
        down(GROUPS - 1, True)

        def norm_tile(t):
            lo, hi = LAST_TILES[t]
            pe.wait_ge(s_drA, A_N3)
            pe.wait_ge(f_ssum, KB - 1 + t + 1)
            nc.tensor.matmul(ps[:, t, 0:hi - lo], ones[:], tmp[:, 1, lo:hi], start=True, stop=True)\
                .then_inc(f_norm, 1)
        pe.wait_ge(s_drB, B_ML + 8 * GROUPS - 1)
        for t, (lo, hi) in enumerate(LAST_TILES):
            for k in range(KB):
                if t == 0 and k % 4 == 0:
                    pe.wait_ge(s_wlo, W_END - 1 + k // 4)
                if t == 1 and k == 5:
                    norm_tile(0)
                w = [x[:, k // 4, (k % 4) * P:(k % 4 + 1) * P] for x in (w_hi, w_lo)]
                x_hi, x_lo = (x[:, k, lo:hi] for x in (act_hi, act_lo))
                for n, (l, r) in enumerate(((w[0], x_hi), (w[0], x_lo), (w[1], x_hi))):
                    mm = nc.tensor.matmul(ps[:, 3 + t, 0:hi - lo], l, r,
                                          start=(k == 0 and n == 0), stop=(k == KB - 1 and n == 2))
            mm.then_inc(f_mm, 1)
        norm_tile(1)
        norm_tile(2)

    @block.scalar
    def _(act):
        def a(out, in_, f, inc, **kw):
            nc.scalar.activation(out, in_, f, **kw).then_inc(inc, 1)

        act.sem_inc(s_drA, 1)
        act.sem_inc(s_drB, 1)
        act.sem_inc(ao_st, 16)
        act.sem_inc(m_cout, 16)
        act.wait_ge(s_const, 2)
        act.wait_ge(s_small, 16)

        act.wait_ge(s_spv, 1)
        a(c8[:, 2, :], c8[:, 1, :], ACT.Exp, s_sp, scale=-1.0)
        for j in range(KB):
            act.wait_ge(s_x[j], 16)
            a(u_hi[:, j, :], acc[:, j, :], ACT.Copy, s_nhi, scale=gain(j))
            if j >= 3:
                act.wait_ge(s_ssum, j - 2)
            a(p0[:, j % 2 if j else 2, :], acc[:, j, :], ACT.Square, s_sq)

        act.wait_ge(s_norm, 1)
        a(rcol[:], ps[:, 6, 0:NCH], ACT.Sqrt, s_std, scale=1.0 / D_MODEL, bias=eps_c[:, 0:1])
        for t in range(TILES):
            act.wait_ge(n_bc, t + 1)
            a(rstd[:, t * TW:(t + 1) * TW], ps[:, 6 + t % 2, 0:TW], ACT.Copy, n_out)

        def convolve(n):
            act.wait_ge(r_pad, n + 1)
            a(acc[:, XC, :], rpre[:, 0:COLS], ACT.Identity, r_tap0, scale=rp[:, 0:1], bias=rp[:, 4:5])

        def x_hi(n):
            act.wait_ge(r_conv, TAIL * n + TAIL)
            a(rx_hi[:], acc[:, XC, :], ACT.Copy, r_xhi)

        def gates_out(n):
            act.wait_ge(s_r_mm, n + 1)
            nc.scalar.activation(as3(acc[:, R, :]), slot_a, ACT.Sigmoid, bias=rp[:, 5:6]).then_inc(s_drA, 1)
            act.wait_ge(s_chunk, W_RG + 5 * n + 5)
            nc.scalar.activation(as3(acc[:, I, :]), slot_b, ACT.Sigmoid, bias=rp[:, 6:7]).then_inc(s_drB, 1)

        def y_hi(n):
            act.wait_ge(r_y, n + 1)
            a(blk(ya_hi, n), acc[:, GG, :], ACT.Copy, r_yhi)

        def rg(n, last):
            act.wait_ge(s_drB, B_RG + 2 * n + 1)
            a(acc[:, SQ, :], acc[:, G, :], ACT.Square, r_sq)
            act.wait_ge(s_drA, A_RG + 2 * n + 2)
            a(acc[:, TH, :], acc[:, R, :], ACT.Tanh, r_th, scale=rc8[:, 0:1])
            act.wait_ge(r_inner, n + 1)
            a(acc[:, SQ, :], acc[:, SQ, :], ACT.Tanh, r_tg, scale=GELU_C * GELU_K)
            act.wait_ge(r_th, n + 1)
            a(acc[:, R, :], acc[:, R, :], ACT.Exp, r_a, scale=rc8[:, 0:1])
            if not last:
                act.wait_ge(r_ix, n + 1)
                convolve(n + 1)
            act.wait_ge(r_p, n + 1)
            a(acc[:, TH, :], acc[:, TH, :], ACT.Sqrt, r_gain, scale=-1.0)
            if not last:
                x_hi(n + 1)
                nc.scalar.activation(warm[:], eps_c[:], ACT.Sigmoid).then_inc(s_warm, 1)
                act.wait_ge(r_scan, n + 1)
                gates_out(n + 1)
            y_hi(n)
        convolve(0)
        x_hi(0)
        gates_out(0)
        loop(act, KB - 1, lambda n: rg(n, False))
        rg(KB - 1, True)

        act.wait_ge(r_ylo, KB + FREE)
        act.dma_start(acc[0:HEADS, MASK, :], rowmask_d).then_inc(s_rowmask, 16)
        row = lambda j: acc[0:HEADS, j, :]
        act.wait_ge(w_pre, 1)
        a(row(IG), row(IG), ACT.Identity, w_act, bias=small[0:HEADS, S_BIF:S_BIF + 1])
        act.wait_ge(s_drA, A_AO)
        a(row(LF), acc[32:32 + HEADS, LF, :], ACT.Identity, w_act, bias=small[32:32 + HEADS, S_BIF:S_BIF + 1])

        def ao(n):
            act.wait_ge(s_drB, B_AO + n + 1)
            a(rpre[:, 0:COLS], rpre[:, 0:COLS], ACT.Sigmoid, ao_sig)
            dst = mixa_d[bass.ds(n, 1)].rearrange("a p c -> p (a c)")
            act.wait_ge(s_drA, A_AO + n + 1)
            act.dma_start(dst, rpre[:, 0:COLS]).then_inc(ao_st, 16)

        act.wait_ge(w_dve, 1)
        a(row(EM), row(EM), ACT.Exp, w_act, scale=-1.0)
        act.wait_ge(w_act, 3)
        a(row(EM), row(EM), ACT.Ln, w_act, bias=ones[0:HEADS, 0:1])
        ao(0)
        act.wait_ge(w_dve, 7)
        a(row(EM), row(MM), ACT.Exp, w_act, scale=-1.0)
        act.wait_ge(w_dve, 14)
        a(row(LF), row(LF), ACT.Exp, w_act)
        act.wait_ge(w_dve, ROWS_DVE)
        a(row(MASK), row(MASK), ACT.Exp, w_act)
        act.wait_ge(w_act, ROWS_ACT)
        for n, r in enumerate((AR, LF, EM)):
            act.dma_start(rows_d[:, n, :], row(r)).then_inc(w_st, 16)
        with act.Fori(1, KB) as n:
            ao(n)

        def xm(h):
            for cb in range(2):
                act.wait_ge(m_pad, 4 * h + 2 * cb + 2)
                if cb:
                    act.wait_ge(m_clo, 2 * h + 1)
                a(conv1, preq[:, 0:COLS], ACT.Identity, m_tap0, scale=bp[:, cb, 0:1], bias=bp[:, cb, 4:5])
                a(xm_hi[:, cb, :], preq[:, TAIL:], ACT.Copy, m_xhi)
                act.wait_ge(m_conv, TAIL * (2 * h + cb) + TAIL)
                a(conv2, conv1, ACT.Sigmoid, m_sig)
                act.wait_ge(m_silu, 2 * h + cb + 1)
                a(xc_hi[:, cb, :], conv1, ACT.Copy, m_chi)

        def load_head(h):
            one = bass.ds(h, 1)
            src = rows_d[one].rearrange("a r c -> a (r c)")
            act.dma_start(bc[:, 0:2, :].rearrange("p r c -> p (r c)"),
                          src[:, 0:2 * COLS].broadcast_to([P, 2 * COLS])).then_inc(m_bc, 16)
            act.dma_start(csm[:, 0:DV], c0_d[one].rearrange("a p v -> p (a v)")).then_inc(m_c0, 16)

        act.wait_ge(s_chunk, W_X0 + 2)
        act.wait_ge(w_st, 48)
        act.wait_ge(ao_st, 16 * KB + 16)
        load_head(0)
        xm(0)

        flat = ps[:].rearrange("p a b -> p (a b)")

        def head(h, last):
            c0 = W_HEAD + PER_HEAD * h
            em_row = rows_d[bass.ds(h, 1)].rearrange("a r c -> a (r c)")[:, 2 * COLS:]
            act.wait_ge(s_k_mm, h + 1)
            nc.scalar.activation(as3(kz), slot_a, ACT.Copy).then_inc(s_drA, 1)
            act.wait_ge(s_chunk, c0 + 1)
            nc.scalar.activation(as3(preq[:, 0:COLS]), slot_b, ACT.Copy, scale=float(DK) ** -0.5)\
                .then_inc(s_drB, 1)
            act.dma_start(em[:, 0, :], em_row.broadcast_to([P, COLS])).then_inc(m_em, 16)
            act.wait_ge(m_mask, NCH * (h + 1))
            for s in (slice(0, SEQ), slice(SAMPLE0, COLS)):
                a(bc[:, 0, s], bc[:, 0, s], ACT.Exp, m_e)
            act.wait_ge(s_va, h + 1)
            act.wait_ge(m_clo, 2 * h + 2)
            half_v = lambda lo, n: flat[:, lo * BANK:lo * BANK + n * DV].rearrange("p (c v) -> p c v", v=DV)
            nc.scalar.activation(vt3[:, 0:6, 0:DV], half_v(0, 6), ACT.Copy).then_inc(s_drA, 1)
            act.wait_ge(s_chunk, c0 + 2)
            nc.scalar.activation(vt3[:, 6:NCH, 0:DV], half_v(3, NCH - 6), ACT.Copy).then_inc(s_drB, 1)

            def keys(c):
                act.wait_ge(m_s_mm, NCH * h + c + 1)
                if c >= 2:
                    act.wait_ge(m_u_mm, NCH * h + c - 1)
                a(kt[:, c % 2, :], ps[:, 2 + 3 * (c % 2), 0:P], ACT.Copy, m_kt, scale=hcol[:, 1, c:c + 1])
            keys(0)
            keys(1)
            for c in range(NCH):
                t0, n = COL0[c], CLEN[c]
                act.wait_ge(m_o_mm, NCH * h + c + 1)
                o = ps[:, 3 + c % 2, 0:3 * P].rearrange("p (j t) -> p j t", j=3)[:, :, 0:n]
                a(bc[:, 0:3, t0:t0 + n], o, ACT.Copy, m_oe)
                if c + 2 < NCH:
                    keys(c + 2)
            act.wait_ge(m_c, NCH * (h + 1))
            for s in range(2):
                act.dma_start(c_d[bass.ds(h + HEADS * s, 1)].rearrange("a p v -> p (a v)"), cst[:, s, 0:DV])\
                   .then_inc(m_cout, 16)
            act.wait_ge(s_drA, A_HD + 8 * h + 3)
            a(kz, kz, ACT.Sigmoid, m_zs)
            act.wait_ge(m_y, 2 * h + 1)
            a(yb_hi[:, 0, :], bc[:, 0, :], ACT.Copy, m_yhi)
            act.wait_ge(s_drB, B_HD + 8 * h + 3)
            a(preq[:, 0:COLS], preq[:, 0:COLS], ACT.Sigmoid, m_zs)
            act.wait_ge(m_y, 2 * h + 2)
            a(yb_hi[:, 1, :], bc[:, 1, :], ACT.Copy, m_yhi)
            if not last:
                act.wait_ge(m_ylo, 2 * h + 2)
                act.wait_ge(m_o_mm, NCH * (h + 1))
                load_head(h + 1)
                xm(h + 1)
        loop(act, HEADS - 1, lambda h: head(h, False))
        head(HEADS - 1, True)

        act.wait_ge(s_drB, B_GB)
        act.wait_ge(s_drA, A_GB)
        act.wait_ge(m_cout, 32 * HEADS + 16)

        def load(dram, n, dst, inc):
            act.dma_start(dst, dram[bass.ds(n, 1)].rearrange("a p c -> p (a c)")).then_inc(inc, 16)

        for half in range(2):
            load(mixa_d, half, tmp[:, 2 + half, :], g_in[half])

        def gb(i, last):
            for half in range(2):
                n = 2 * i + half
                act.wait_ge(s_dr[half], (A_GB, B_GB)[half] + i + 1)
                a(tmp[:, half, :], tmp[:, half, :], ACT.Sigmoid, g_sig)
                act.wait_ge(g_mix, n + 1)
                a(blk(act_hi, n), tmp[:, half, :], ACT.Copy, g_hi)
                if not last:
                    load(mixa_d, n + 2, tmp[:, 2 + half, :], g_in[half])
        loop(act, KB // 2 - 1, lambda i: gb(i, False))
        gb(KB // 2 - 1, True)

        act.wait_ge(g_lo, KB)
        for half in range(2):
            load(x_t, half, tmp[:, half, :], o_in[half])

        def wo(i, last):
            for half in range(2):
                n = 2 * i + half
                act.wait_ge(s_dr[half], (A_WO, B_WO)[half] + i + 1)
                a(blk(u_hi, n), blk(acc, n), ACT.Identity, s_nhi, scale=gain2(n))
                a(tmp[:, 2, :], blk(acc, n), ACT.Square, o_sq)
                if not last:
                    load(x_t, n + 2, tmp[:, half, :], o_in[half])
        loop(act, KB // 2 - 1, lambda i: wo(i, False))
        wo(KB // 2 - 1, True)

        def up(g):
            def pair(i):
                for half in range(2):
                    j = 8 * g + 2 * i + half
                    act.wait_ge(s_chunk, W_MLP + 32 * g + 4 * i + 2 * half + 2)
                    act.wait_ge(h_s, j - 1 + 2 * FREE)
                    nc.scalar.activation(as3(tmp[:, half, :]), slots[half], ACT.Relu).then_inc(s_dr[half], 1)
                    act.wait_ge(s_dr[half], a_up(g, half) + i + 1)
                    a(blk(act_hi, 2 * i + half), tmp[:, half, :], ACT.Square, h_hi)
            loop(act, KB // 2, pair)
        up(0)
        act.wait_ge(s_norm, 2)
        nc.scalar.activation(as3(tmp[:, 3, :]), slot_a, ACT.Identity, scale=1.0 / D_MODEL, bias=eps_c[:, 0:1])\
            .then_inc(s_drA, 1)
        with act.Fori(1, GROUPS) as g:
            up(g)

        nc.scalar.activation(warm[:], eps_c[:], ACT.Sqrt).then_inc(s_warm, 1)

        def final(n, s, step):
            act.wait_ge(h_acc, KB * (GROUPS - 1) + step + 1 + FREE)
            a(tmp[:, 0, s], blk(acc, n)[:, s], ACT.Square, f_sq)
            act.wait_ge(f_sq, step + 1)
            a(blk(acc, n)[:, s], blk(acc, n)[:, s], ACT.Copy, f_gain, scale=gain3(n))
        loop(act, KB - 1, lambda n: final(n, slice(0, COLS), n))

        def last_std(t):
            lo, hi = LAST_TILES[t]
            act.wait_ge(f_norm, t + 1)
            nc.scalar.activation(rstd[:, lo:hi], ps[:, t, 0:hi - lo], ACT.Sqrt, scale=1.0 / D_MODEL,
                                 bias=eps_c[:, 0:1]).then_inc(f_std, 1)
        for t, (lo, hi) in enumerate(LAST_TILES):
            final(KB - 1, slice(lo, hi), KB - 1 + t)
            last_std(t)

    @block.vector
    def _(dve):
        V = nc.vector

        def stt(out, in0, scalar, in1, op0, op1, inc):
            V.scalar_tensor_tensor(out, in0, scalar, in1, op0, op1).then_inc(inc, 1)

        def tt(out, in0, in1, op, inc):
            V.tensor_tensor(out, in0, in1, op).then_inc(inc, 1)

        dve.sem_inc(r_ylo, FREE)
        dve.sem_inc(h_s, 2 * FREE)
        dve.sem_inc(h_lo, FREE)
        dve.sem_inc(h_acc, FREE)
        V.memset(rpre[:, 0:TAIL], 0.0).then_inc(s_const_dve, 1)
        dve.wait_ge(s_small, 16)

        lam = small[:, S_RG + 7:S_RG + 13 * KB:13]
        c = [c8[:, j, :] for j in range(8)]
        steps = [
            lambda: V.scalar_tensor_tensor(c[1], lam, -1.0, lam, ALU.mult, ALU.max),
            lambda: V.tensor_scalar(c[3], c[2], 2.0, None, ALU.add),
            lambda: V.reciprocal(c[4], c[3]),
            lambda: V.tensor_tensor(c[5], c[2], c[4], ALU.mult),
            lambda: V.tensor_tensor(c[6], c[5], c[5], ALU.mult),
            lambda: V.tensor_scalar(c[7], c[6], 1.0 / 15, None, ALU.mult),
        ] + [
            (lambda k=k: V.scalar_tensor_tensor(c[7], c[7], 1.0 / k, c[6], ALU.add, ALU.mult))
            for k in (13, 11, 9, 7, 5, 3)
        ] + [
            lambda: V.scalar_tensor_tensor(c[3], c[7], 1.0, c[5], ALU.add, ALU.mult),
            lambda: V.tensor_tensor(c[4], c[1], lam, ALU.subtract),
            lambda: V.tensor_scalar(c[4], c[4], -RG_C / 2, None, ALU.mult),
            lambda: V.scalar_tensor_tensor(c[0], c[3], -2 * RG_C, c[4], ALU.mult, ALU.add),
        ]
        steps[0]().then_inc(s_spv, 1)

        def rest(slot, dst, inc):
            tt(as3(dst), slot, as3(rstd[:]), ALU.mult, inc)

        for j in range(KB):
            dve.wait_ge(s_nhi, j + 1)
            stt(u_lo[:, j, :], acc[:, j, :], gain(j), u_hi[:, j, :].bitcast(F32), ALU.mult, ALU.subtract, s_nlo)
            dve.wait_ge(s_sq, j + 1)
            if j:
                if j >= 2:
                    dve.wait_ge(s_ssum, j - 1)
                tt(p0[:, 2, :], p0[:, 2, :], p0[:, j % 2, :], ALU.add, s_ssum)
        dve.wait_ge(s_std, 1)
        V.reciprocal(rcol[:], rcol[:]).then_inc(s_rstd, 1)
        dve.wait_ge(s_rstd, 1)
        ident = small[:, S_ID:S_ID + P]
        full_w, rest_w = NCH - 1, COLS - SEQ
        tt(p0[:, 3, 0:SEQ].rearrange("p (c t) -> p c t", t=CH),
           ident.rearrange("p (a t) -> p a t", a=1).broadcast_to([P, full_w, CH]),
           rcol[:, 0:full_w].rearrange("p (c a) -> p c a", a=1).broadcast_to([P, full_w, CH]), ALU.mult, n_diag)
        V.tensor_scalar(p0[:, 3, SEQ:], ident[:, CH - rest_w:], rcol[:, NCH - 1:NCH], None, ALU.mult)\
            .then_inc(n_diag, 1)
        dve.wait_ge(s_sp, 1)
        for k, step in enumerate(steps[1:]):
            dve.wait_ge(s_spv, k + 1)
            step().then_inc(s_spv, 1)

        dve.wait_ge(s_spv, len(steps))
        dve.wait_ge(s_const_dve, 1)
        dve.wait_ge(n_out, TILES)

        def tails(pre, n, inc):
            o = cso[:, bass.ds(n, 1), :].rearrange("p a s -> p (a s)")
            V.tensor_copy(o[:, 0:TAIL], pre[:, SEQ:SEQ + TAIL]).then_inc(inc, 1)
            V.tensor_copy(o[:, TAIL:], pre[:, COLS:COLS + TAIL]).then_inc(inc, 1)

        def convolve(n):
            V.tensor_copy(rp[:], small[:, bass.ds(13 * n + S_RG, 13)]).then_inc(r_rp, 1)
            V.tensor_copy(rc8[:], c8[:, 0, bass.ds(n, 1)]).then_inc(r_rp, 1)
            dve.wait_ge(s_chunk, W_RG + 5 * n + 2)
            rest(slot_a, rpre[:, TAIL:], s_drA)
            dve.wait_ge(r_rp, 2 * n + 2)
            dve.wait_ge(s_drA, A_RG + 2 * n + 1)
            V.tensor_copy(rpre[:, SAMPLE0:SAMPLE0 + TAIL], rp[:, 8:8 + TAIL]).then_inc(r_pad, 1)
            tails(rpre, n, r_cs)
            for k in range(1, CONV_W):
                dve.wait_ge(r_tap0, n + 1)
                if k > 1:
                    dve.wait_ge(r_conv, TAIL * n + k - 1)
                stt(acc[:, XC, :], rpre[:, k:k + COLS], rp[:, k:k + 1], acc[:, XC, :], ALU.mult, ALU.add, r_conv)

        def gr_out(n):
            dve.wait_ge(s_chunk, W_RG + 5 * n + 4)
            rest(slot_b, acc[:, G, :], s_drB)

        def x_lo(n):
            dve.wait_ge(r_xhi, n + 1)
            dve.wait_ge(r_conv, TAIL * n + TAIL)
            tt(rx_lo[:], acc[:, XC, :], rx_hi[:].bitcast(F32), ALU.subtract, r_xlo)

        def inner(n):
            dve.wait_ge(r_sq, n + 1)
            stt(acc[:, SQ, :], acc[:, SQ, :], 1.0 / GELU_C, acc[:, G, :], ALU.add, ALU.mult, r_inner)

        def ix(n):
            dve.wait_ge(s_drB, B_RG + 2 * n + 2)
            tt(acc[:, I, :], acc[:, I, :], acc[:, XC, :], ALU.mult, r_ix)

        def rg(n, last):
            inner(n)
            dve.wait_ge(r_tg, n + 1)
            dve.wait_ge(r_ylo, n + FREE)
            stt(acc[:, GG, :], acc[:, SQ, :], 1.0, acc[:, G, :], ALU.add, ALU.mult, r_gg)
            dve.wait_ge(r_a, n + 1)
            tt(acc[:, H, :], acc[:, R, :], acc[:, R, :], ALU.mult, r_a2)
            dve.wait_ge(r_a2, n + 1)
            stt(acc[:, TH, :], acc[:, H, :], 1.0, acc[:, TH, :], ALU.add, ALU.mult, r_p)
            if not last:
                convolve(n + 1)
            dve.wait_ge(r_gain, n + 1)
            dve.wait_ge(r_ix, n + 1)
            tt(acc[:, I, :], acc[:, I, :], acc[:, TH, :], ALU.mult, r_b)
            dve.wait_ge(r_b, n + 1)
            V.memset(acc[:, R, CARRY:CARRY + 1], 0.0).then_inc(r_fix, 1)
            V.tensor_copy(acc[:, I, CARRY:CARRY + 1], h0(n)).then_inc(r_fix, 1)
            if not last:
                x_lo(n + 1)
            dve.wait_ge(r_fix, 2 * n + 2)
            V.tensor_tensor_scan(acc[:, H, :], acc[:, R, :], acc[:, I, :], 0.0, ALU.mult, ALU.add)\
                .then_inc(r_scan, 1)
            if not last:
                gr_out(n + 1)
            dve.wait_ge(r_scan, n + 1)
            o = hso[:, bass.ds(n, 1), :].rearrange("p a s -> p (a s)")
            V.tensor_copy(o[:, 0:1], acc[:, H, SEQ - 1:SEQ]).then_inc(r_hs, 1)
            V.tensor_copy(o[:, 1:2], acc[:, H, COLS - 1:COLS]).then_inc(r_hs, 1)
            dve.wait_ge(r_gg, n + 1)
            stt(acc[:, GG, :], acc[:, GG, :], 0.5, acc[:, H, :], ALU.mult, ALU.mult, r_y)
            if not last:
                ix(n + 1)
            dve.wait_ge(r_y, n + 1)
            dve.wait_ge(r_yhi, n + 1)
            tt(blk(ya_lo, n), acc[:, GG, :], blk(ya_hi, n).bitcast(F32), ALU.subtract, r_ylo)

        h0 = lambda n: small[:, bass.ds(13 * n + S_RG + 11, 1)]
        convolve(0)
        x_lo(0)
        gr_out(0)
        ix(0)
        loop(dve, KB - 1, lambda n: rg(n, False))
        rg(KB - 1, True)

        row = lambda j, s=slice(0, COLS): acc[0:HEADS, j, s]
        pr, gap, sa = slice(0, SEQ), slice(SEQ, SAMPLE0), slice(SAMPLE0, COLS)
        chunks = lambda ap: ap.rearrange("p (c t) -> p c t", t=CH)

        def ends(j, first, n):
            e = acc[0:HEADS, j, first:first + CH * n].rearrange("p (c t) -> p c t", t=CH)[:, :, CH - 1:CH]
            return e.broadcast_to([HEADS, n, CH])

        row_steps = [
            lambda: V.scalar_tensor_tensor(row(EM), row(LF), -1.0, row(LF), ALU.mult, ALU.max),
            lambda: V.scalar_tensor_tensor(row(LF), row(LF), 0.0, row(EM), ALU.min, ALU.subtract),
            lambda: V.tensor_tensor_scan(row(FF), row(MASK), row(LF), 0.0, ALU.mult, ALU.add),
            lambda: V.tensor_tensor(row(EE), row(IG), row(FF), ALU.subtract),
            lambda: V.memset(row(LF, slice(CARRY, CARRY + 1)), -1e30),
            lambda: V.tensor_copy(row(IG, slice(CARRY, CARRY + 1)), small[0:HEADS, S_M0:S_M0 + 1]),
            lambda: V.tensor_tensor_scan(row(MM), row(LF), row(IG), 0.0, ALU.add, ALU.max),
            lambda: V.tensor_copy(mso[:, 0:1], row(MM, slice(SEQ - 1, SEQ))),
            lambda: V.tensor_copy(mso[:, 1:2], row(MM, slice(COLS - 1, COLS))),
            lambda: V.tensor_tensor(row(AR), row(FF), row(MM), ALU.subtract),
            lambda: V.tensor_copy(row(LF, slice(0, CH)), row(AR, slice(0, CH))),
            lambda: V.tensor_tensor(chunks(row(LF, slice(CH, SEQ))), chunks(row(AR, slice(CH, SEQ))),
                                    ends(MM, 0, SEQ // CH - 1), ALU.add),
            lambda: V.memset(row(LF, gap), 0.0),
            lambda: V.tensor_scalar(row(LF, sa), row(AR, sa), row(MM, slice(CARRY, CARRY + 1)), None, ALU.add),
            lambda: V.tensor_tensor(chunks(row(MASK, pr)), chunks(row(EE, pr)), ends(AR, 0, SEQ // CH), ALU.add),
            lambda: V.memset(row(MASK, gap), 0.0),
            lambda: V.tensor_scalar(row(MASK, sa), row(EE, sa), row(AR, slice(COLS - 1, COLS)), None, ALU.add),
            lambda: V.memset(row(AR, gap), 0.0),
        ]
        assert len(row_steps) == ROWS_DVE
        dve.wait_ge(s_chunk, W_GATES + 2)
        dve.wait_ge(r_yhi, KB)
        tt(as3(row(IG)), slot_a[0:HEADS], as3(rstd[0:HEADS]), ALU.mult, w_pre)
        tt(as3(acc[32:32 + HEADS, LF, :]), slot_a[32:32 + HEADS], as3(rstd[32:32 + HEADS]), ALU.mult, s_drA)
        dve.wait_ge(w_act, 2)
        def some_rows(first, end):
            for k in range(first, end):
                if k:
                    dve.wait_ge(w_dve, k)
                if k == 1:
                    dve.wait_ge(w_act, 4)
                if k == 2:
                    dve.wait_ge(s_rowmask, 16)
                row_steps[k]().then_inc(w_dve, 1)

        def ao(n):
            dve.wait_ge(s_chunk, W_AO + 4 * n + 2)
            dve.wait_ge(ao_st, 16 * n + 16)
            rest(slot_b, rpre[:, 0:COLS], s_drB)
            dve.wait_ge(ao_sig, n + 1)
            dve.wait_ge(s_chunk, W_AO + 4 * n + 4)
            o = as3(rpre[:, 0:COLS])
            tt(o, slot_a, o, ALU.mult, s_drA)
        some_rows(0, 7)
        ao(0)
        some_rows(7, ROWS_DVE)
        with dve.Fori(1, KB) as n:
            ao(n)

        dve.wait_ge(w_st, 48)
        for first, end in ((0, MASK), (MASK + 1, EE)):
            V.memset(acc[:, first:end, :], 0.0).then_inc(s_zero, 1)

        def xm(h, chunk, drained, between=lambda step: None):
            V.tensor_copy(bp[:].rearrange("p a b -> p (a b)"), small[:, bass.ds(16 * h + S_ML, 16)])\
                .then_inc(m_bp, 1)

            def xm_out(cb):
                dve.wait_ge(s_chunk, chunk + 2 * cb + 2)
                rest(slots[cb], preq[:, TAIL:], s_dr[cb])
            xm_out(0)
            dve.wait_ge(m_bp, h + 1)
            for cb in range(2):
                other = between if cb else (lambda step: None)
                dve.wait_ge(s_dr[cb], drained[cb])
                V.tensor_copy(preq[:, SAMPLE0:SAMPLE0 + TAIL], bp[:, cb, 5:5 + TAIL]).then_inc(m_pad, 1)
                V.memset(preq[:, 0:TAIL], 0.0).then_inc(m_pad, 1)
                tails(preq, 2 * h + cb + KB, m_cs2)
                for k in range(1, CONV_W):
                    other(k - 1)
                    dve.wait_ge(m_tap0, 2 * h + cb + 1)
                    if k > 1:
                        dve.wait_ge(m_conv, TAIL * (2 * h + cb) + k - 1)
                    stt(conv1, preq[:, k:k + COLS], bp[:, cb, k:k + 1], conv1, ALU.mult, ALU.add, m_conv)
                dve.wait_ge(m_xhi, 2 * h + cb + 1)
                tt(xm_lo[:, cb, :], preq[:, TAIL:], xm_hi[:, cb, :].bitcast(F32), ALU.subtract, m_xlo)
                other(3)
                dve.wait_ge(m_sig, 2 * h + cb + 1)
                tt(conv1, conv1, conv2, ALU.mult, m_silu)
                if cb == 0:
                    dve.wait_ge(m_conv, TAIL * (2 * h + 1))
                    dve.wait_ge(m_xlo, 2 * h + 1)
                    xm_out(1)
                other(4)
                dve.wait_ge(m_chi, 2 * h + cb + 1)
                dve.wait_ge(m_silu, 2 * h + cb + 1)
                tt(xc_lo[:, cb, :], conv1, xc_hi[:, cb, :].bitcast(F32), ALU.subtract, m_clo)
        xm(0, W_X0, (A_HD, B_HD))
        dve.wait_ge(w_tr, 1)
        V.tensor_copy(ecol[:].rearrange("p r c h -> p (r c h)"), ps[:, 6, 0:2 * NCH * HEADS]).then_inc(w_col, 1)
        dve.wait_ge(w_col, 1)
        V.memset(ecol[0:CH - DEC_SEQ, 1, NCH - 1, :], 0.0).then_inc(w_colz, 1)
        for row_used in (MASK, EE):
            V.memset(acc[:, row_used, :], 0.0).then_inc(s_zero, 1)
        dve.wait_ge(w_colz, 1)
        dve.wait_ge(s_zero, 4)

        def head(h, last):
            c0, a0, b0 = W_HEAD + PER_HEAD * h, A_HD + 8 * h, B_HD + 8 * h
            V.tensor_copy(hcol[:].rearrange("p r c -> p (r c)"),
                          ecol[:, :, :, bass.ds(h, 1)].rearrange("p r c a -> p (r c a)")).then_inc(m_hcol, 1)
            V.tensor_copy(csm[:, DV:], small[:, bass.ds(h + S_N0, 1)]).then_inc(m_cs, 1)
            dve.wait_ge(m_clo, 2 * h + 2)
            V.memset(vt3[:, :, DV:], 1.0).then_inc(m_one, 1)
            dve.wait_ge(m_bc, 16 * h + 16)
            V.tensor_copy(dec[:, 0:NCH - 1], bc[:, 1, CH - 1:SEQ:CH]).then_inc(m_dec, 1)
            V.tensor_copy(dec[:, NCH - 1:], bc[:, 1, COLS - 1:COLS]).then_inc(m_dec, 1)
            dve.wait_ge(m_hcol, h + 1)
            for c in range(NCH):
                t, n = slice(COL0[c], COL0[c] + CLEN[c]), CLEN[c]
                mask = small[:, S_MASK:S_MASK + n] if c < NCH - 1 else small[:, S_MASK8:S_MASK8 + n]
                stt(bc[:, 0, t], bc[:, 0, t], hcol[:, 0, c:c + 1], mask, ALU.add, ALU.add, m_mask)
            dve.wait_ge(s_drB, b0 + 1)
            dve.wait_ge(m_dec, 2 * h + 2)
            tt(bc[:, 1, :], bc[:, 1, :], preq[:, 0:COLS], ALU.mult, m_qw)

            def weigh(c):
                t0, n = COL0[c], CLEN[c]
                dve.wait_ge(m_s_mm, NCH * h + c + 1)
                dve.wait_ge(m_e, 2 * h + 2)
                if c >= 2:
                    dve.wait_ge(m_o_mm, NCH * h + c - 1)
                tt(sw[:, c % 2, 0:n], ps[:, 6 + c % 2, 0:n], bc[:, 0, t0:t0 + n], ALU.mult, m_sw)

            weigh(0)
            weigh(1)
            for c in range(NCH):
                t0, n = COL0[c], CLEN[c]
                dve.wait_ge(m_u_mm, NCH * h + c + 1)
                new = ps[:, c % 2, 0:VW]
                if c == 0:
                    dve.wait_ge(m_cout, 32 * h + 16)
                    V.tensor_copy(cst[:, 1, :], new).then_inc(m_c, 1)
                elif c < NCH - 1:
                    dve.wait_ge(m_c, NCH * h + c)
                    stt(cst[:, (c + 1) % 2, :], cst[:, c % 2, :], dec[:, c:c + 1], new, ALU.mult, ALU.add, m_c)
                else:
                    dve.wait_ge(m_c0, 16 * h + 16)
                    dve.wait_ge(m_cs, h + 1)
                    stt(cst[:, 1, :], csm[:], dec[:, c:c + 1], new, ALU.mult, ALU.add, m_c)
                if c + 1 < NCH:
                    t1, n1 = COL0[c + 1], CLEN[c + 1]
                    state = csm if c + 2 == NCH else cst[:, (c + 1) % 2, :]
                    dve.wait_ge(m_c, NCH * h + c + 1)
                    dve.wait_ge(m_cs, h + 1)
                    dve.wait_ge(m_qw, h + 1)
                    dve.wait_ge(m_sw, NCH * h + c + 2)
                    if c >= 1:
                        dve.wait_ge(m_o_mm, NCH * h + c)
                    stt(zw[:, (c + 1) % 2, 0:n1], bc[:, 1, t1:t1 + n1], state[:, DV:VW],
                        sw[:, (c + 1) % 2, 0:n1], ALU.mult, ALU.add, m_z)
                if c + 2 < NCH:
                    weigh(c + 2)
            o = nso[:, bass.ds(h, 1), :].rearrange("p a s -> p (a s)")
            dve.wait_ge(m_c, NCH * (h + 1))
            for s in range(2):
                V.tensor_copy(o[:, s:s + 1], cst[:, s, DV:DV + 1]).then_inc(m_no, 1)
            dve.wait_ge(m_oe, NCH * (h + 1))
            dve.wait_ge(m_em, 16 * h + 16)
            r = em[:, 0, :]
            stt(r, kz, -1.0, r, ALU.mult, ALU.max, m_rec)
            dve.wait_ge(m_rec, 3 * h + 1)
            tt(r, kz, r, ALU.max, m_rec)
            dve.wait_ge(m_rec, 3 * h + 2)
            V.reciprocal(r, r).then_inc(m_rec, 1)
            dve.wait_ge(m_rec, 3 * h + 3)
            tt(bc[:, 0:2, :], bc[:, 0:2, :], em[:].broadcast_to([P, 2, COLS]), ALU.mult, m_hn)
            dve.wait_ge(m_hn, h + 1)
            dve.wait_ge(s_chunk, c0 + 4)
            rest(slot_a, kz, s_drA)
            dve.wait_ge(m_zs, 2 * h + 1)
            tt(bc[:, 0, :], bc[:, 0, :], kz, ALU.mult, m_y)
            def y_lo(cb):
                dve.wait_ge(m_y, 2 * h + cb + 1)
                dve.wait_ge(m_yhi, 2 * h + cb + 1)
                tt(yb_lo[:, cb, :], bc[:, cb, :], yb_hi[:, cb, :].bitcast(F32), ALU.subtract, m_ylo)
            y_lo(0)
            dve.wait_ge(s_chunk, c0 + 6)
            rest(slot_b, preq[:, 0:COLS], s_drB)
            dve.wait_ge(m_zs, 2 * h + 2)
            tt(bc[:, 1, :], bc[:, 1, :], preq[:, 0:COLS], ALU.mult, m_y)
            y_lo(1)
            cy = c0 + (6 if last else 10)

            def add(m):
                if m % 2 == 0:
                    dve.wait_ge(s_bb, 4 * h + m // 2 + 1)
                else:
                    dve.wait_ge(s_chunk, cy + m // 2 + 1)
                tt(as3(acc[:, m, :]), slots[m % 2], as3(acc[:, m, :]), ALU.add, s_dr[m % 2])
            done = 0
            if not last:
                done = 5
                xm(h + 1, c0 + 6, (a0 + 4, b0 + 4), add)
            for m in range(done, KB):
                add(m)
        loop(dve, HEADS - 1, lambda h: head(h, False))
        head(HEADS - 1, True)

        dve.wait_ge(s_drA, A_GB)
        dve.wait_ge(s_drB, B_GB)

        def gb(i):
            for half in range(2):
                n = 2 * i + half
                dve.wait_ge(s_chunk, W_GB + 2 * n + 2)
                rest(slots[half], tmp[:, half, :], s_dr[half])
                dve.wait_ge(g_sig, n + 1)
                tt(tmp[:, half, :], tmp[:, half, :], blk(acc, n), ALU.mult, g_t)
                dve.wait_ge(g_t, n + 1)
                dve.wait_ge(g_in[half], 16 * i + 16)
                tt(tmp[:, half, :], tmp[:, half, :], tmp[:, 2 + half, :], ALU.add, g_mix)
                dve.wait_ge(g_mix, n + 1)
                dve.wait_ge(g_hi, n + 1)
                tt(blk(act_lo, n), tmp[:, half, :], blk(act_hi, n).bitcast(F32), ALU.subtract, g_lo)
        loop(dve, KB // 2, gb)

        V.memset(tmp[:, 3, :], 0.0).then_inc(s_zero, 1)
        dve.wait_ge(s_zero, 5)

        def wo(i):
            for half in range(2):
                n = 2 * i + half
                dve.wait_ge(s_chunk, W_OUT + 2 * n + 2)
                dve.wait_ge(o_in[half], 16 * i + 16)
                tt(as3(blk(acc, n)), slots[half], as3(tmp[:, half, :]), ALU.add, s_dr[half])
                dve.wait_ge(s_dr[half], (A_WO, B_WO)[half] + i + 1)
                dve.wait_ge(s_nhi, KB + n + 1)
                stt(blk(u_lo, n), blk(acc, n), gain2(n), blk(u_hi, n).bitcast(F32), ALU.mult, ALU.subtract, s_nlo)
                dve.wait_ge(o_sq, n + 1)
                tt(tmp[:, 3, :], tmp[:, 3, :], tmp[:, 2, :], ALU.add, o_ssum)
                dve.wait_ge(o_ssum, n + 1)
        loop(dve, KB // 2, wo)

        def up(g):
            def pair(i):
                dve.wait_ge(h_acc, KB * g + FREE)
                for half in range(2):
                    j = 8 * g + 2 * i + half
                    dve.wait_ge(s_dr[half], a_up(g, half) + i + 1)
                    dve.wait_ge(h_lo, j + FREE)
                    tt(tmp[:, 2, :], tmp[:, half, :], tmp[:, half, :], ALU.mult, h_s)
                    dve.wait_ge(h_s, j + 1 + 2 * FREE)
                    dve.wait_ge(h_hi, j + 1)
                    tt(blk(act_lo, 2 * i + half), tmp[:, 2, :],
                       blk(act_hi, 2 * i + half).bitcast(F32), ALU.subtract, h_lo)
            loop(dve, KB // 2, pair)

        def down(g, last=False):
            def pair(i, halves=2):
                dve.wait_ge(h_lo, 8 * g + 8 + FREE)
                for half in range(halves):
                    n = 2 * i + half
                    dve.wait_ge(s_chunk, W_MLP + 32 * g + 16 + 2 * n + 2)
                    dve.wait_ge(h_acc, KB * g + n + FREE)
                    tt(as3(tmp[:, 2, :]), slots[half], as3(tmp[:, 3, :]), ALU.mult, s_dr[half])
                    dve.wait_ge(s_dr[half], (A_ML + 1, B_ML)[half] + 8 * g + 4 + i + 1)
                    tt(blk(acc, n), blk(acc, n), tmp[:, 2, :], ALU.add, h_acc)
                    if last:
                        dve.wait_ge(f_sq, n + 1)
                        tt(tmp[:, 1, :], tmp[:, 1, :], tmp[:, 0, :], ALU.add, f_ssum)
                        dve.wait_ge(f_ssum, n + 1)
            loop(dve, KB // 2 - last, pair)
            if last:
                pair(KB // 2 - 1, 1)
        up(0)
        dve.wait_ge(s_drA, A_N2 + 1)
        V.reciprocal(tmp[:, 3, :], tmp[:, 3, :]).then_inc(s_rstd, 1)
        dve.wait_ge(s_rstd, 2)
        down(0)
        with dve.Fori(1, GROUPS - 1) as g:
            up(g)
            down(g)
        up(GROUPS - 1)
        V.memset(tmp[:, 1, :], 0.0).then_inc(s_zero, 1)
        dve.wait_ge(s_zero, 6)
        down(GROUPS - 1, True)

        h0_last = KB * (GROUPS - 1) + KB - 1 + FREE

        def last_block(t):
            lo, hi = LAST_TILES[t]
            dve.wait_ge(f_mm, t + 1)
            dve.wait_ge(h_acc, h0_last + t)
            tt(tmp[:, 2, lo:hi], ps[:, 3 + t, 0:hi - lo], tmp[:, 3, lo:hi], ALU.mult, f_prod)
            dve.wait_ge(f_prod, t + 1)
            tt(acc[:, KB - 1, lo:hi], acc[:, KB - 1, lo:hi], tmp[:, 2, lo:hi], ALU.add, h_acc)

        def last_ssum(t):
            lo, hi = LAST_TILES[t]
            dve.wait_ge(f_sq, KB + t)
            tt(tmp[:, 1, lo:hi], tmp[:, 1, lo:hi], tmp[:, 0, lo:hi], ALU.add, f_ssum)

        def last_recip(t):
            lo, hi = LAST_TILES[t]
            dve.wait_ge(f_std, t + 1)
            V.reciprocal(rstd[:, lo:hi], rstd[:, lo:hi]).then_inc(f_rstd, 1)

        def last_y(t):
            lo, hi = LAST_TILES[t]
            dve.wait_ge(f_gain, KB + t)
            dve.wait_ge(f_rstd, t + 1)
            y = acc[:, POOL_BLOCKS:, lo:hi]
            tt(y, y, last_rstd(lo, hi, KB - POOL_BLOCKS), ALU.mult, f_yv)
        last_block(0)
        last_ssum(0)
        last_recip(0)
        last_block(1)
        last_ssum(1)
        last_y(0)
        last_block(2)
        last_recip(1)
        last_ssum(2)
        last_y(1)
        last_recip(2)
        last_y(2)

    outer.close()


def kernel(**inputs):
    import concourse.bacc as _bacc
    from concourse.bass_utils import run_bass_kernel_spmd as _run

    x = {k: np.asarray(v) for k, v in inputs.items()}
    f32 = np.float32

    cols = np.zeros((D_MODEL, COLS), f32)
    cols[:, :SEQ] = x["x_prompt"][0].T
    cols[:, SAMPLE0:] = x["x_sample"][0].T
    x_t = cols.reshape(KB, P, COLS)

    def tiles(w):
        k, m = w.shape
        t = w.reshape(k // (4 * P), 4, P, m // P, P).transpose(3, 0, 2, 1, 4)
        return t.reshape(m // P, k // (4 * P), P, CHUNK)

    w_in = x["w_in"][0]
    at = np.cumsum([0, D_RNN, D_RNN, D_ML, D_ML, HEADS, HEADS, D_MODEL, D_MODEL])
    xr, gr, xm, zm = (tiles(w_in[:, at[i]:at[i + 1]]) for i in range(4))
    ga, gb = (tiles(w_in[:, at[i]:at[i + 1]]) for i in (6, 7))
    gates = np.zeros((D_MODEL, P), f32)
    gates[:, 0:HEADS] = w_in[:, at[4]:at[5]]
    gates[:, 32:32 + HEADS] = w_in[:, at[5]:at[6]]
    wa, wx = x["rglru_wa"][0], x["rglru_wx"][0]
    wpa, wout = tiles(x["w_branch_a"][0]), tiles(x["w_out"][0])
    wpb, wup = x["w_branch_b"][0], tiles(x["w_mlp_up"][0])
    wdn = tiles(x["w_mlp_down"][0])
    wq, wk, wv = x["mlstm_wq"][0], x["mlstm_wk"][0], x["mlstm_wv"][0]
    ch = []
    for n in range(KB):
        pair = np.zeros((1, P, CHUNK), f32)
        pair[0, :, 0:P], pair[0, :, P:2 * P] = wa[n], wx[n]
        ch += [xr[n], gr[n], pair]
    ch += [tiles(gates)[0]]
    for n in range(KB):
        ch += [ga[n], wpa[n]]
    ch += [xm[0], xm[1]]
    for h in range(HEADS):
        v = wv[h].reshape(2, P, DV).transpose(1, 0, 2).reshape(1, P, CHUNK)
        kq = np.stack([wk[h].reshape(2, P, DK), wq[h].reshape(2, P, DK)])
        ch += [kq.transpose(2, 0, 1, 3).reshape(1, P, CHUNK), v, zm[2 * h], zm[2 * h + 1]]
        if h + 1 < HEADS:
            ch += [xm[2 * h + 2], xm[2 * h + 3]]
        b = wpb[h * DV:(h + 1) * DV].reshape(2, P, 4, 2, P).transpose(2, 1, 3, 0, 4)
        ch += [b.reshape(4, P, CHUNK)]
    ch += [gb[n] for n in range(KB)] + [wout[n] for n in range(KB)]
    for g in range(GROUPS):
        ch += [wup[KB * g + j] for j in range(KB)]
        ch += [wdn[n, 2 * g:2 * g + 2] for n in range(KB)]
    w = np.concatenate(ch)
    assert w.shape == (W_END, P, CHUNK)

    small = np.zeros((P, S_COLS), f32)
    small[:, S_ID:S_ID + P] = np.eye(P, dtype=f32)
    key, query = np.arange(P)[:, None], np.arange(P)[None, :]
    small[:, S_MASK:S_MASK + P] = np.where(key <= query, 0.0, -1e30)
    shift = key - (P - DEC_SEQ)
    small[:, S_MASK8:S_MASK8 + DEC_SEQ] = np.where((shift >= 0) & (shift <= query[:, :DEC_SEQ]), 0.0, -1e30)
    rg = np.zeros((KB, P, 13), f32)
    rg[:, :, 0:4] = x["conv_rglru_w"][0].reshape(CONV_W, KB, P).transpose(1, 2, 0)
    for i, k in ((4, "conv_rglru_b"), (5, "rglru_ba"), (6, "rglru_bx"), (7, "rglru_lambda")):
        rg[:, :, i] = x[k][0].reshape(KB, P)
    rg[:, :, 8:11] = x["state_rglru_conv"][0, 0].reshape(TAIL, KB, P).transpose(1, 2, 0)
    rg[:, :, 11] = x["state_rglru_h"][0, 0].reshape(KB, P)
    small[:, S_RG:S_ML] = rg.transpose(1, 0, 2).reshape(P, -1)
    ml = np.zeros((2 * HEADS, P, 8), f32)
    ml[:, :, 0:4] = x["conv_mlstm_w"][0].reshape(CONV_W, 2 * HEADS, P).transpose(1, 2, 0)
    ml[:, :, 4] = x["conv_mlstm_b"][0].reshape(2 * HEADS, P)
    ml[:, :, 5:8] = x["state_mlstm_conv"][0, 0].reshape(TAIL, 2 * HEADS, P).transpose(1, 2, 0)
    small[:, S_ML:S_GAIN] = ml.transpose(1, 0, 2).reshape(P, -1)
    gains = np.stack([x["norm_mix"][0], x["norm_mlp"][0], x["norm_final"]])
    small[:, S_GAIN:S_N0] = gains.reshape(3, KB, P).transpose(2, 0, 1).reshape(P, -1)
    small[:, S_N0:S_BIF] = x["state_mlstm_n"][0, 0].T
    small[0:HEADS, S_BIF] = x["b_if"][0, :HEADS]
    small[32:32 + HEADS, S_BIF] = x["b_if"][0, HEADS:]
    small[0:HEADS, S_M0] = x["state_mlstm_m"][0, 0]
    rowmask = np.ones((HEADS, COLS), f32)
    rowmask[:, COL0 + [SEQ]] = 0.0

    nc = _bacc.Bacc("TRN2", target_bir_lowering=False, num_devices=1)
    arrays = {
        "x_t": x_t, "small": small, "rowmask": rowmask, "w": w,
        "c0": np.ascontiguousarray(x["state_mlstm_C"][0, 0].transpose(0, 2, 1)),
    }
    given = {k: nc.dram_tensor("in_" + k, v.shape, F32, kind="ExternalInput").ap() for k, v in arrays.items()}
    made = {k: nc.dram_tensor("out_" + k, s, F32, kind=kind).ap() for k, s, kind in (
        ("rows", (HEADS, 3, COLS), "Internal"), ("mixa", (KB, P, COLS), "Internal"),
        ("y", (KB, P, COLS), "ExternalOutput"), ("conv", (P, 24, 6), "ExternalOutput"),
        ("hlast", (P, KB, 2), "ExternalOutput"), ("c", (2 * HEADS, P, DV), "ExternalOutput"),
        ("n", (P, HEADS, 2), "ExternalOutput"), ("m", (HEADS, 2), "ExternalOutput"))}
    build(nc, given["x_t"], given["small"], given["rowmask"], given["w"], given["c0"], made["rows"],
          made["mixa"], made["y"], made["conv"], made["hlast"], made["c"], made["n"], made["m"])
    r = _run(nc, [{"in_" + k: np.ascontiguousarray(v) for k, v in arrays.items()}], core_ids=[0]).results[0]

    y = r["out_y"].reshape(D_MODEL, COLS).T
    c = r["out_c"].reshape(2, HEADS, P, DV).transpose(0, 1, 3, 2)
    out = [np.ascontiguousarray(y[None, :SEQ]), np.ascontiguousarray(y[None, SAMPLE0:])]
    for s in range(2):
        conv = r["out_conv"][:, :, TAIL * s:TAIL * s + TAIL].transpose(2, 1, 0)
        out += [
            conv[:, :KB].reshape(1, 1, TAIL, D_RNN),
            r["out_hlast"][:, :, s].T.reshape(1, 1, D_RNN),
            conv[:, KB:].reshape(1, 1, TAIL, D_ML),
            c[s].reshape(1, 1, HEADS, DV, DK),
            r["out_n"][:, :, s].T.reshape(1, 1, HEADS, DK),
            r["out_m"][:, s].reshape(1, 1, HEADS),
        ]
    return tuple(np.ascontiguousarray(o) for o in out)
```
